# Optimizing a Trainium2 kernel written in Bass

```python
import math
import jax, jax.numpy as jnp
from jax import lax
import numpy as np

D_MODEL = 1024
BATCH = 1
SEQ = 256
DEPTH = 2

D_FF = 2816
HALF_STEP = 0.5
S5_WIDTH = D_MODEL // 2
S5_GROUP = 16
S5_GROUPS = S5_WIDTH // S5_GROUP
S5_STATE = 64
FOX_HEADS = 8
FOX_HEAD_DIM = 64
MLA_HEADS = 8
MLA_Q_RANK = 384
MLA_KV_RANK = 256
MLA_NOPE_DIM = 64
MLA_ROPE_DIM = 32
MLA_V_DIM = 64
ROPE_THETA = 10000.0
NSA_HEADS = 8
NSA_KV_HEADS = 2
NSA_GROUP = NSA_HEADS // NSA_KV_HEADS
NSA_HEAD_DIM = 64
CMP_LEN = 32
CMP_STRIDE = 16
CMP_HIDDEN = 128
SLC_LEN = 64
SLC_TOPK = 16
WINDOW = 512
FORCED_SCORE = 1e4
REL_BUCKETS = 32
REL_MAX_DIST = 128
Q_BLOCK = 128
NEG_INF = -1e30
EPS = 1e-6
EVEN_IN = S5_WIDTH + 3 * FOX_HEADS * FOX_HEAD_DIM + FOX_HEADS
EVEN_OUT = S5_WIDTH + FOX_HEADS * FOX_HEAD_DIM
ODD_IN = MLA_Q_RANK + MLA_KV_RANK + MLA_ROPE_DIM + NSA_HEADS * NSA_HEAD_DIM + 6 * NSA_KV_HEADS * NSA_HEAD_DIM + 3 * NSA_HEADS
ODD_OUT = MLA_HEADS * MLA_V_DIM + NSA_HEADS * NSA_HEAD_DIM

kernel_name = 'hybrid_s5_fox_mla_nsa_macaron'

def _rmsnorm(x, g):
    xf = x.astype(jnp.float32)
    y = xf * lax.rsqrt(jnp.mean(xf * xf, axis=-1, keepdims=True) + EPS)
    return (y * g.astype(jnp.float32)).astype(x.dtype)

def _swiglu(h, w_gate, w_up, w_down):
    return (jax.nn.silu(h @ w_gate) * (h @ w_up)) @ w_down

def _split(x, sizes):
    return jnp.split(x, np.cumsum(sizes)[:-1].tolist(), axis=-1)

def _masked_softmax(s, mask):
    s = jnp.where(mask, s, NEG_INF)
    m = jnp.max(s, axis=-1, keepdims=True)
    p = jnp.where(mask, jnp.exp(s - m), 0.0)
    return p / jnp.maximum(jnp.sum(p, axis=-1, keepdims=True), 1e-30)

def _sweep_query_blocks(fn, seq_len):
    starts = jnp.arange(seq_len // Q_BLOCK, dtype=jnp.int32) * Q_BLOCK
    out = lax.map(fn, starts)
    out = jnp.moveaxis(out, 0, -3)
    return out.reshape(out.shape[:-3] + (seq_len, out.shape[-1]))

def _dense_causal_attention(q, k, v, logit_bias_fn=None):
    seq_len = q.shape[2]
    scale = q.shape[-1] ** -0.5
    kpos = jnp.arange(seq_len)

    def block(q0):
        qb = lax.dynamic_slice_in_dim(q, q0, Q_BLOCK, axis=2)
        s = jnp.einsum('bhqd,bhkd->bhqk', qb, k).astype(jnp.float32) * scale
        if logit_bias_fn is not None:
            s = s + logit_bias_fn(q0)
        qpos = q0 + jnp.arange(Q_BLOCK)
        p = _masked_softmax(s, kpos[None, :] <= qpos[:, None])
        return jnp.einsum('bhqk,bhkd->bhqd', p.astype(v.dtype), v)

    return _sweep_query_blocks(block, seq_len)

def _rope(x, pos):
    half = x.shape[-1] // 2
    freqs = ROPE_THETA ** (-jnp.arange(half, dtype=jnp.float32) / half)
    ang = pos.astype(jnp.float32)[:, None] * freqs[None, :]
    cos = jnp.cos(ang)[None, :, None, :]
    sin = jnp.sin(ang)[None, :, None, :]
    xf = x.astype(jnp.float32)
    x1, x2 = xf[..., :half], xf[..., half:]
    return jnp.concatenate([x1 * cos - x2 * sin, x2 * cos + x1 * sin], axis=-1).astype(x.dtype)

def _t5_bucket(dist):
    n = jnp.maximum(dist, 0)
    max_exact = REL_BUCKETS // 2
    large = max_exact + (jnp.log(jnp.maximum(n, max_exact).astype(jnp.float32) / max_exact)
                         / math.log(REL_MAX_DIST / max_exact) * (REL_BUCKETS - max_exact)).astype(jnp.int32)
    large = jnp.minimum(large, REL_BUCKETS - 1)
    return jnp.where(n < max_exact, n, large)

def _t5_bias(rel_bias, dist):
    tbl = rel_bias.astype(jnp.float32).reshape(REL_BUCKETS, NSA_KV_HEADS, NSA_GROUP).transpose(1, 0, 2)
    b = tbl[jnp.arange(NSA_KV_HEADS)[:, None, None], _t5_bucket(dist)]
    return jnp.moveaxis(b, -1, -3)

def _s5_combine(e1, e2):
    a1r, a1i, b1r, b1i = e1
    a2r, a2i, b2r, b2i = e2
    return (a2r * a1r - a2i * a1i, a2r * a1i + a2i * a1r,
            a2r * b1r - a2i * b1i + b2r, a2r * b1i + a2i * b1r + b2i)

def _s5_glu(u, lam_re, lam_im, log_dt, b_re, b_im, c_re, c_im, d_skip, w_glu, b_glu):
    bsz, seq_len, _ = u.shape
    f32 = jnp.float32
    uf = u.astype(f32)
    ug = uf.reshape(bsz, seq_len, S5_GROUPS, S5_GROUP)
    lr, li = lam_re.astype(f32), lam_im.astype(f32)
    dt = jnp.exp(log_dt.astype(f32))[:, None]
    mag = jnp.exp(lr * dt)
    ar, ai = mag * jnp.cos(li * dt), mag * jnp.sin(li * dt)
    den = lr * lr + li * li
    nr, ni = ar - 1.0, ai
    fr = (nr * lr + ni * li) / den
    fi = (ni * lr - nr * li) / den
    br, bi = b_re.astype(f32), b_im.astype(f32)
    bbr = fr[..., None] * br - fi[..., None] * bi
    bbi = fr[..., None] * bi + fi[..., None] * br
    bu_r = jnp.einsum('btgc,gpc->btgp', ug, bbr)
    bu_i = jnp.einsum('btgc,gpc->btgp', ug, bbi)
    a_r = jnp.broadcast_to(ar, bu_r.shape)
    a_i = jnp.broadcast_to(ai, bu_i.shape)
    _, _, xr, xi = lax.associative_scan(_s5_combine, (a_r, a_i, bu_r, bu_i), axis=1)
    y = (jnp.einsum('btgp,gcp->btgc', xr, c_re.astype(f32))
         - jnp.einsum('btgp,gcp->btgc', xi, c_im.astype(f32)))
    y = y.reshape(bsz, seq_len, S5_WIDTH) + d_skip.astype(f32) * uf
    hg = jax.nn.gelu(y)
    out = hg * jax.nn.sigmoid(hg @ w_glu.astype(f32) + b_glu.astype(f32))
    return out.astype(u.dtype)

def _fox_attention(q, k, v, f_logit, b_f):
    bsz, _, seq_len, _ = q.shape
    log_f = jax.nn.log_sigmoid(f_logit.astype(jnp.float32) + b_f.astype(jnp.float32))
    cum = jnp.cumsum(log_f, axis=1).transpose(0, 2, 1)

    def decay_bias(q0):
        cq = lax.dynamic_slice_in_dim(cum, q0, Q_BLOCK, axis=2)
        return cq[..., :, None] - cum[..., None, :]

    o = _dense_causal_attention(q, k, v, decay_bias)
    return o.transpose(0, 2, 1, 3).reshape(bsz, seq_len, FOX_HEADS * FOX_HEAD_DIM)

def _even_mixer(h, w_in, lam_re, lam_im, log_dt, b_re, b_im, c_re, c_im, d_skip, w_glu, b_glu, fox_b_f, w_out):
    bsz, seq_len, _ = h.shape
    fw = FOX_HEADS * FOX_HEAD_DIM
    u, q, k, v, f_logit = _split(h @ w_in, [S5_WIDTH, fw, fw, fw, FOX_HEADS])
    y_s5 = _s5_glu(u, lam_re, lam_im, log_dt, b_re, b_im, c_re, c_im, d_skip, w_glu, b_glu)

    def heads(t):
        return t.reshape(bsz, seq_len, FOX_HEADS, FOX_HEAD_DIM).transpose(0, 2, 1, 3)

    y_fox = _fox_attention(heads(q), heads(k), heads(v), f_logit, fox_b_f)
    return jnp.concatenate([y_s5, y_fox.astype(y_s5.dtype)], axis=-1) @ w_out

def _nsa(q, k_cmp_raw, v_cmp_raw, k_slc, v_slc, k_win, v_win, gate_logit, b_gate,
         pe_k, pe_v, k_w1, k_w2, v_w1, v_w2, rel_bias):
    bsz, seq_len, _ = q.shape
    G, R, dh = NSA_KV_HEADS, NSA_GROUP, NSA_HEAD_DIM
    scale = dh ** -0.5
    qh = q.reshape(bsz, seq_len, G, R, dh).transpose(0, 2, 3, 1, 4)

    def kv_heads(t):
        return t.reshape(bsz, seq_len, G, dh).transpose(0, 2, 1, 3)

    k_cmp_raw, v_cmp_raw, k_slc, v_slc, k_win, v_win = [
        kv_heads(t) for t in (k_cmp_raw, v_cmp_raw, k_slc, v_slc, k_win, v_win)]
    gates = jax.nn.sigmoid(gate_logit.astype(jnp.float32) + b_gate.astype(jnp.float32))
    gates = gates.reshape(bsz, seq_len, G, R, 3).transpose(0, 2, 3, 1, 4)

    n_cmp = (seq_len - CMP_LEN) // CMP_STRIDE + 1
    cmp_idx = np.arange(n_cmp)[:, None] * CMP_STRIDE + np.arange(CMP_LEN)[None, :]

    def compress(t, pe, w1, w2):
        blk = t[:, :, cmp_idx, :] + pe
        return jax.nn.gelu(blk.reshape(bsz, G, n_cmp, CMP_LEN * dh) @ w1) @ w2

    k_c = compress(k_cmp_raw, pe_k, k_w1, k_w2)
    v_c = compress(v_cmp_raw, pe_v, v_w1, v_w2)
    cmp_end = jnp.arange(n_cmp) * CMP_STRIDE + CMP_LEN - 1

    n_slc = seq_len // SLC_LEN
    ratio = SLC_LEN // CMP_STRIDE
    n_sel = min(SLC_TOPK, n_slc)
    k_sb = k_slc.reshape(bsz, G, n_slc, SLC_LEN, dh)
    v_sb = v_slc.reshape(bsz, G, n_slc, SLC_LEN, dh)
    slc_ids = jnp.arange(n_slc)
    gather_blocks = jax.vmap(jax.vmap(lambda blocks, ids: blocks[ids]))

    pad = ((0, 0), (0, 0), (WINDOW, 0), (0, 0))
    k_wp = jnp.pad(k_win, pad)
    v_wp = jnp.pad(v_win, pad)

    def block(q0):
        qb = lax.dynamic_slice_in_dim(qh, q0, Q_BLOCK, axis=3)
        qpos = q0 + jnp.arange(Q_BLOCK)
        s = jnp.einsum('bgrqd,bgnd->bgrqn', qb, k_c).astype(jnp.float32) * scale
        s = s + _t5_bias(rel_bias, qpos[:, None] - cmp_end[None, :])
        p_c = _masked_softmax(s, cmp_end[None, :] <= qpos[:, None])
        o_c = jnp.einsum('bgrqn,bgnd->bgrqd', p_c.astype(v_c.dtype), v_c)
        imp = jnp.pad(p_c.sum(axis=2), ((0, 0), (0, 0), (0, 0), (0, n_slc * ratio - n_cmp)))
        imp = imp.reshape(bsz, G, Q_BLOCK, n_slc, ratio)
        straddle = jnp.pad(imp[..., :-1, ratio - 1], ((0, 0), (0, 0), (0, 0), (1, 0)))
        imp = imp.sum(axis=-1) + straddle
        cur = (qpos // SLC_LEN)[:, None]
        forced = (slc_ids[None, :] == 0) | (slc_ids[None, :] == cur) | (slc_ids[None, :] == cur - 1)
        imp = jnp.where(slc_ids[None, :] > cur, NEG_INF, jnp.where(forced, imp + FORCED_SCORE, imp))
        vals, idx = lax.top_k(imp, n_sel)
        valid = vals > 0.5 * NEG_INF
        flat = idx.reshape(bsz, G, Q_BLOCK * n_sel)
        kg = gather_blocks(k_sb, flat).reshape(bsz, G, Q_BLOCK, n_sel * SLC_LEN, dh)
        vg = gather_blocks(v_sb, flat).reshape(bsz, G, Q_BLOCK, n_sel * SLC_LEN, dh)
        kpos = (idx[..., None] * SLC_LEN + jnp.arange(SLC_LEN)).reshape(bsz, G, Q_BLOCK, n_sel * SLC_LEN)
        smask = jnp.repeat(valid, SLC_LEN, axis=-1) & (kpos <= qpos[:, None])
        s = jnp.einsum('bgrqd,bgqkd->bgrqk', qb, kg).astype(jnp.float32) * scale
        s = s + _t5_bias(rel_bias, qpos[:, None] - kpos)
        p_s = _masked_softmax(s, smask[:, :, None])
        o_s = jnp.einsum('bgrqk,bgqkd->bgrqd', p_s.astype(vg.dtype), vg)
        kw = lax.dynamic_slice_in_dim(k_wp, q0, Q_BLOCK + WINDOW, axis=2)
        vw = lax.dynamic_slice_in_dim(v_wp, q0, Q_BLOCK + WINDOW, axis=2)
        wpos = q0 - WINDOW + jnp.arange(Q_BLOCK + WINDOW)
        dist = qpos[:, None] - wpos[None, :]
        wmask = (wpos[None, :] >= 0) & (dist >= 0) & (dist < WINDOW)
        s = jnp.einsum('bgrqd,bgkd->bgrqk', qb, kw).astype(jnp.float32) * scale
        s = s + _t5_bias(rel_bias, dist)
        p_w = _masked_softmax(s, wmask)
        o_w = jnp.einsum('bgrqk,bgkd->bgrqd', p_w.astype(vw.dtype), vw)
        g = lax.dynamic_slice_in_dim(gates, q0, Q_BLOCK, axis=3)
        return g[..., 0:1] * o_c + g[..., 1:2] * o_s + g[..., 2:3] * o_w

    o = _sweep_query_blocks(block, seq_len)
    return o.transpose(0, 3, 1, 2, 4).reshape(bsz, seq_len, NSA_HEADS * dh).astype(q.dtype)

def _odd_mixer(h, w_in, q_norm, w_uq, kv_norm, w_ukv, pe_k, pe_v, k_w1, k_w2, v_w1, v_w2, b_gate, w_out, rel_bias):
    bsz, seq_len, _ = h.shape
    pos = jnp.arange(seq_len, dtype=jnp.int32)
    kvw = NSA_KV_HEADS * NSA_HEAD_DIM
    c_q, c_kv, k_rope, q_n, k_c, v_c, k_s, v_s, k_w, v_w, g_logit = _split(
        h @ w_in, [MLA_Q_RANK, MLA_KV_RANK, MLA_ROPE_DIM, NSA_HEADS * NSA_HEAD_DIM,
                   kvw, kvw, kvw, kvw, kvw, kvw, 3 * NSA_HEADS])
    q = (_rmsnorm(c_q, q_norm) @ w_uq).reshape(bsz, seq_len, MLA_HEADS, MLA_NOPE_DIM + MLA_ROPE_DIM)
    q = jnp.concatenate([q[..., :MLA_NOPE_DIM], _rope(q[..., MLA_NOPE_DIM:], pos)], axis=-1)
    kv = (_rmsnorm(c_kv, kv_norm) @ w_ukv).reshape(bsz, seq_len, MLA_HEADS, MLA_NOPE_DIM + MLA_V_DIM)
    k_r = jnp.broadcast_to(_rope(k_rope[:, :, None, :], pos), (bsz, seq_len, MLA_HEADS, MLA_ROPE_DIM))
    k = jnp.concatenate([kv[..., :MLA_NOPE_DIM], k_r], axis=-1)
    v = kv[..., MLA_NOPE_DIM:]
    y_mla = _dense_causal_attention(q.transpose(0, 2, 1, 3), k.transpose(0, 2, 1, 3), v.transpose(0, 2, 1, 3))
    y_mla = y_mla.transpose(0, 2, 1, 3).reshape(bsz, seq_len, MLA_HEADS * MLA_V_DIM)
    y_nsa = _nsa(q_n, k_c, v_c, k_s, v_s, k_w, v_w, g_logit, b_gate, pe_k, pe_v, k_w1, k_w2, v_w1, v_w2, rel_bias)
    return jnp.concatenate([y_mla, y_nsa.astype(y_mla.dtype)], axis=-1) @ w_out

def setup_inputs(seed: int = 0) -> dict:
    key = jax.random.key(seed)
    keys = iter(jax.random.split(key, 128))
    f32 = jnp.float32

    def nrm(shape, scale):
        return scale * jax.random.normal(next(keys), shape, f32)

    def gain(n):
        return 1.0 + 0.05 * jax.random.normal(next(keys), (n,), f32)

    def ffn(d, prefix):
        d[prefix + '_norm'] = gain(D_MODEL)
        d[prefix + '_w_gate'] = nrm((D_MODEL, D_FF), D_MODEL ** -0.5)
        d[prefix + '_w_up'] = nrm((D_MODEL, D_FF), D_MODEL ** -0.5)
        d[prefix + '_w_down'] = nrm((D_FF, D_MODEL), D_FF ** -0.5)

    d = {}
    d['x'] = nrm((BATCH, SEQ, D_MODEL), 1.0)
    d['rel_bias'] = nrm((REL_BUCKETS, NSA_HEADS), 0.5)
    ffn(d, 'l0_ffn1')
    d['l0_mix_norm'] = gain(D_MODEL)
    d['l0_w_in'] = nrm((D_MODEL, EVEN_IN), D_MODEL ** -0.5)
    d['l0_s5_lambda_re'] = -0.5 + nrm((S5_GROUPS, S5_STATE), 0.01)
    d['l0_s5_lambda_im'] = jnp.pi * jnp.arange(S5_STATE, dtype=f32)[None, :] + nrm((S5_GROUPS, S5_STATE), 0.01)
    d['l0_s5_log_dt'] = jax.random.uniform(next(keys), (S5_GROUPS,), f32, math.log(1e-3), math.log(1e-1))
    d['l0_s5_b_re'] = nrm((S5_GROUPS, S5_STATE, S5_GROUP), (2 * S5_GROUP) ** -0.5)
    d['l0_s5_b_im'] = nrm((S5_GROUPS, S5_STATE, S5_GROUP), (2 * S5_GROUP) ** -0.5)
    d['l0_s5_c_re'] = nrm((S5_GROUPS, S5_GROUP, S5_STATE), S5_STATE ** -0.5)
    d['l0_s5_c_im'] = nrm((S5_GROUPS, S5_GROUP, S5_STATE), S5_STATE ** -0.5)
    d['l0_s5_d'] = nrm((S5_WIDTH,), 1.0)
    d['l0_s5_w_glu'] = nrm((S5_WIDTH, S5_WIDTH), S5_WIDTH ** -0.5)
    d['l0_s5_b_glu'] = nrm((S5_WIDTH,), 0.01)
    d['l0_fox_b_f'] = 2.0 + nrm((FOX_HEADS,), 0.5)
    d['l0_w_out'] = nrm((EVEN_OUT, D_MODEL), EVEN_OUT ** -0.5)
    ffn(d, 'l0_ffn2')
    ffn(d, 'l1_ffn1')
    d['l1_mix_norm'] = gain(D_MODEL)
    d['l1_w_in'] = nrm((D_MODEL, ODD_IN), D_MODEL ** -0.5)
    d['l1_mla_q_norm'] = gain(MLA_Q_RANK)
    d['l1_mla_w_uq'] = nrm((MLA_Q_RANK, MLA_HEADS * (MLA_NOPE_DIM + MLA_ROPE_DIM)), MLA_Q_RANK ** -0.5)
    d['l1_mla_kv_norm'] = gain(MLA_KV_RANK)
    d['l1_mla_w_ukv'] = nrm((MLA_KV_RANK, MLA_HEADS * (MLA_NOPE_DIM + MLA_V_DIM)), MLA_KV_RANK ** -0.5)
    d['l1_nsa_cmp_pe_k'] = nrm((CMP_LEN, NSA_HEAD_DIM), 0.1)
    d['l1_nsa_cmp_pe_v'] = nrm((CMP_LEN, NSA_HEAD_DIM), 0.1)
    d['l1_nsa_cmp_k_w1'] = nrm((CMP_LEN * NSA_HEAD_DIM, CMP_HIDDEN), (CMP_LEN * NSA_HEAD_DIM) ** -0.5)
    d['l1_nsa_cmp_k_w2'] = nrm((CMP_HIDDEN, NSA_HEAD_DIM), CMP_HIDDEN ** -0.5)
    d['l1_nsa_cmp_v_w1'] = nrm((CMP_LEN * NSA_HEAD_DIM, CMP_HIDDEN), (CMP_LEN * NSA_HEAD_DIM) ** -0.5)
    d['l1_nsa_cmp_v_w2'] = nrm((CMP_HIDDEN, NSA_HEAD_DIM), CMP_HIDDEN ** -0.5)
    d['l1_nsa_b_gate'] = nrm((3 * NSA_HEADS,), 0.1)
    d['l1_w_out'] = nrm((ODD_OUT, D_MODEL), ODD_OUT ** -0.5)
    ffn(d, 'l1_ffn2')
    d['final_norm'] = gain(D_MODEL)
    return d

def reference(x, rel_bias,
              l0_ffn1_norm, l0_ffn1_w_gate, l0_ffn1_w_up, l0_ffn1_w_down,
              l0_mix_norm, l0_w_in, l0_s5_lambda_re, l0_s5_lambda_im, l0_s5_log_dt,
              l0_s5_b_re, l0_s5_b_im, l0_s5_c_re, l0_s5_c_im, l0_s5_d, l0_s5_w_glu, l0_s5_b_glu,
              l0_fox_b_f, l0_w_out,
              l0_ffn2_norm, l0_ffn2_w_gate, l0_ffn2_w_up, l0_ffn2_w_down,
              l1_ffn1_norm, l1_ffn1_w_gate, l1_ffn1_w_up, l1_ffn1_w_down,
              l1_mix_norm, l1_w_in, l1_mla_q_norm, l1_mla_w_uq, l1_mla_kv_norm, l1_mla_w_ukv,
              l1_nsa_cmp_pe_k, l1_nsa_cmp_pe_v, l1_nsa_cmp_k_w1, l1_nsa_cmp_k_w2,
              l1_nsa_cmp_v_w1, l1_nsa_cmp_v_w2, l1_nsa_b_gate, l1_w_out,
              l1_ffn2_norm, l1_ffn2_w_gate, l1_ffn2_w_up, l1_ffn2_w_down,
              final_norm):
    layers = (
        ((l0_ffn1_norm, l0_ffn1_w_gate, l0_ffn1_w_up, l0_ffn1_w_down),
         (l0_mix_norm, l0_w_in, l0_s5_lambda_re, l0_s5_lambda_im, l0_s5_log_dt, l0_s5_b_re, l0_s5_b_im,
          l0_s5_c_re, l0_s5_c_im, l0_s5_d, l0_s5_w_glu, l0_s5_b_glu, l0_fox_b_f, l0_w_out),
         (l0_ffn2_norm, l0_ffn2_w_gate, l0_ffn2_w_up, l0_ffn2_w_down)),
        ((l1_ffn1_norm, l1_ffn1_w_gate, l1_ffn1_w_up, l1_ffn1_w_down),
         (l1_mix_norm, l1_w_in, l1_mla_q_norm, l1_mla_w_uq, l1_mla_kv_norm, l1_mla_w_ukv,
          l1_nsa_cmp_pe_k, l1_nsa_cmp_pe_v, l1_nsa_cmp_k_w1, l1_nsa_cmp_k_w2,
          l1_nsa_cmp_v_w1, l1_nsa_cmp_v_w2, l1_nsa_b_gate, l1_w_out),
         (l1_ffn2_norm, l1_ffn2_w_gate, l1_ffn2_w_up, l1_ffn2_w_down)),
    )
    h = x
    for i in range(DEPTH):
        ffn1, mix, ffn2 = layers[i]
        h = h + HALF_STEP * _swiglu(_rmsnorm(h, ffn1[0]), *ffn1[1:])
        hn = _rmsnorm(h, mix[0])
        if i % 2 == 0:
            h = h + _even_mixer(hn, *mix[1:])
        else:
            h = h + _odd_mixer(hn, *mix[1:], rel_bias)
        h = h + HALF_STEP * _swiglu(_rmsnorm(h, ffn2[0]), *ffn2[1:])
    return _rmsnorm(h, final_norm)


_drawn_inputs = setup_inputs


def setup_inputs(seed=0):
    import zlib

    import numpy as np

    out = dict(_drawn_inputs(seed))
    spreads = {}
    factors = {'l0_s5_lambda_re': 64.0,
     'l0_s5_lambda_im': 3.057,
     'l0_s5_log_dt': 3.148,
     'l0_s5_b_re': 4.279,
     'l0_s5_b_im': 4.33,
     'l0_s5_c_re': 4.178,
     'l0_s5_c_im': 4.356,
     'l0_s5_b_glu': 8.0,
     'l0_ffn2_norm': 2.909,
     'l1_ffn1_norm': 3.013,
     'l1_mix_norm': 3.571,
     'l1_mla_q_norm': 8.0,
     'l1_mla_kv_norm': 6.502,
     'l1_nsa_cmp_pe_k': 8.0,
     'l1_nsa_cmp_pe_v': 11.765,
     'l1_nsa_b_gate': 5.585,
     'l1_ffn2_norm': 3.234}
    for name, (base, spread) in spreads.items():
        noise = np.random.default_rng([zlib.crc32(name.encode()), seed]).standard_normal(out[name].shape)
        drawn = base * np.exp(spread * noise) if base else spread * noise
        out[name] = __import__('jax').numpy.asarray(drawn.astype(out[name].dtype))
    for name, factor in factors.items():
        out[name] = (out[name] * factor).astype(out[name].dtype)
    return out
```

```python
import math
from contextlib import ExitStack

import concourse.bass as bass
from concourse import mybir

F32 = mybir.dt.float32
F32R = mybir.dt.float32r
ALU = mybir.AluOpType
ACT = mybir.ActivationFunctionType
AX = mybir.AxisListType

P = 128
D = 1024
SEQ = 256
KD = D // P
TT = SEQ // P
D_FF = 2816
CH = D_FF // P
EPS = 1e-6
PHASES = ['ffn0', 'mix0', 'ffn1', 'ffn2', 'mix1', 'ffn3', 'final']

S5_WIDTH = D // 2
S5_GROUP = 16
S5_STATE = 64
LANES = 2 * S5_STATE
SG = S5_WIDTH // S5_GROUP // 2
UB = S5_WIDTH // P
PER = SG // UB
GC = 2 * S5_GROUP
HEADS = 8
DH = 64
PAIRS = HEADS // 2
F_ROWS = 104
MASKED = -1e30
ARENA = 15360
RING = 3
ATT_COLS = 3 * P
KEYS = [slice(0, P), slice(P, 3 * P)]

Q_RANK = 384
KV_RANK = 256
QB = Q_RANK // P
KVB = KV_RANK // P
LB = QB + KVB
ROPE = 32
GROUPS = 2
REP = HEADS // GROUPS
CMP_LEN = 32
CMP_STRIDE = 16
N_CMP = (SEQ - CMP_LEN) // CMP_STRIDE + 1
CMP_PAIRS = CMP_LEN // 2
T5_COLS = 3 * P
BUCKETS = 32
OC = {'rope': slice(0, 256), 'sel': slice(256, 320), 'mask': slice(320, 352), 'block': slice(352, 360)}
N_OC = 360

PARAMS = {}
_at = 0
for _name, _n in [('gain', len(PHASES) * KD), ('lam_re', SG), ('lam_im', SG), ('log_dt', SG), ('d_skip', UB), ('b_glu', UB),
                  ('b_f', 1), ('fox_a', HEADS), ('fox_b', HEADS), ('fox_l', 2), ('q_norm', 3), ('kv_norm', 2),
                  ('b_gate', 24), ('pe', 32), ('w2', 128), ('rel', 8)]:
    PARAMS[_name] = slice(_at, _at + _n)
    _at += _n
N_PARAMS = _at

MAG = 1
MAGIC = 12582912.0
TWO_PI = (6.28125, 1.93500518798828125e-3, 3.01991598196765e-7)
LN2 = (0.693359375, -2.12194440e-4)
NORM = {p: m for m, p in enumerate(PHASES)}
XF = {p: m for m, p in enumerate([p for p in PHASES if not p.startswith('ffn')])}


def trunk(nc, x_t, w_gate_up, w_down, params, s5_bc, mix_units, ident_in, causal_in, odd_consts, onehot, t5_rows, out):
    phases = PHASES
    with ExitStack() as ctx:
        def sb(name, shape, dt=F32):
            return ctx.enter_context(nc.sbuf_tensor(name, shape, dt))

        def sem(name):
            return ctx.enter_context(nc.semaphore(name))

        h = sb('h', [P, KD, SEQ])
        xf = sb('xf', [P, KD, SEQ])
        xh = sb('xh', [P, KD, SEQ], F32R)
        xl = sb('xl', [P, KD, SEQ], F32R)
        sq = sb('sq', [P, KD, SEQ])
        raw_gu = sb('raw_gu', [P, 2, 2 * KD * P])
        raw_d = sb('raw_d', [P, 2, D])
        hi_gu = sb('hi_gu', [P, 2, 2 * KD * P], F32R)
        lo_gu = sb('lo_gu', [P, 2, 2 * KD * P], F32R)
        hi_d = sb('hi_d', [P, 2, D], F32R)
        lo_d = sb('lo_d', [P, 2, D], F32R)
        scratch = sb('scratch', [P, 10 * SEQ])
        gs = scratch[:, 0:4 * SEQ].rearrange('p (s a t) -> p s a t', s=2, a=2)
        th = scratch[:, 4 * SEQ:6 * SEQ].rearrange('p (s t) -> p s t', s=2)
        ga = scratch[:, 6 * SEQ:8 * SEQ].rearrange('p (s t) -> p s t', s=2)
        diag = scratch[:, 0:TT * P].rearrange('p (t n) -> p t n', t=TT)
        prod = scratch[:, 8 * SEQ:10 * SEQ].rearrange('p (s t) -> p s t', s=2)
        ph = sb('ph', [P, 2, SEQ], F32R)
        pl = sb('pl', [P, 2, SEQ], F32R)
        par = sb('par', [P, N_PARAMS])
        gain = par[:, PARAMS['gain']].rearrange('p (m k) -> p m k', k=KD)
        ring = sb('ring', [P, RING, D])
        causal = sb('causal', [P, ATT_COLS], mybir.dt.bfloat16)
        arena = sb('arena', [P, ARENA])
        ident = sb('ident', [P, P])
        ones = sb('ones', [P, P])
        halves = sb('halves', [P, 4])
        ms = sb('ms', [P, TT])
        rstd = sb('rstd', [P, TT])
        rbc = sb('rbc', [P, SEQ])
        o_sb = raw_gu[:, :, 0:D]

        at = 0

        def region(n):
            nonlocal at
            at += n
            assert at <= ARENA
            return arena[:, at - n:at]

        cos_t = region(SG * SEQ).rearrange('p (j t) -> p j t', j=SG)
        sin_t = region(SG * SEQ).rearrange('p (j t) -> p j t', j=SG)
        u_t = region(UB * SEQ).rearrange('p (b t) -> p b t', b=UB)
        q_t = region(PAIRS * SEQ).rearrange('p (b t) -> p b t', b=PAIRS)
        k_t = region(PAIRS * SEQ).rearrange('p (b t) -> p b t', b=PAIRS)
        v_n = region(TT * HEADS * DH).rearrange('p (t n) -> p t n', t=TT)
        b_t = region(2 * UB * P).rearrange('p (c b n) -> p c b n', c=2, b=UB)
        c_d = region(2 * SG * GC).rearrange('p (c j n) -> p c j n', c=2, j=SG)
        cum = region(SEQ)
        fox_lhs = region(SEQ)
        fox_rhs = region(2 * SEQ).rearrange('p (s t) -> p s t', s=2)
        s5z = sb('s5z', [P, 4 * SEQ])
        small = sb('small', [P, 13, SG])
        s5_out = arena[:, 0:UB * SEQ].rearrange('p (b t) -> p b t', b=UB)
        quarter = arena[:, UB * SEQ:2 * UB * SEQ].rearrange('p (b t) -> p b t', b=UB)
        at = 0
        t5 = region(HEADS * T5_COLS).rearrange('p (h x) -> p h x', h=HEADS)
        lat = region(LB * SEQ).rearrange('p (b t) -> p b t', b=LB)
        mq = region(HEADS * SEQ).rearrange('p (h t) -> p h t', h=HEADS)
        mk = region(HEADS * SEQ).rearrange('p (h t) -> p h t', h=HEADS)
        mv = region(TT * HEADS * DH).rearrange('p (t n) -> p t n', t=TT)
        nq = region(REP * SEQ).rearrange('p (r t) -> p r t', r=REP)
        kv_raw = region(2 * SEQ).rearrange('p (c t) -> p c t', c=2)
        ksw = region(2 * SEQ).rearrange('p (c t) -> p c t', c=2)
        vsw = region(TT * 2 * P).rearrange('p (t n) -> p t n', t=TT)
        win = region(4 * SEQ).rearrange('p (c g t) -> p c g t', c=2, g=GROUPS)
        blk = region(2 * CMP_PAIRS * GROUPS * N_CMP).rearrange('p (c i g n) -> p c i g n', c=2, i=CMP_PAIRS, g=GROUPS)
        oc = region(N_OC)
        kr = region(SEQ)
        hid = region(4 * N_CMP).rearrange('p (a n) -> p a n', a=2)
        hid_t = region(4 * N_CMP).rearrange('p (a n) -> p a n', a=2)
        hid_v = region(P)
        rope = oc[:, OC['rope']]
        t5_onehot = mv[:, 0, :]
        t5_row = mv[:, 1, :]
        v_block = s5z[:, 0:HEADS * DH].rearrange('p (h d) -> p h d', h=HEADS)
        pc = s5z[:, 512:768].rearrange('p (t h n) -> p t h n', t=TT, h=HEADS)
        pc_t = s5z[:, 768:1024]
        sflat = small[:].rearrange('p a b -> p (a b)')
        gates = sflat[:, 0:48].rearrange('p (t n) -> p t n', t=TT)
        logits = sflat[:, 48:96].rearrange('p (t n) -> p t n', t=TT)
        kc = sflat[:, 96:96 + N_CMP]
        c_max = sflat[:, 112:128].rearrange('p (t h) -> p t h', t=TT)
        c_sum = sflat[:, 128:144].rearrange('p (t h) -> p t h', t=TT)
        lat_ms = sflat[:, 144:148]
        lat_rstd = sflat[:, 148:152]
        lat_diag = scratch[:, 0:4 * P].rearrange('p (t n) -> p t n', t=4)
        bc_raw = k_t.rearrange('p b t -> p (b t)').rearrange('p (c j n) -> p c j n', c=4, j=SG)
        b_blocks = v_n.rearrange('p t n -> p (t n)').rearrange('p (c j n) -> p c j n', c=2, j=SG)
        tmp1 = arena[:, 2 * SG * SEQ:2 * SG * SEQ + SG * P].rearrange('p (j t) -> p j t', j=SG)
        tmp2 = sq[:].rearrange('p k t -> p (k t)').rearrange('p (j t) -> p j t', j=SG)
        sqf = sq[:].rearrange('p k t -> p (k t)')
        bu = [sqf[:, 2 * i * SEQ:2 * (i + 1) * SEQ].rearrange('p (c t) -> p c t', c=2) for i in range(2)]
        cos_in = sqf[:, 4 * SEQ:6 * SEQ].rearrange('p (c t) -> p c t', c=2)
        sin_in = sqf[:, 6 * SEQ:8 * SEQ].rearrange('p (c t) -> p c t', c=2)
        sin_out = scratch[:, 5 * ATT_COLS:5 * ATT_COLS + 2 * SEQ].rearrange('p (c t) -> p c t', c=2)
        states = [s5z[:, 2 * i * SEQ:2 * (i + 1) * SEQ].rearrange('p (c t) -> p c t', c=2) for i in range(2)]
        probs = [scratch[:, i * ATT_COLS:(i + 1) * ATT_COLS] for i in range(3)]
        probs_t = [scratch[:, (3 + i) * ATT_COLS:(4 + i) * ATT_COLS] for i in range(2)]
        states_tanh = sin_t[:, 0:SG:PER, :]
        minus_one = sb('minus_one', [P, SG])
        half_b = sb('half_b', [P, UB])
        stats = sb('stats', [P, 3, 3, TT])

        bank = [ctx.enter_context(nc.psum_tensor(f'bank{i}', [P, 512], F32)) for i in range(8)]

        def acc(j):
            return bank[j // 2][:, (j % 2) * SEQ:(j % 2 + 1) * SEQ]

        GU = [bank[4], bank[5]]
        misc = bank[7]
        final_bank = [[bank[4], bank[5]], [bank[6], bank[0]]]

        params_in = sem('params_in')
        x_in = [sem('x_in0'), sem('x_in1')]
        first_gate_in = sem('first_gate_in')
        ident_loaded = sem('ident_loaded')
        tables_in = sem('tables_in')
        raw_gu_in = [sem('raw_gu_in0'), sem('raw_gu_in1')]
        raw_d_in = [sem('raw_d_in0'), sem('raw_d_in1')]
        gu_hi = sem('gu_hi')
        gu_lo = sem('gu_lo')
        d_hi = sem('d_hi')
        d_lo = sem('d_lo')
        consts_set = sem('consts_set')
        h_ready = sem('h_ready')
        xf_ready = sem('xf_ready')
        sq_ready = sem('sq_ready')
        x_hi = sem('x_hi')
        x_lo = sem('x_lo')
        ss_done = sem('ss_done')
        ms_ready = sem('ms_ready')
        rstd_ready = sem('rstd_ready')
        diag_ready = sem('diag_ready')
        rbc_done = sem('rbc_done')
        rbc_ready = sem('rbc_ready')
        gateup_done = sem('gateup_done')
        gate_scaled = sem('gate_scaled')
        tanh_done = sem('tanh_done')
        a_ready = sem('a_ready')
        prod_ready = sem('prod_ready')
        ph_ready = sem('ph_ready')
        act_lo = sem('act_lo')
        down_done = sem('down_done')
        unit_in = [sem(f'unit_in{i}') for i in range(RING)]
        unit_used = sem('unit_used')
        s5_prep = sem('s5_prep')
        b_t_done = sem('b_t_done')
        b_t_ready = sem('b_t_ready')
        proj_read = sem('proj_read')
        v_ready = sem('v_ready')
        f_x = sem('f_x')
        f_neg = sem('f_neg')
        f_exp = sem('f_exp')
        f_ln = sem('f_ln')
        f_log = sem('f_log')
        cum_ready = sem('cum_ready')
        fox_lhs_ready = sem('fox_lhs_ready')
        fox_rhs_ready = sem('fox_rhs_ready')
        scores_done = sem('scores_done')
        biased = sem('biased')
        neg_max = sem('neg_max')
        exp_done = sem('exp_done')
        factor = sem('factor')
        probs_ready = sem('probs_ready')
        probs_t_done = sem('probs_t_done')
        probs_t_ready = sem('probs_t_ready')
        heads_done = sem('heads_done')
        heads_out = sem('heads_out')
        bu_done = sem('bu_done')
        bu_ready = sem('bu_ready')
        cos_in_ready = sem('cos_in_ready')
        sin_in_ready = sem('sin_in_ready')
        zin_ready = sem('zin_ready')
        scanned = sem('scanned')
        cos_out_ready = sem('cos_out_ready')
        sin_out_ready = sem('sin_out_ready')
        state_ready = sem('state_ready')
        y_done = sem('y_done')
        y_read = sem('y_read')
        y_square = sem('y_square')
        y_inner = sem('y_inner')
        gelu_tanh = sem('gelu_tanh')
        gelu_ready = sem('gelu_ready')
        quarter_ready = sem('quarter_ready')
        glu_done = sem('glu_done')
        glu_tanh = sem('glu_tanh')
        s5_ready = sem('s5_ready')
        mix_done = sem('mix_done')
        tables_ready = sem('tables_ready')
        t5_copied = sem('t5_copied')
        t5_stored = sem('t5_stored')
        t5_in = sem('t5_in')
        odd_in = sem('odd_in')
        lat_squared = sem('lat_squared')
        lat_ss_done = sem('lat_ss_done')
        lat_ms_ready = sem('lat_ms_ready')
        lat_rstd_ready = sem('lat_rstd_ready')
        lat_diag_ready = sem('lat_diag_ready')
        lat_spread_done = sem('lat_spread_done')
        lat_ready = sem('lat_ready')
        krope_scaled = sem('krope_scaled')
        krope_ready = sem('krope_ready')
        krope_done = sem('krope_done')
        krope_copied = sem('krope_copied')
        logits_read = sem('logits_read')
        gate_tanh = sem('gate_tanh')
        gates_ready = sem('gates_ready')
        windows_in = sem('windows_in')
        blocks_ready = sem('blocks_ready')
        hid_read = sem('hid_read')
        hid_square = sem('hid_square')
        hid_inner = sem('hid_inner')
        hid_tanh = sem('hid_tanh')
        hid_ready = sem('hid_ready')
        hid_v_ready = sem('hid_v_ready')
        cmp_made = sem('cmp_made')
        kc_ready = sem('kc_ready')
        v_block_ready = sem('v_block_ready')
        cmp_scored = sem('cmp_scored')
        cmp_step = sem('cmp_step')
        cmp_exp = sem('cmp_exp')
        cmp_ready = sem('cmp_ready')
        cmp_turned = sem('cmp_turned')
        pc_t_ready = sem('pc_t_ready')
        cmp_weighed = sem('cmp_weighed')
        mla_v_ready = sem('mla_v_ready')
        many_done = sem('many_done')
        even_done = sem('even_done')
        final_t = sem('final_t')
        scaled_dve = sem('scaled_dve')
        scaled_act = sem('scaled_act')
        stored = sem('stored')

        n_ffn = sum(p.startswith('ffn') for p in phases)

        def pairs(eng, step, n):
            c0 = CH * n
            lead = 1 if n == 0 else 0
            tail = 1 if n == n_ffn - 1 else 0
            if lead:
                step(0, 0, 0)
                step(1, 1, 0)
            with eng.Fori(lead, CH // 2 - tail) as i:
                step(c0 + 2 * i, 0, c0 // 2 + i)
                step(c0 + 2 * i + 1, 1, c0 // 2 + i)
            if tail:
                c = c0 + CH - 2
                step(c, 0, c // 2, more_gu=False)
                step(c + 1, 1, c // 2, more_gu=False, more_d=False)

        even = [('b_t', 0), ('u', 0), ('squares', 0), ('u', 1), ('spread', 0), ('u', 2), ('u', 3), ('f', 0)]
        inputs = [(x, i) for i in range(PAIRS) for x in 'qk'] + [('v', i) for i in range(4)]
        att = [('fox', s) for s in range(HEADS + 3)]
        for j in range(SG + 3):
            if inputs:
                even.append(inputs.pop(0))
            else:
                even.append(att.pop(0))
            even.append(('s5', j))
            if j % PER == 2 and j > PER:
                even.append(('gelu', j // PER - 1))
        even += att + [('out', i) for i in range(4)] + [('glu', i) for i in range(4)] + [('out', 4 + i) for i in range(4)]
        assert not inputs
        EVEN = {'u': 0, 'f': 4, 'qk': 5, 'v': 13, 'out': 17, 'glu': 21}
        even_units = 27
        ODD = {'cq': 0, 'ckv': 3, 'krg': 5, 'nq': 6, 'kv': 10, 'vsw': 14, 'uq': 16, 'uk': 20, 'uv': 21, 'w1': 22, 'out': 26}
        odd_units = 34
        odd = [('t5', 0), ('cq', 0), ('squares', 0), ('cq', 1), ('spread', 0), ('cq', 2), ('ckv', 0), ('ckv', 1), ('krg', 0),
               ('nq', 0), ('lat_squares', 0), ('nq', 1), ('sel', 0), ('nq', 2), ('lat_spread', 0), ('nq', 3)]
        odd += [('kv', i) for i in range(4)] + [('vsw', i) for i in range(2)] + [('uq', i) for i in range(HEADS)]
        odd += [('uk', i) for i in range(HEADS)] + [('uv', 0)]
        odd_heads = 3 * HEADS
        between = {0: ('w1', 0), 1: ('w1', 1), 2: ('w1', 2), 3: ('w1', 3), 4: ('hidden', 0), 6: ('compress', 0),
                   7: ('cmp_scores', 0), 8: ('cmp_softmax', 0), 9: ('cmp_turn', 0)}
        for s in range(odd_heads + 3):
            odd.append(('att', s))
            if s in between:
                odd.append(between[s])
        odd += [('out', i) for i in range(KD)]
        has_even = 'mix0' in phases
        units_before = {'mix0': 0, 'mix1': even_units if has_even else 0}
        units_of = {'mix0': even_units, 'mix1': odd_units}
        v0 = TT if has_even else 0
        o_bank = bank[7]
        small_ps = bank[1]
        heads0 = HEADS if has_even else 0
        reads0 = UB + 1 + 2 * PAIRS if has_even else 0
        out0 = PAIRS if has_even else 0
        gated = sem('gated')
        mixes0 = KD - 1 if has_even else 0

        def nsa(s):
            return s // 4, s // 2 % 2, s % 2

        block = ctx.enter_context(nc.Block())

        @block.sync
        def _(sp):
            def load_gu(c, s):
                sp.dma_start(raw_gu[:, s, :], w_gate_up[bass.ds(c, 1)].rearrange('o p n -> (o p) n')).then_inc(raw_gu_in[s], 16)

            def load_d(c, s):
                sp.dma_start(raw_d[:, s, :], w_down[bass.ds(c, 1)].rearrange('o p n -> (o p) n')).then_inc(raw_d_in[s], 16)

            def load_pairs(first, count):
                with sp.Fori(first, first + count) as i:
                    for s in range(2):
                        sp.wait_ge(gu_lo, 2 * (2 * i + s - 1))
                        load_gu(2 * i + s, s)
                        sp.wait_ge(d_lo, 2 * i + s - 1)
                        load_d(2 * i + s, s)

            sp.dma_start(par[:], params).then_inc(params_in, 16)
            for half in range(2):
                ks = slice(half * KD // 2, (half + 1) * KD // 2)
                sp.dma_start(h[:, ks, :], x_t[:, ks, :]).then_inc(x_in[half], 16)
            sp.dma_start(raw_gu[:, 0, 0:D], w_gate_up[0, :, 0:D]).then_inc(first_gate_in, 16)
            sp.dma_start(raw_gu[:, 0, D:2 * D], w_gate_up[0, :, D:2 * D]).then_inc(raw_gu_in[0], 16)
            sp.dma_start(ident[:], ident_in).then_inc(ident_loaded, 16)
            load_d(0, 0)
            load_gu(1, 1)
            load_d(1, 1)
            def load_unit(u, slot):
                sp.dma_start(ring[:, slot, :], mix_units[bass.ds(u, 1)].rearrange('o p n -> (o p) n')).then_inc(unit_in[slot], 16)

            def load_units(first, count):
                for u in range(first, first + count):
                    if u >= RING:
                        sp.wait_ge(unit_used, u - RING + 1)
                    load_unit(u, u % RING)

            sp.dma_start(arena[:, 2 * SG * SEQ + 2 * UB * SEQ:2 * SG * SEQ + 3 * UB * SEQ], s5_bc).then_inc(tables_in, 16)
            sp.dma_start(causal[:], causal_in).then_inc(tables_in, 16)
            n = 0
            first = 1
            for p in phases:
                if p.startswith('ffn'):
                    n += 1
                    last = CH // 2 * n + (1 if n < n_ffn else 0)
                    load_pairs(first, last - first)
                    first = last
                elif p.startswith('mix'):
                    load_units(units_before[p], units_of[p])

            for i in range(2):
                for t, scaled in enumerate((scaled_dve, scaled_act)):
                    cols = slice(i * 512, (i + 1) * 512)
                    sp.wait_ge(scaled, i + 1)
                    sp.dma_start(out[t * P:(t + 1) * P, cols], o_sb[:, t, cols]).then_inc(stored, 16)
            sp.wait_ge(stored, 64)

        @block.tensor
        def _(pe):
            def product3(dst, w_hi, w_lo, x_hi_ap, x_lo_ap, start, stop):
                nc.tensor.matmul(dst, w_hi, x_hi_ap, start=start, stop=False, skip_group_check=True)
                nc.tensor.matmul(dst, w_hi, x_lo_ap, start=False, stop=False, skip_group_check=True)
                return nc.tensor.matmul(dst, w_lo, x_hi_ap, start=False, stop=stop, skip_group_check=True)

            def square_sums(m):
                for t in range(TT):
                    for k in range(KD):
                        if t == 0:
                            pe.wait_ge(sq_ready, KD * m + k + 1)
                        last = nc.tensor.matmul(misc[:, t:t + 1], sq[:, k, t * P:(t + 1) * P], ones[:, 0:1],
                                                start=(k == 0), stop=(k == KD - 1))
                last.then_inc(ss_done, 1)

            def spread_rstd(m):
                pe.wait_ge(diag_ready, TT * (m + 1))
                for t in range(TT):
                    last = nc.tensor.matmul(misc[:, SEQ + t * P:SEQ + (t + 1) * P], ones[:], diag[:, t, :],
                                            start=True, stop=True)
                last.then_inc(rbc_done, 1)

            def gateup(c, s, first=None, second=None):
                if not (isinstance(c, int) and c < 2):
                    pe.wait_ge(gate_scaled, c - 1)
                pe.wait_ge(gu_lo, 2 * c + 1)
                order = [(half, k) for half in range(2) for k in range(KD)]
                if first:
                    order = [(half, k) for k in range(KD) for half in range(2)]
                for at_, (half, k) in enumerate(order):
                    if first is not None and half == 0:
                        pe.wait_ge(x_lo, KD * first + k + 1)
                    if at_ == (1 if first else KD):
                        pe.wait_ge(gu_lo, 2 * c + 2)
                    if second is not None and at_ == KD:
                        spread_rstd(norm_of[second])
                    w = slice((half * KD + k) * P, (half * KD + k + 1) * P)
                    last = product3(GU[s][:, half * SEQ:(half + 1) * SEQ], hi_gu[:, s, w], lo_gu[:, s, w],
                                    xh[:, k, :], xl[:, k, :], at_ == 0, False)
                last.then_inc(gateup_done, 1)
                if first is not None:
                    square_sums(norm_of[first])

            def down(c, s, first=False):
                pe.wait_ge(act_lo, c + 1)
                pe.wait_ge(d_lo, c + 1)
                for j in range(KD):
                    w = slice(j * P, (j + 1) * P)
                    product3(acc(j), hi_d[:, s, w], lo_d[:, s, w], ph[:, s, :], pl[:, s, :],
                             first and j % 2 == 0, False).then_inc(down_done, 1)

            norm_of = [NORM[p] for p in phases if p.startswith('ffn')]

            def ffn(n):
                c0 = CH * n
                gateup(c0, 0, first=n)
                gateup(c0 + 1, 1, second=n)
                down(c0, 0, first=True)
                with pe.Fori(0, CH // 2 - 1) as i:
                    gateup(c0 + 2 * i + 2, 0)
                    down(c0 + 2 * i + 1, 1)
                    gateup(c0 + 2 * i + 3, 1)
                    down(c0 + 2 * i + 2, 0)
                down(c0 + CH - 1, 1)

            def final():
                m = NORM['final']
                for k in range(KD):
                    pe.wait_ge(xf_ready, KD * XF['final'] + k + 1)
                    for t in range(TT):
                        last = nc.tensor.transpose(final_bank[k // 4][t][:, (k % 4) * P:(k % 4 + 1) * P],
                                                   xf[:, k, t * P:(t + 1) * P], ident[:])
                    if k % 4 == 3:
                        last.then_inc(final_t, 1)
                square_sums(m)

            def unit(u):
                pe.wait_ge(unit_in[u % RING], 16 * (u // RING) + 16)
                return ring[:, u % RING, :]

            def project(u, it, m, rows=P, cols=P, at=0, fenced=False):
                w = unit(u)
                if it >= 2 and not fenced:
                    pe.wait_ge(proj_read, it - 1)
                for k in range(KD):
                    pe.wait_ge(xf_ready, KD * XF[phases[m]] + k + 1)
                    last = nc.tensor.matmul(GU[it % 2][at:at + rows, 0:SEQ], w[:, k * cols:(k + 1) * cols], xf[:, k, :],
                                            start=(k == 0), stop=(k == KD - 1))
                return last

            def scores(g, q, k, more=None):
                if g >= 2:
                    pe.wait_ge(biased, 2 * (g - 1))
                for t in range(TT):
                    dst = bank[2 + g % 2][:, KEYS[t]]
                    nk = (t + 1) * P
                    last = nc.tensor.matmul(dst, q[:, t * P:(t + 1) * P], k[:, 0:nk], start=True, stop=more is None)
                    if more is not None:
                        last = nc.tensor.matmul(dst, more[0][:, t * P:(t + 1) * P], more[1][:, 0:nk], start=False, stop=True)
                return last.then_inc(scores_done, 1)

            def turn_probs(g):
                pe.wait_ge(probs_ready, 2 * (g + 1))
                if g >= 2:
                    pe.wait_ge(probs_t_ready, g - 1)
                src = probs[g % 3]
                for i in range(3):
                    last = nc.tensor.transpose(GU[g % 2][:, i * P:(i + 1) * P], src[:, i * P:(i + 1) * P], ident[:])
                last.then_inc(probs_t_done, 1)

            def weigh_values(g, dst, v, start=True, stop=True):
                pe.wait_ge(probs_t_ready, g + 1)
                src = probs_t[g % 2]
                nc.tensor.matmul(dst, v[0], src[:, 0:SEQ], start=start, stop=False, skip_group_check=True)
                return nc.tensor.matmul(dst[:, P:SEQ], v[1], src[:, SEQ:SEQ + P], start=False, stop=stop,
                                        skip_group_check=True).then_inc(heads_done, 1)

            def mix_out(u, i, src):
                w = unit(u)
                for j in range(KD):
                    last = nc.tensor.matmul(acc(j), w[:, j * P:(j + 1) * P], src, start=(i == 0 and j % 2 == 0),
                                            stop=False, skip_group_check=True)
                    if i == KD - 1 and j < KD - 1:
                        last.then_inc(mix_done, 1)
                last.then_inc(unit_used, 1)

            def even_mixer(m):
                u0 = units_before['mix0']
                u = u0
                it = 0
                for what, i in even:
                    if what == 'b_t':
                        pe.wait_ge(tables_ready, 1)
                        for c, dst in enumerate((bank[6], GU[1])):
                            for b in range(UB):
                                last = nc.tensor.transpose(dst[:, b * P:(b + 1) * P],
                                                           b_blocks[:, c, PER * b:PER * (b + 1), :], ident[:])
                            last.then_inc(b_t_done, 1)
                    elif what == 'squares':
                        square_sums(m)
                    elif what == 'spread':
                        spread_rstd(m)
                    elif what in 'uqk':
                        if (what, i) == ('u', 1):
                            pe.wait_ge(b_t_ready, 2)
                        project(u, it, m).then_inc(unit_used, 1)
                        u += 1
                        it += 1
                    elif what == 'f':
                        project(u, it, m, rows=F_ROWS, cols=F_ROWS).then_inc(unit_used, 1)
                        u += 1
                        it += 1
                    elif what == 'v':
                        w = unit(u)
                        for kk in range(2):
                            for t in range(TT):
                                last = nc.tensor.matmul(bank[2 + t][:], xf[:, 2 * i + kk, t * P:(t + 1) * P],
                                                        w[:, kk * 512:(kk + 1) * 512], start=(i + kk == 0),
                                                        stop=(i == 3 and kk == 1))
                        last.then_inc(unit_used, 1)
                        u += 1
                    elif what == 's5':
                        if i < SG:
                            if i == 0:
                                pe.wait_ge(proj_read, UB)
                            if i >= 2:
                                pe.wait_ge(bu_ready, i - 1)
                            r = slice(GC * (i % PER), GC * (i % PER + 1))
                            for c in range(2):
                                last = nc.tensor.matmul((bank[6], bank[0])[i % 2][:, c * SEQ:(c + 1) * SEQ],
                                                        b_t[r, c, i // PER, :], u_t[r, i // PER, :], start=True, stop=True)
                            last.then_inc(bu_done, 1)
                        j = i - 3
                        if j >= 0:
                            pe.wait_ge(state_ready, 2 * (j + 1))
                            if j % PER == 0 and j:
                                pe.wait_ge(y_read, j // PER)
                            r = slice(GC * (j % PER), GC * (j % PER + 1))
                            for c in range(2):
                                last = nc.tensor.matmul(bank[1][r, 0:SEQ], c_d[:, c, j, :], states[j % 2][:, c, :],
                                                        start=(c == 0), stop=(c == 1))
                            last.then_inc(y_done, 1)
                    elif what == 'fox':
                        if i < HEADS:
                            if i == 0:
                                pe.wait_ge(proj_read, UB + 1 + 2 * PAIRS)
                                pe.wait_ge(v_ready, TT)
                                pe.wait_ge(fox_lhs_ready, 1)
                            pe.wait_ge(fox_rhs_ready, i + 1)
                            r = slice(DH * (i % 2), DH * (i % 2 + 1))
                            fr = slice(DH * (i % 2), DH * (i % 2) + 40)
                            scores(i, q_t[r, i // 2, :], k_t[r, i // 2, :], (fox_lhs[fr, :], fox_rhs[fr, i % 2, :]))
                        if 0 <= i - 2 < HEADS:
                            turn_probs(i - 2)
                        g = i - 3
                        if g >= 0:
                            if g % 2 == 0 and g:
                                pe.wait_ge(heads_out, g // 2)
                            if g == 0:
                                pe.wait_ge(rbc_ready, m + 1)
                            weigh_values(g, misc[DH * (g % 2):DH * (g % 2 + 1), 0:SEQ],
                                         [v_n[:, t, g * DH:(g + 1) * DH] for t in range(TT)])
                    elif what == 'out':
                        if i == 0:
                            pe.wait_ge(heads_out, PAIRS)
                            pe.wait_ge(y_read, UB)
                            pe.wait_ge(bu_ready, SG)
                        if i == 4:
                            pe.wait_ge(s5_ready, UB)
                        mix_out(u, i, q_t[:, i, :] if i < 4 else s5_out[:, i - 4, :])
                        u += 1
                    elif what == 'glu':
                        if i % 2 == 0:
                            w = unit(u)
                        pe.wait_ge(gelu_ready, UB)
                        if i >= 2:
                            pe.wait_ge(s5_ready, i - 1)
                        for k in range(UB):
                            last = nc.tensor.matmul(GU[i % 2][:, 0:SEQ], w[:, (i % 2 * UB + k) * P:(i % 2 * UB + k + 1) * P],
                                                    u_t[:, k, :], start=(k == 0), stop=(k == UB - 1))
                        last.then_inc(unit_used if i % 2 else glu_done, 1)
                        u += i % 2
                assert u == u0 + even_units

            def odd_mixer(m):
                u0 = units_before['mix1']
                it = 0

                def next_bank():
                    if it >= 1 and reads0 + it - 1 > 0:
                        pe.wait_ge(proj_read, reads0 + it - 1)
                    return GU[it % 2]

                for what, i in odd:
                    if what == 't5':
                        pe.wait_ge(odd_in, 32)
                        nc.tensor.matmul(bank[6][0:HEADS, :], par[0:BUCKETS + 1, PARAMS['rel']], t5_onehot[0:BUCKETS + 1, :],
                                         start=True, stop=True).then_inc(even_done, 1)
                    elif what == 'squares':
                        square_sums(m)
                    elif what == 'spread':
                        spread_rstd(m)
                    elif what in ('cq', 'ckv', 'nq', 'kv'):
                        next_bank()
                        project(u0 + ODD[what] + i, it, m, fenced=True).then_inc(unit_used, 1)
                        it += 1
                    elif what == 'krg':
                        next_bank()
                        project(u0 + ODD[what], it, m, rows=2 * ROPE, cols=2 * ROPE, at=DH, fenced=True)
                        it += 1
                        w = unit(u0 + ODD[what])[:, KD * 2 * ROPE:]
                        pe.wait_ge(rbc_ready, m + 1)
                        for t in range(TT):
                            for k in range(KD):
                                last = nc.tensor.matmul(misc[:, 8 + 24 * t:32 + 24 * t], xf[:, k, t * P:(t + 1) * P],
                                                        w[:, 24 * k:24 * (k + 1)], start=(k == 0), stop=(k == KD - 1))
                        last.then_inc(unit_used, 1)
                    elif what == 'lat_squares':
                        pe.wait_ge(lat_squared, LB)
                        pe.wait_ge(logits_read, TT)
                        for c, chunks in enumerate((range(QB), range(QB, LB))):
                            for t in range(TT):
                                for k in chunks:
                                    last = nc.tensor.matmul(misc[:, 64 + 2 * c + t:65 + 2 * c + t], sq[:, k, t * P:(t + 1) * P],
                                                            ones[:, 0:1], start=(k == chunks[0]), stop=(k == chunks[-1]))
                        last.then_inc(lat_ss_done, 1)
                    elif what == 'sel':
                        pe.wait_ge(krope_ready, 1)
                        pe.wait_ge(t5_copied, 1)
                        nc.tensor.matmul(bank[6][DH:P, 0:SEQ], oc[DH:P, OC['sel']], kr[DH:P, :], start=True,
                                         stop=True).then_inc(krope_done, 1)
                    elif what == 'lat_spread':
                        pe.wait_ge(lat_diag_ready, 4)
                        pe.wait_ge(krope_copied, 1)
                        for t in range(4):
                            last = nc.tensor.matmul(bank[6][:, t * P:(t + 1) * P], ones[:], lat_diag[:, t, :], start=True, stop=True)
                        last.then_inc(lat_spread_done, 1)
                    elif what == 'vsw':
                        w = unit(u0 + ODD[what] + i)
                        for kk in range(4):
                            k = 4 * i + kk
                            for t in range(TT):
                                last = nc.tensor.matmul(bank[2 + t][:, 0:2 * P], xf[:, k, t * P:(t + 1) * P],
                                                        w[:, kk * 2 * P:(kk + 1) * 2 * P], start=(k == 0), stop=(k == KD - 1))
                        last.then_inc(unit_used, 1)
                    elif what == 'uq':
                        b = next_bank()
                        it += 1
                        if i == 0:
                            pe.wait_ge(lat_ready, LB)
                        w = unit(u0 + ODD[what] + i // 2)
                        for k in range(QB):
                            c = (2 * k + i % 2) * P
                            last = nc.tensor.matmul(b[:, 0:SEQ], w[:, c:c + P], lat[:, k, :], start=(k == 0), stop=(k == QB - 1))
                        last.then_inc(unit_used if i % 2 else many_done, 1)
                    elif what == 'uk':
                        b = next_bank()
                        it += 1
                        w = unit(u0 + ODD[what])
                        for k in range(KVB):
                            c = k * HEADS * DH + i * DH
                            last = nc.tensor.matmul(b[0:DH, 0:SEQ], w[:, c:c + DH], lat[:, QB + k, :], start=(k == 0),
                                                    stop=(k == KVB - 1))
                        last.then_inc(unit_used if i == HEADS - 1 else many_done, 1)
                    elif what == 'uv':
                        w = unit(u0 + ODD[what])
                        pe.wait_ge(v_ready, v0 + TT)
                        for t in range(TT):
                            for k in range(KVB):
                                last = nc.tensor.matmul(bank[2 + t][:], lat[:, QB + k, t * P:(t + 1) * P],
                                                        w[:, k * 512:(k + 1) * 512], start=(k == 0), stop=(k == KVB - 1))
                        last.then_inc(unit_used, 1)
                    elif what == 'w1':
                        w = unit(u0 + ODD[what] + i)
                        pe.wait_ge(blocks_ready, 2)
                        c = i // 2
                        for k in range(CMP_PAIRS // 2):
                            kk = i % 2 * (CMP_PAIRS // 2) + k
                            last = nc.tensor.matmul(small_ps[:, 128 + 32 * c:128 + 32 * c + 2 * N_CMP], w[:, k * P:(k + 1) * P],
                                                    blk[:, c, kk].rearrange('p g n -> p (g n)'), start=(kk == 0),
                                                    stop=(kk == CMP_PAIRS - 1))
                        last.then_inc(unit_used, 1)
                    elif what == 'compress':
                        pe.wait_ge(hid_v_ready, 1)
                        w2 = par[:, PARAMS['w2']]
                        for g in range(GROUPS):
                            nc.tensor.matmul(small_ps[DH * g:DH * (g + 1), 192:192 + N_CMP], w2[:, 0:DH],
                                             hid[:, 0, g * N_CMP:(g + 1) * N_CMP], start=True, stop=True)
                        nc.tensor.matmul(small_ps[:, 256:256 + DH], hid_v, w2[:, DH:2 * DH], start=True, stop=True).then_inc(cmp_made, 1)
                    elif what == 'cmp_scores':
                        pe.wait_ge(kc_ready, 1)
                        for g in range(GROUPS):
                            rows = slice(DH * g, DH * (g + 1))
                            for t in range(TT):
                                for r in range(REP):
                                    c = (t * REP + r) * 16
                                    last = nc.tensor.matmul((bank[6], bank[0])[g][:, c:c + N_CMP], nq[rows, r, t * P:(t + 1) * P],
                                                            kc[rows, :], start=True, stop=True)
                        last.then_inc(cmp_scored, 1)
                    elif what == 'cmp_turn':
                        pe.wait_ge(cmp_ready, 1)
                        pe.wait_ge(v_block_ready, 1)
                        for t in range(TT):
                            last = nc.tensor.transpose(bank[1][:, t * P:(t + 1) * P], pc[:, t].rearrange('p h n -> p (h n)'), ident[:])
                        last.then_inc(cmp_turned, 1)
                    elif what == 'att':
                        if i < HEADS:
                            if i == 0:
                                pe.wait_ge(proj_read, reads0 + it)
                                pe.wait_ge(mla_v_ready, TT)
                            scores(heads0 + i, mq[:, i, :], mk[:, i, :])
                        elif i < odd_heads:
                            r, g, w = nsa(i - HEADS)
                            rows = slice(DH * g, DH * (g + 1))
                            scores(heads0 + i, nq[rows, r, :], ksw[rows, w, :])
                        if 0 <= i - 2 < odd_heads:
                            turn_probs(heads0 + i - 2)
                        j = i - 3
                        if 0 <= j < HEADS:
                            if j % 2 == 0 and j + out0:
                                pe.wait_ge(heads_out, out0 + j // 2)
                            weigh_values(heads0 + j, o_bank[DH * (j % 2):DH * (j % 2 + 1), 0:SEQ],
                                         [mv[:, t, j * DH:(j + 1) * DH] for t in range(TT)])
                        elif j >= 0:
                            r, g, w = nsa(j - HEADS)
                            if g + w == 0:
                                pe.wait_ge(heads_out, out0 + PAIRS + r)
                            dst = o_bank[DH * g:DH * (g + 1), 0:SEQ]
                            weigh_values(heads0 + j, dst, [vsw[:, t, (2 * w + g) * DH:(2 * w + g + 1) * DH] for t in range(TT)],
                                         start=(w == 0), stop=False)
                            if w:
                                pe.wait_ge(pc_t_ready, 1)
                                nc.tensor.matmul(dst, v_block[:, g * REP + r, :], pc_t, start=False, stop=True,
                                                 skip_group_check=True).then_inc(cmp_weighed, 1)
                    elif what == 'out':
                        if i == 0:
                            pe.wait_ge(heads_out, out0 + 2 * PAIRS)
                        mix_out(u0 + ODD[what] + i, i, mq[:, i, :] if i < PAIRS else nq[:, i - PAIRS, :])

            pe.wait_ge(consts_set, 3)
            pe.wait_ge(ident_loaded, 16)
            n = 0
            for p in phases:
                if p.startswith('ffn'):
                    ffn(n)
                    n += 1
                elif p == 'mix0':
                    even_mixer(NORM[p])
                elif p == 'mix1':
                    odd_mixer(NORM[p])
                elif p == 'final':
                    final()

        @block.scalar
        def _(act):
            def split_gu(c, s, c_half, half):
                act.wait_ge(raw_gu_in[s], 16 * c_half + 16)
                if not (isinstance(c, int) and c < 2):
                    act.wait_ge(gateup_done, c - 1)
                w = slice(half * D, (half + 1) * D)
                nc.scalar.copy(hi_gu[:, s, w], raw_gu[:, s, w]).then_inc(gu_hi, 1)

            def split_d(c, s, c_half):
                act.wait_ge(raw_d_in[s], 16 * c_half + 16)
                if not (isinstance(c, int) and c < 2):
                    act.wait_ge(down_done, KD * (c - 1))
                nc.scalar.copy(hi_d[:, s, :], raw_d[:, s, :]).then_inc(d_hi, 1)

            def step(c, s, c_half, more_gu=True, more_d=True):
                act.wait_ge(gate_scaled, c + 1)
                nc.scalar.activation(th[:, s, :], gs[:, s, 0, :], ACT.Tanh, scale=0.5).then_inc(tanh_done, 1)
                act.wait_ge(prod_ready, c + 1)
                nc.scalar.copy(ph[:, s, :], prod[:, s, :]).then_inc(ph_ready, 1)
                if more_gu:
                    split_gu(c + 2, s, c_half + 1, 0)
                if more_d:
                    split_d(c + 1, 1 - s, c_half + s)
                if more_gu:
                    split_gu(c + 2, s, c_half + 1, 1)

            def h_wait(m, k):
                if m == 0:
                    act.wait_ge(x_in[2 * k // KD], 16)
                else:
                    act.wait_ge(h_ready, KD * m + k + 1 - KD)

            def norm_inputs(p):
                m = NORM[p]
                for k in range(KD):
                    h_wait(m, k)
                    g = gain[:, m, k:k + 1]
                    if p.startswith('ffn'):
                        nc.scalar.activation(xh[:, k, :], h[:, k, :], ACT.Copy, scale=g).then_inc(x_hi, 1)
                    else:
                        nc.scalar.activation(xf[:, k, :], h[:, k, :], ACT.Copy, scale=g).then_inc(xf_ready, 1)

            def exp_scores(g):
                for t in range(TT):
                    act.wait_ge(neg_max, g + 1)
                    nc.scalar.activation(probs[g % 3][:, KEYS[t]], probs[g % 3][:, KEYS[t]], ACT.Exp,
                                         bias=stats[:, g % 3, 0, t:t + 1], accum_out=stats[:, g % 3, 1, t:t + 1]).then_inc(exp_done, 1)

            def copy_probs_t(g):
                act.wait_ge(probs_t_done, g + 1)
                if g >= 2:
                    act.wait_ge(heads_done, g - 1)
                nc.scalar.copy(probs_t[g % 2], GU[g % 2][:, 0:ATT_COLS]).then_inc(probs_t_ready, 1)

            def even_mixer(m):
                u0 = units_before['mix0']
                for what, i in even:
                    if what == 'b_t':
                        for c, src in enumerate((bank[6], GU[1])):
                            act.wait_ge(b_t_done, c + 1)
                            nc.scalar.copy(b_t[:, c, :, :], src[:].rearrange('p (b n) -> p b n', b=UB)).then_inc(b_t_ready, 1)
                    elif what == 'f':
                        act.wait_ge(f_neg, 1)
                        nc.scalar.activation(fox_rhs[0:F_ROWS, 1, :], fox_rhs[0:F_ROWS, 0, :], ACT.Exp).then_inc(f_exp, 1)
                        act.wait_ge(f_exp, 1)
                        nc.scalar.activation(fox_rhs[0:F_ROWS, 0, :], fox_rhs[0:F_ROWS, 1, :], ACT.Ln, bias=1.0).then_inc(f_ln, 1)
                    elif what == 'v' and i == 3:
                        act.wait_ge(unit_used, u0 + EVEN['v'] + 4)
                        act.wait_ge(rstd_ready, m + 1)
                        for t in range(TT):
                            nc.scalar.activation(v_n[:, t, :], bank[2 + t][:], ACT.Copy, scale=rstd[:, t:t + 1]).then_inc(v_ready, 1)
                    elif what == 's5' and i < SG:
                        act.wait_ge(bu_done, i + 1)
                        if i >= 2:
                            act.wait_ge(cos_out_ready, i - 1)
                            act.wait_ge(sin_out_ready, i - 1)
                        nc.scalar.copy(bu[i % 2], (bank[6], bank[0])[i % 2][:].rearrange('p (c t) -> p c t', c=2)).then_inc(bu_ready, 1)
                    elif what == 'fox':
                        if i < HEADS:
                            exp_scores(i)
                        if 0 <= i - 2 < HEADS:
                            copy_probs_t(i - 2)
                        if i - 3 >= 0 and (i - 3) % 2:
                            act.wait_ge(heads_done, i - 2)
                            nc.scalar.copy(q_t[:, (i - 3) // 2, :], misc[:, 0:SEQ]).then_inc(heads_out, 1)
                    elif what == 'gelu':
                        act.wait_ge(y_inner, i + 1)
                        nc.scalar.activation(states_tanh[:, i, :], states_tanh[:, i, :], ACT.Tanh, scale=0.7978845608028654).then_inc(gelu_tanh, 1)
                    elif what == 'glu':
                        if i % 2:
                            act.wait_ge(unit_used, u0 + EVEN['glu'] + i // 2 + 1)
                        else:
                            act.wait_ge(glu_done, i // 2 + 1)
                        nc.scalar.activation(k_t[:, i, :], GU[i % 2][:, 0:SEQ], ACT.Tanh, scale=0.25,
                                             bias=half_b[:, i:i + 1]).then_inc(glu_tanh, 1)

            def odd_mixer(m):
                u0 = units_before['mix1']
                for what, i in odd:
                    if what == 't5':
                        act.wait_ge(even_done, 1)
                        nc.scalar.mul(t5_row[0:HEADS, :], bank[6][0:HEADS, :], 8.0).then_inc(t5_copied, 1)
                    elif what == 'krg':
                        act.wait_ge(logits_read, TT)
                        nc.scalar.activation(gates, logits, ACT.Tanh, scale=0.5).then_inc(gate_tanh, 1)
                    elif what == 'sel':
                        act.wait_ge(krope_done, 1)
                        nc.scalar.copy(mk[DH:P, :, :], bank[6][DH:P, 0:SEQ].unsqueeze(1).broadcast_to([DH, HEADS, SEQ])
                                       ).then_inc(krope_copied, 1)
                    elif what == 'vsw' and i == 1:
                        act.wait_ge(unit_used, u0 + ODD['vsw'] + 2)
                        act.wait_ge(rstd_ready, m + 1)
                        for t in range(TT):
                            nc.scalar.activation(vsw[:, t, :], bank[2 + t][:, 0:2 * P], ACT.Copy, scale=rstd[:, t:t + 1]).then_inc(v_ready, 1)
                    elif what == 'uv':
                        act.wait_ge(unit_used, u0 + ODD['uv'] + 1)
                        act.wait_ge(t5_stored, 16)
                        for t in range(TT):
                            nc.scalar.copy(mv[:, t, :], bank[2 + t][:]).then_inc(mla_v_ready, 1)
                    elif what == 'hidden':
                        act.wait_ge(hid_inner, 1)
                        nc.scalar.activation(hid_t, hid_t, ACT.Tanh, scale=0.7978845608028654).then_inc(hid_tanh, 1)
                    elif what == 'cmp_softmax':
                        act.wait_ge(cmp_step, 5)
                        flat = pc.rearrange('p t h n -> p (t h n)')
                        nc.scalar.activation(flat, flat, ACT.Exp, scale=DH ** -0.5).then_inc(cmp_exp, 1)
                    elif what == 'cmp_turn':
                        act.wait_ge(cmp_turned, 1)
                        nc.scalar.copy(pc_t, bank[1][:, 0:SEQ]).then_inc(pc_t_ready, 1)
                    elif what == 'att':
                        if i < odd_heads:
                            exp_scores(heads0 + i)
                        if 0 <= i - 2 < odd_heads:
                            copy_probs_t(heads0 + i - 2)
                        j = i - 3
                        if 0 <= j < HEADS and j % 2:
                            act.wait_ge(heads_done, heads0 + j + 1)
                            nc.scalar.copy(mq[:, j // 2, :], o_bank[:, 0:SEQ]).then_inc(heads_out, 1)
                        elif j >= HEADS and nsa(j - HEADS)[1:] == (1, 1):
                            r = nsa(j - HEADS)[0]
                            act.wait_ge(cmp_weighed, 2 * (r + 1))
                            nc.scalar.copy(nq[:, r, :], o_bank[:, 0:SEQ]).then_inc(heads_out, 1)

            act.wait_ge(params_in, 16)
            n = 0
            for p in phases:
                norm_inputs(p)
                if p == 'mix0':
                    even_mixer(NORM[p])
                if p == 'mix1':
                    odd_mixer(NORM[p])
                if p.startswith('ffn'):
                    if n == 0:
                        act.wait_ge(first_gate_in, 16)
                        nc.scalar.copy(hi_gu[:, 0, 0:D], raw_gu[:, 0, 0:D]).then_inc(gu_hi, 1)
                        split_gu(0, 0, 0, 1)
                        split_gu(1, 1, 0, 0)
                        split_gu(1, 1, 0, 1)
                        split_d(0, 0, 0)
                    pairs(act, step, n)
                    n += 1
                if p == 'final':
                    act.wait_ge(rstd_ready, NORM[p] + 1)
                    for i in range(2):
                        act.wait_ge(final_t, i + 1)
                        nc.scalar.activation(o_sb[:, 1, i * 512:(i + 1) * 512], final_bank[i][1][:], ACT.Copy,
                                             scale=rstd[:, 1:2]).then_inc(scaled_act, 1)

        @block.vector
        def _(dve):
            def x_rest(n, k):
                dve.wait_ge(x_hi, KD * n + k + 1)
                m = NORM[f'ffn{n}']
                nc.vector.scalar_tensor_tensor(xl[:, k, :], h[:, k, :], gain[:, m, k:k + 1], xh[:, k, :].bitcast(F32), ALU.mult,
                                               ALU.subtract).then_inc(x_lo, 1)

            def rms(m):
                dve.wait_ge(ss_done, m + 1)
                nc.vector.tensor_scalar(ms[:], misc[:, 0:TT], 1.0 / D, EPS, ALU.mult, ALU.add).then_inc(ms_ready, 1)
                dve.wait_ge(rstd_ready, m + 1)
                for t in range(TT):
                    nc.vector.tensor_scalar(diag[:, t, :], ident[:], rstd[:, t:t + 1], None,
                                            ALU.mult).then_inc(diag_ready, 1)
                dve.wait_ge(rbc_done, m + 1)
                nc.vector.tensor_copy(rbc[:], misc[:, SEQ:2 * SEQ]).then_inc(rbc_ready, 1)
                dve.wait_ge(rbc_ready, m + 1)

            def split_gu(c, s, half):
                dve.wait_ge(gu_hi, 2 * c + half + 1)
                w = slice(half * D, (half + 1) * D)
                nc.vector.tensor_tensor(lo_gu[:, s, w], raw_gu[:, s, w], hi_gu[:, s, w].bitcast(F32),
                                        ALU.subtract).then_inc(gu_lo, 1)

            def split_d(c, s):
                dve.wait_ge(d_hi, c + 1)
                nc.vector.tensor_tensor(lo_d[:, s, :], raw_d[:, s, :], hi_d[:, s, :].bitcast(F32),
                                        ALU.subtract).then_inc(d_lo, 1)

            def step(c, s, c_half, more_gu=True, more_d=True):
                dve.wait_ge(gateup_done, c + 1)
                nc.vector.tensor_tensor(gs[:, s, :, :], GU[s][:].rearrange('p (a t) -> p a t', a=2),
                                        rbc[:].unsqueeze(1).broadcast_to([P, 2, SEQ]), ALU.mult).then_inc(gate_scaled, 1)
                dve.wait_ge(tanh_done, c + 1)
                nc.vector.scalar_tensor_tensor(ga[:, s, :], th[:, s, :], 1.0, gs[:, s, 0, :], ALU.add,
                                               ALU.mult).then_inc(a_ready, 1)
                dve.wait_ge(a_ready, c + 1)
                nc.vector.tensor_tensor(prod[:, s, :], ga[:, s, :], gs[:, s, 1, :], ALU.mult).then_inc(prod_ready, 1)
                dve.wait_ge(ph_ready, c + 1)
                nc.vector.tensor_tensor(pl[:, s, :], prod[:, s, :], ph[:, s, :].bitcast(F32),
                                        ALU.subtract).then_inc(act_lo, 1)
                if more_gu:
                    split_gu(c + 2, s, 0)
                if more_d:
                    split_d(c + 1, 1 - s)
                if more_gu:
                    split_gu(c + 2, s, 1)

            def stat_rows(g, bias, scale):
                dve.wait_ge(scores_done, g + 1)
                if g >= 3:
                    dve.wait_ge(probs_t_done, g - 2)
                for t in range(TT):
                    nc.vector.tensor_tensor_reduce(probs[g % 3][:, KEYS[t]], bank[2 + g % 2][:, KEYS[t]], bias[t], scale, -3e38,
                                                   ALU.add, ALU.max, stats[:, g % 3, 2, t:t + 1]).then_inc(biased, 1)
                dve.wait_ge(biased, 2 * (g + 1))
                nc.vector.tensor_scalar(stats[:, g % 3, 0, :], stats[:, g % 3, 2, :], -1.0, None, ALU.mult).then_inc(neg_max, 1)

            def normalise(g, gate=None):
                dve.wait_ge(exp_done, 2 * (g + 1))
                nc.vector.reciprocal(stats[:, g % 3, 2, :], stats[:, g % 3, 1, :]).then_inc(factor, 1)
                dve.wait_ge(factor, g + 1)
                if gate is not None:
                    nc.vector.tensor_tensor(stats[:, g % 3, 2, :], stats[:, g % 3, 2, :], gate, ALU.mult).then_inc(gated, 1)
                    dve.wait_ge(gated, g + 1 - heads0 - HEADS)
                for t in range(TT):
                    nc.vector.tensor_scalar(probs[g % 3][:, KEYS[t]], probs[g % 3][:, KEYS[t]], stats[:, g % 3, 2, t:t + 1], None,
                                            ALU.mult).then_inc(probs_ready, 1)

            def even_mixer(m):
                u0 = units_before['mix0']
                it = 0
                for what, i in even:
                    if what == 'spread':
                        rms(m)
                        for b in range(2):
                            dve.wait_ge(unit_used, u0 + b + 1)
                            nc.vector.tensor_tensor(u_t[:, b, :], GU[b % 2][:, 0:SEQ], rbc[:], ALU.mult).then_inc(proj_read, 1)
                        it = 2
                    elif what in 'uqk':
                        if it < 2:
                            continue
                        dve.wait_ge(unit_used, u0 + it + 1)
                        dst = {'u': u_t, 'q': q_t, 'k': k_t}[what][:, i, :]
                        nc.vector.tensor_tensor(dst, GU[it % 2][:, 0:SEQ], rbc[:], ALU.mult).then_inc(proj_read, 1)
                        it += 1
                    elif what == 'f':
                        dve.wait_ge(unit_used, u0 + it + 1)
                        rows = slice(0, F_ROWS)
                        nc.vector.tensor_tensor(fox_lhs[rows, :], GU[it % 2][rows, 0:SEQ], rbc[rows, :], ALU.mult).then_inc(proj_read, 1)
                        it += 1
                        dve.wait_ge(proj_read, it)
                        nc.vector.tensor_scalar(fox_lhs[rows, :], fox_lhs[rows, :], par[rows, PARAMS['b_f']], None, ALU.add).then_inc(f_x, 1)
                        dve.wait_ge(f_x, 1)
                        nc.vector.scalar_tensor_tensor(fox_rhs[rows, 0, :], fox_lhs[rows, :], -1.0, fox_lhs[rows, :], ALU.mult,
                                                       ALU.min).then_inc(f_neg, 1)
                        dve.wait_ge(f_ln, 1)
                        nc.vector.scalar_tensor_tensor(fox_rhs[rows, 1, :], fox_lhs[rows, :], 0.0, fox_rhs[rows, 0, :], ALU.min,
                                                       ALU.subtract).then_inc(f_log, 1)
                        dve.wait_ge(f_log, 1)
                        nc.vector.tensor_tensor_scan(cum[rows, :], ones[rows, 0:1].broadcast_to([F_ROWS, SEQ]), fox_rhs[rows, 1, :],
                                                     0.0, ALU.mult, ALU.add).then_inc(cum_ready, 1)
                    elif what == 's5':
                        cos2 = [cos_t[:, j, :].unsqueeze(1).broadcast_to([P, 2, SEQ]) for j in range(SG)]
                        j = i - 1
                        if 0 <= j < SG:
                            dve.wait_ge(sin_in_ready, j + 1)
                            dve.wait_ge(cos_in_ready, j + 1)
                            nc.vector.tensor_tensor(cos_in[:, 0, :], cos_in[:, 0, :], sin_in[:, 1, :], ALU.add).then_inc(zin_ready, 1)
                            nc.vector.tensor_tensor(cos_in[:, 1, :], cos_in[:, 1, :], sin_in[:, 0, :], ALU.subtract).then_inc(zin_ready, 1)
                            mag = small[:, MAG, j:j + 1].broadcast_to([P, SEQ])
                            for c in range(2):
                                dve.wait_ge(zin_ready, 2 * j + c + 1)
                                nc.vector.tensor_tensor_scan(bu[j % 2][:, c, :], mag, cos_in[:, c, :], 0.0, ALU.mult,
                                                             ALU.add).then_inc(scanned, 1)
                        e = i - 2
                        if 0 <= e < SG:
                            dve.wait_ge(sin_out_ready, e + 1)
                            dve.wait_ge(cos_out_ready, e + 1)
                            nc.vector.tensor_tensor(states[e % 2][:, 0, :], states[e % 2][:, 0, :], sin_out[:, 1, :],
                                                    ALU.subtract).then_inc(state_ready, 1)
                            nc.vector.tensor_tensor(states[e % 2][:, 1, :], states[e % 2][:, 1, :], sin_out[:, 0, :],
                                                    ALU.add).then_inc(state_ready, 1)
                        if i < SG:
                            dve.wait_ge(bu_ready, i + 1)
                            if i >= 1:
                                dve.wait_ge(scanned, 2 * i)
                            nc.vector.tensor_tensor(cos_in, bu[i % 2], cos2[i], ALU.mult).then_inc(cos_in_ready, 1)
                        if 0 <= j < SG:
                            if j >= 2:
                                dve.wait_ge(y_done, j - 1)
                            dve.wait_ge(scanned, 2 * (j + 1))
                            nc.vector.tensor_tensor(states[j % 2], bu[j % 2], cos2[j], ALU.mult).then_inc(cos_out_ready, 1)
                    elif what == 'gelu':
                        dve.wait_ge(y_done, PER * (i + 1))
                        nc.vector.scalar_tensor_tensor(u_t[:, i, :], u_t[:, i, :], par[:, PARAMS['d_skip']][:, i:i + 1],
                                                       bank[1][:, 0:SEQ], ALU.mult, ALU.add).then_inc(y_read, 1)
                        if i >= 1:
                            gelu_end(i - 1)
                        if i == UB - 1:
                            gelu_end(i)
                    elif what == 'fox':
                        if i < HEADS:
                            stat_rows(i, [causal[:, KEYS[t]] for t in range(TT)], DH ** -0.5)
                        if 0 <= i - 1 < HEADS:
                            normalise(i - 1)
                    elif what == 'glu':
                        dve.wait_ge(glu_tanh, i + 1)
                        dve.wait_ge(quarter_ready, UB)
                        nc.vector.scalar_tensor_tensor(s5_out[:, i, :], k_t[:, i, :], 1.0, quarter[:, i, :], ALU.add,
                                                       ALU.mult).then_inc(s5_ready, 1)

            def odd_mixer(m):
                u0 = units_before['mix1']
                it = 0

                def scaled(dst, n, rows=slice(0, P), by=None):
                    dve.wait_ge(unit_used, n)
                    return nc.vector.tensor_tensor(dst, GU[it % 2][rows, 0:SEQ], (rbc if by is None else by)[rows, :],
                                                   ALU.mult).then_inc(proj_read, 1)

                for what, i in odd:
                    n = u0 + ODD.get(what, 0) + i + 1
                    if what == 'spread':
                        rms(m)
                        for j in range(2):
                            scaled(lat[:, j, :], u0 + j + 1)
                            it += 1
                    elif what == 'cq' and i < 2:
                        continue
                    elif what in ('cq', 'ckv'):
                        scaled(lat[:, i + (QB if what == 'ckv' else 0), :], n)
                        it += 1
                    elif what == 'nq':
                        scaled(nq[:, i, :], n)
                        it += 1
                    elif what == 'kv':
                        scaled(kv_raw[:, i, :] if i < 2 else ksw[:, i - 2, :], n)
                        it += 1
                    elif what == 'krg':
                        rows = slice(DH, P)
                        scaled(kr[rows, :], n, rows)
                        it += 1
                        dve.wait_ge(proj_read, reads0 + it)
                        nc.vector.tensor_tensor(kr[rows, :], kr[rows, :], rope[rows, :], ALU.mult).then_inc(krope_ready, 1)
                        for t in range(TT):
                            nc.vector.scalar_tensor_tensor(logits[:, t, :], misc[:, 8 + 24 * t:32 + 24 * t], rstd[:, t:t + 1],
                                                           par[:, PARAMS['b_gate']], ALU.mult, ALU.add).then_inc(logits_read, 1)
                        dve.wait_ge(gate_tanh, 1)
                        nc.vector.tensor_scalar(gates, gates, 0.5, 0.5, ALU.mult, ALU.add).then_inc(gates_ready, 1)
                    elif what == 'lat_squares':
                        dve.wait_ge(lat_ss_done, 1)
                        nc.vector.tensor_scalar(lat_ms[:, 0:2], misc[:, 64:66], 1.0 / Q_RANK, EPS, ALU.mult, ALU.add).then_inc(lat_ms_ready, 1)
                        nc.vector.tensor_scalar(lat_ms[:, 2:4], misc[:, 66:68], 1.0 / KV_RANK, EPS, ALU.mult, ALU.add).then_inc(lat_ms_ready, 1)
                        dve.wait_ge(lat_rstd_ready, 1)
                        for t in range(4):
                            nc.vector.tensor_scalar(lat_diag[:, t, :], ident[:], lat_rstd[:, t:t + 1], None,
                                                    ALU.mult).then_inc(lat_diag_ready, 1)
                    elif what == 'lat_spread':
                        dve.wait_ge(lat_spread_done, 1)
                        for k in range(LB):
                            c = 0 if k < QB else 1
                            g_ = par[:, PARAMS['q_norm']][:, k:k + 1] if k < QB else par[:, PARAMS['kv_norm']][:, k - QB:k - QB + 1]
                            nc.vector.scalar_tensor_tensor(lat[:, k, :], lat[:, k, :], g_, bank[6][:, c * SEQ:(c + 1) * SEQ], ALU.mult,
                                                           ALU.mult).then_inc(lat_ready, 1)
                    elif what == 'uq':
                        dve.wait_ge(*((unit_used, u0 + ODD['uq'] + i // 2 + 1) if i % 2 else (many_done, i // 2 + 1)))
                        nc.vector.tensor_tensor(mq[:, i, :], GU[it % 2][:, 0:SEQ], rope, ALU.mult).then_inc(proj_read, 1)
                        it += 1
                    elif what == 'uk':
                        dve.wait_ge(*((unit_used, u0 + ODD['uk'] + 1) if i == HEADS - 1 else (many_done, HEADS // 2 + i + 1)))
                        nc.vector.tensor_copy(mk[0:DH, i, :], GU[it % 2][0:DH, 0:SEQ]).then_inc(proj_read, 1)
                        it += 1
                        if i == 0:
                            dve.wait_ge(windows_in, 64)
                            for c in range(2):
                                shape = [P, CMP_PAIRS, N_CMP]
                                for g in range(GROUPS):
                                    w_ap = win[:, c, g, :]
                                    src = bass.AP(w_ap.tensor, w_ap.offset, [w_ap.ap[0], (2, CMP_PAIRS), (CMP_STRIDE, N_CMP)])
                                    pe_ = par[:, PARAMS['pe']][:, c * CMP_PAIRS:(c + 1) * CMP_PAIRS].unsqueeze(2).broadcast_to(shape)
                                    ins = nc.vector.tensor_tensor(blk[:, c, :, g, :], src, pe_, ALU.add)
                                ins.then_inc(blocks_ready, 1)
                    elif what == 'hidden':
                        dve.wait_ge(unit_used, u0 + ODD['w1'] + 4)
                        nc.vector.tensor_copy(hid, small_ps[:, 128:192].rearrange('p (a n) -> p a n', a=2)[:, :, 0:2 * N_CMP]
                                              ).then_inc(hid_read, 1)
                    elif what == 'compress':
                        dve.wait_ge(hid_tanh, 1)
                        nc.vector.scalar_tensor_tensor(hid, hid_t, 1.0, hid, ALU.add, ALU.mult).then_inc(hid_ready, 1)
                        nc.vector.memset(hid_v, 0.0).then_inc(hid_ready, 1)
                        dve.wait_ge(hid_ready, 2)
                        nc.vector.tensor_copy(hid_v.rearrange('p (g r n) -> p g r n', g=GROUPS, r=REP)[:, :, :, 0:N_CMP],
                                              hid[:, 1, :].rearrange('p (g n) -> p g n', g=GROUPS).unsqueeze(2).broadcast_to(
                                                  [P, GROUPS, REP, N_CMP])).then_inc(hid_v_ready, 1)
                        dve.wait_ge(cmp_made, 1)
                        nc.vector.tensor_scalar(kc, small_ps[:, 192:192 + N_CMP], 0.5, None, ALU.mult).then_inc(kc_ready, 1)
                        nc.vector.tensor_tensor(v_block, small_ps[:, 256:256 + DH].unsqueeze(1).broadcast_to([P, HEADS, DH]),
                                                oc[:, OC['block']].unsqueeze(2).broadcast_to([P, HEADS, DH]), ALU.mult
                                                ).then_inc(v_block_ready, 1)
                    elif what == 'cmp_softmax':
                        dve.wait_ge(cmp_scored, 1)
                        dve.wait_ge(t5_in, 16)
                        nc.vector.memset(s5z[:, 512:768], 0.0).then_inc(cmp_step, 1)
                        dve.wait_ge(cmp_step, 1)
                        for g in range(GROUPS):
                            sc = (bank[6], bank[0])[g][:, 0:P].rearrange('p (t r n) -> p t r n', t=TT, r=REP)
                            for t in range(TT):
                                first = CMP_LEN - 1 + (P if t == 0 else 0)
                                bias = t5[:, g * REP:(g + 1) * REP, first:first + CMP_STRIDE * (N_CMP - 1) + 1:CMP_STRIDE]
                                last = nc.vector.tensor_tensor(pc[:, t, g * REP:(g + 1) * REP, 0:N_CMP], sc[:, t, :, 0:N_CMP],
                                                               bias, ALU.add)
                            last.then_inc(cmp_step, 1)
                        dve.wait_ge(cmp_step, 3)
                        th_ = pc.rearrange('p t h n -> p (t h) n')[:, :, 0:N_CMP]
                        flat_max, flat_sum = c_max.rearrange('p t h -> p (t h)'), c_sum.rearrange('p t h -> p (t h)')
                        wide = [P, TT * HEADS, N_CMP]
                        nc.vector.tensor_reduce(flat_max, th_, AX.X, ALU.max).then_inc(cmp_step, 1)
                        dve.wait_ge(cmp_step, 4)
                        nc.vector.tensor_tensor(th_, th_, flat_max.unsqueeze(2).broadcast_to(wide), ALU.subtract).then_inc(cmp_step, 1)
                        dve.wait_ge(cmp_exp, 1)
                        mask = oc[:, OC['mask']].rearrange('p (t n) -> p t n', t=TT)[:, :, 0:N_CMP]
                        for t in range(TT):
                            nc.vector.tensor_tensor(pc[:, t, :, 0:N_CMP], pc[:, t, :, 0:N_CMP],
                                                    mask[:, t, :].unsqueeze(1).broadcast_to([P, HEADS, N_CMP]), ALU.mult).then_inc(cmp_step, 1)
                        dve.wait_ge(cmp_step, 7)
                        nc.vector.tensor_reduce(flat_sum, th_, AX.X, ALU.add).then_inc(cmp_step, 1)
                        dve.wait_ge(cmp_step, 8)
                        nc.vector.tensor_scalar(flat_sum, flat_sum, 1e-30, None, ALU.max).then_inc(cmp_step, 1)
                        dve.wait_ge(cmp_step, 9)
                        nc.vector.reciprocal(flat_max, flat_sum).then_inc(cmp_step, 1)
                        dve.wait_ge(cmp_step, 10)
                        nc.vector.tensor_tensor(c_sum, c_max, gates[:, :, 0::3], ALU.mult).then_inc(cmp_step, 1)
                        dve.wait_ge(cmp_step, 11)
                        nc.vector.tensor_tensor(th_, th_, flat_sum.unsqueeze(2).broadcast_to(wide), ALU.mult).then_inc(cmp_ready, 1)
                    elif what == 'att':
                        if i < odd_heads:
                            if i < HEADS:
                                stat_rows(heads0 + i, [causal[:, KEYS[t]] for t in range(TT)], (DH + ROPE) ** -0.5)
                            else:
                                r, g, w = nsa(i - HEADS)
                                dve.wait_ge(t5_in, 16)
                                stat_rows(heads0 + i, [t5[:, g * REP + r, P:2 * P], t5[:, g * REP + r, 0:SEQ]], DH ** -0.5)
                        j = i - 1
                        if 0 <= j < HEADS:
                            normalise(heads0 + j)
                        elif HEADS <= j < odd_heads:
                            r, g, w = nsa(j - HEADS)
                            normalise(heads0 + j, gates[:, :, 3 * (g * REP + r) + 1 + w])

            def gelu_end(b):
                dve.wait_ge(gelu_tanh, b + 1)
                nc.vector.scalar_tensor_tensor(u_t[:, b, :], states_tanh[:, b, :], 1.0, u_t[:, b, :], ALU.add,
                                               ALU.mult).then_inc(gelu_ready, 1)

            def residual(p, k):
                if p.startswith('ffn'):
                    n = int(p[3])
                    dve.wait_ge(down_done, KD * (CH * (n + 1) - 1) + (k | 1) + 1)
                    nc.vector.scalar_tensor_tensor(h[:, k, :], acc(k), 0.25, h[:, k, :], ALU.mult, ALU.add).then_inc(h_ready, 1)
                    return
                if k < KD - 2:
                    dve.wait_ge(mix_done, (mixes0 if p == 'mix1' else 0) + (k | 1) + 1)
                else:
                    dve.wait_ge(unit_used, units_before[p] + units_of[p])
                nc.vector.tensor_tensor(h[:, k, :], acc(k), h[:, k, :], ALU.add).then_inc(h_ready, 1)

            nc.vector.memset(ones[:], 1.0).then_inc(consts_set, 1)
            nc.vector.memset(halves[:], -0.5).then_inc(consts_set, 1)
            nc.vector.memset(minus_one[:], -1.0).then_inc(consts_set, 1)
            dve.wait_ge(params_in, 16)
            n = 0
            for m, p in enumerate(phases):
                for k in range(KD + 1):
                    if m and k < KD:
                        residual(phases[m - 1], k)
                    if p.startswith('ffn') and k:
                        x_rest(n, k - 1)
                if p.startswith('ffn'):
                    if n == 0:
                        for c in range(2):
                            for half in range(2):
                                split_gu(c, c, half)
                        split_d(0, 0)
                        dve.wait_ge(ident_loaded, 16)
                    rms(m)
                    pairs(dve, step, n)
                    n += 1
                elif p == 'mix0':
                    dve.wait_ge(tables_in, 32)
                    even_mixer(m)
                elif p == 'mix1':
                    odd_mixer(m)
                elif p == 'final':
                    dve.wait_ge(ss_done, m + 1)
                    nc.vector.tensor_scalar(ms[:], misc[:, 0:TT], 1.0 / D, EPS, ALU.mult, ALU.add).then_inc(ms_ready, 1)
                    dve.wait_ge(rstd_ready, m + 1)
                    for i in range(2):
                        dve.wait_ge(final_t, i + 1)
                        nc.vector.tensor_scalar(o_sb[:, 0, i * 512:(i + 1) * 512], final_bank[i][0][:], rstd[:, 0:1],
                                                None, ALU.mult).then_inc(scaled_dve, 1)

        @block.gpsimd
        def _(pool):
            def squares(m):
                for k in range(KD):
                    if m == 0:
                        pool.wait_ge(x_in[2 * k // KD], 16)
                    else:
                        pool.wait_ge(h_ready, KD * m + k + 1 - KD)
                    nc.gpsimd.tensor_tensor(sq[:, k, :], h[:, k, :], h[:, k, :], ALU.mult).then_inc(sq_ready, 1)
                pool.wait_ge(ms_ready, m + 1)
                nc.gpsimd.tensor_tensor(rstd[:], ms[:], halves[:, 0:TT], ALU.pow).then_inc(rstd_ready, 1)

            steps = [0]

            def link(ins):
                steps[0] += 1
                ins.then_inc(s5_prep, 1)
                pool.wait_ge(s5_prep, steps[0])

            def tt(dst, a, b, op):
                link(nc.gpsimd.tensor_tensor(dst, a, b, op))

            def ts(dst, a, s1, op1, s2=None, op2=None):
                if op2 is None:
                    link(nc.gpsimd.tensor_scalar(dst, a, s1, None, op1))
                else:
                    link(nc.gpsimd.tensor_scalar(dst, a, s1, s2, op1, op2))

            S = [small[:, i, :] for i in range(13)]

            def series(dst, x, coeffs):
                ts(dst, x, coeffs[0], ALU.mult, coeffs[1], ALU.add)
                for c in coeffs[2:]:
                    tt(dst, dst, x, ALU.mult)
                    ts(dst, dst, c, ALU.add)

            def exponential(dst, x, k, r):
                ts(k, x, 1 / math.log(2), ALU.mult)
                ts(k, k, 126.0, ALU.min, -126.0, ALU.max)
                ts(k, k, MAGIC, ALU.add)
                ts(k, k, MAGIC, ALU.subtract)
                ts(r, k, LN2[0], ALU.mult)
                tt(r, x, r, ALU.subtract)
                ts(dst, k, LN2[1], ALU.mult)
                tt(r, r, dst, ALU.subtract)
                series(dst, r, [1 / 5040, 1 / 720, 1 / 120, 1 / 24, 1 / 6, 0.5, 1.0, 1.0])
                ts(k, k, 127.0, ALU.add, 8388608.0, ALU.mult)
                link(nc.gpsimd.tensor_copy(r.bitcast(mybir.dt.int32), k))
                tt(dst, dst, r, ALU.mult)

            def sine_cosine(sn, cs, x, k, sq_):
                ts(k, x, 1 / (2 * math.pi), ALU.mult)
                ts(k, k, MAGIC, ALU.add)
                ts(k, k, MAGIC, ALU.subtract)
                for part in TWO_PI:
                    ts(sn, k, part, ALU.mult)
                    tt(x, x, sn, ALU.subtract)
                ts(x, x, 0.25, ALU.mult)
                tt(sq_, x, x, ALU.mult)
                series(sn, sq_, [1 / 362880, -1 / 5040, 1 / 120, -1 / 6, 1.0])
                tt(sn, sn, x, ALU.mult)
                series(cs, sq_, [-1 / 3628800, 1 / 40320, -1 / 720, 1 / 24, -0.5, 1.0])
                for _ in range(2):
                    tt(cs, cs, sn, ALU.mult)
                    tt(sq_, sn, sn, ALU.mult)
                    ts(sn, cs, 2.0, ALU.mult)
                    ts(cs, sq_, -2.0, ALU.mult, 1.0, ALU.add)

            def s5_tables():
                lr, li = par[:, PARAMS['lam_re']], par[:, PARAMS['lam_im']]
                dt, mag, th_, sn, cs, k, r, q, ar, ai, fr, fi, den = [S[i] for i in range(13)]
                exponential(dt, par[:, PARAMS['log_dt']], k, r)
                tt(th_, lr, dt, ALU.mult)
                exponential(mag, th_, k, r)
                tt(th_, li, dt, ALU.mult)
                sine_cosine(sn, cs, th_, k, q)
                tt(ar, mag, cs, ALU.mult)
                ts(ar, ar, -1.0, ALU.add)
                tt(ai, mag, sn, ALU.mult)
                tt(den, lr, lr, ALU.mult)
                tt(q, li, li, ALU.mult)
                tt(den, den, q, ALU.add)
                tt(den, den, minus_one[:, 0:SG], ALU.pow)
                tt(fr, ar, lr, ALU.mult)
                tt(q, ai, li, ALU.mult)
                tt(fr, fr, q, ALU.add)
                tt(fr, fr, den, ALU.mult)
                tt(fi, ai, lr, ALU.mult)
                tt(q, ar, li, ALU.mult)
                tt(fi, fi, q, ALU.subtract)
                tt(fi, fi, den, ALU.mult)
                link(nc.gpsimd.memset(b_blocks, 0.0))
                link(nc.gpsimd.memset(c_d, 0.0))
                wide = [P, SG, S5_GROUP]
                p1 = tmp1[:, :, 0:S5_GROUP]
                p2 = tmp1[:, :, S5_GROUP:2 * S5_GROUP]
                for c in range(2):
                    tt(p1, bc_raw[:, c], fr.unsqueeze(2).broadcast_to(wide), ALU.mult)
                    tt(p2, bc_raw[:, 1 - c], fi.unsqueeze(2).broadcast_to(wide), ALU.mult)
                    for g in range(2):
                        lanes = slice(S5_STATE * g, S5_STATE * (g + 1))
                        cols = slice(S5_GROUP * g, S5_GROUP * (g + 1))
                        tt(b_blocks[lanes, c, :, cols], p1[lanes], p2[lanes], ALU.add if c else ALU.subtract)
                        ts(c_d[lanes, c, :, cols], bc_raw[lanes, 2 + c], -1.0 if c else 1.0, ALU.mult)
                pool.wait_ge(ss_done, 1)
                link(nc.gpsimd.memset(cos_t[:, :, 0:1], 1.0))
                link(nc.gpsimd.memset(sin_t[:, :, 0:1], 0.0))
                n = 1
                while n < SEQ:
                    w = [P, SG, n]
                    wc, ws = cs.unsqueeze(2).broadcast_to(w), sn.unsqueeze(2).broadcast_to(w)
                    c0, s0 = cos_t[:, :, 0:n], sin_t[:, :, 0:n]
                    c1, s1 = cos_t[:, :, n:2 * n], sin_t[:, :, n:2 * n]
                    p1, p2 = tmp1[:, :, 0:n], tmp2[:, :, 0:n]
                    tt(p1, c0, wc, ALU.mult)
                    tt(p2, s0, ws, ALU.mult)
                    tt(c1, p1, p2, ALU.subtract)
                    tt(p1, c0, ws, ALU.mult)
                    tt(p2, s0, wc, ALU.mult)
                    tt(s1, p1, p2, ALU.add)
                    tt(k, cs, sn, ALU.mult)
                    tt(r, sn, sn, ALU.mult)
                    ts(sn, k, 2.0, ALU.mult)
                    ts(cs, r, -2.0, ALU.mult, 1.0, ALU.add)
                    n *= 2
                ts(half_b[:], par[:, PARAMS['b_glu']], 0.5, ALU.mult)
                pool.nop().then_inc(tables_ready, 1)

            def odd_mixer():
                for what, i in odd:
                    if what == 't5':
                        pool.wait_ge(t5_copied, 1)
                        pool.dma_start(t5_rows, t5_row[0:HEADS, :].unsqueeze(1).broadcast_to([HEADS, P, 512])).then_inc(t5_stored, 16)
                        pool.wait_ge(t5_stored, 16)
                        overlapping = bass.AP(t5_rows.tensor, P - 1, [(511, P), (512 * P, HEADS), (1, T5_COLS)])
                        pool.dma_start(t5, overlapping).then_inc(t5_in, 16)
                    elif what in ('cq', 'ckv'):
                        k = i + (QB if what == 'ckv' else 0)
                        pool.wait_ge(proj_read, reads0 + k + 1)
                        if k == 0:
                            pool.wait_ge(ss_done, NORM['mix1'] + 1)
                        nc.gpsimd.tensor_tensor(sq[:, k, :], lat[:, k, :], lat[:, k, :], ALU.mult).then_inc(lat_squared, 1)
                    elif what == 'lat_squares':
                        pool.wait_ge(lat_ms_ready, 2)
                        nc.gpsimd.tensor_tensor(lat_rstd, lat_ms, halves[:], ALU.pow).then_inc(lat_rstd_ready, 1)
                    elif what == 'kv' and i == 1:
                        pool.wait_ge(proj_read, reads0 + LB + 1 + REP + 2)
                        for g in range(GROUPS):
                            rows = slice(DH * g, DH * (g + 1))
                            pool.dma_start(win[0:DH, :, g, :], kv_raw[rows, :, :]).then_inc(windows_in, 16)
                            pool.dma_start(win[DH:P, :, g, 0:SEQ - 1], kv_raw[rows, :, 1:SEQ]).then_inc(windows_in, 16)
                    elif what == 'hidden':
                        pool.wait_ge(hid_read, 1)
                        nc.gpsimd.tensor_tensor(hid_t, hid, hid, ALU.mult).then_inc(hid_square, 1)
                        pool.wait_ge(hid_square, 1)
                        nc.gpsimd.tensor_scalar(hid_t, hid_t, 0.044715, 1.0, ALU.mult, ALU.add).then_inc(hid_square, 1)
                        pool.wait_ge(hid_square, 2)
                        nc.gpsimd.tensor_tensor(hid_t, hid_t, hid, ALU.mult).then_inc(hid_inner, 1)

            def even_mixer():
                rows = slice(0, F_ROWS)

                def fox_right(g):
                    if g >= 2:
                        pool.wait_ge(scores_done, g - 1)
                    fa, fb = par[rows, PARAMS['fox_a']], par[rows, PARAMS['fox_b']]
                    nc.gpsimd.tensor_scalar(fox_rhs[rows, g % 2, :], cum[rows, :], fa[:, g:g + 1], fb[:, g:g + 1], ALU.mult,
                                            ALU.add).then_inc(fox_rhs_ready, 1)

                for what, i in even:
                    if what == 's5':
                        sin2 = [sin_t[:, j, :].unsqueeze(1).broadcast_to([P, 2, SEQ]) for j in range(SG)]
                        j = i - 1
                        if i < SG:
                            pool.wait_ge(bu_ready, i + 1)
                            if i >= 1:
                                pool.wait_ge(zin_ready, 2 * i)
                            nc.gpsimd.tensor_tensor(sin_in, bu[i % 2], sin2[i], ALU.mult).then_inc(sin_in_ready, 1)
                        if 0 <= j < SG:
                            pool.wait_ge(scanned, 2 * (j + 1))
                            if j >= 1:
                                pool.wait_ge(state_ready, 2 * j)
                            nc.gpsimd.tensor_tensor(sin_out, bu[j % 2], sin2[j], ALU.mult).then_inc(sin_out_ready, 1)
                    elif what == 'f':
                        pool.wait_ge(cum_ready, 1)
                        fl = par[rows, PARAMS['fox_l']]
                        nc.gpsimd.tensor_scalar(fox_lhs[rows, :], cum[rows, :], fl[:, 0:1], fl[:, 1:2], ALU.mult,
                                                ALU.add).then_inc(fox_lhs_ready, 1)
                        fox_right(0)
                    elif what == 'fox' and i < HEADS - 1:
                        fox_right(i + 1)
                    elif what == 'gelu':
                        pool.wait_ge(y_read, i + 1)
                        nc.gpsimd.tensor_tensor(states_tanh[:, i, :], u_t[:, i, :], u_t[:, i, :], ALU.mult).then_inc(y_square, 1)
                        pool.wait_ge(y_square, 2 * i + 1)
                        nc.gpsimd.tensor_scalar(states_tanh[:, i, :], states_tanh[:, i, :], 0.044715, 1.0, ALU.mult,
                                                ALU.add).then_inc(y_square, 1)
                        pool.wait_ge(y_square, 2 * i + 2)
                        nc.gpsimd.tensor_tensor(states_tanh[:, i, :], states_tanh[:, i, :], u_t[:, i, :], ALU.mult).then_inc(y_inner, 1)
                    elif what == 'glu':
                        pool.wait_ge(gelu_ready, UB)
                        nc.gpsimd.tensor_scalar(quarter[:, i, :], u_t[:, i, :], 0.25, None, ALU.mult).then_inc(quarter_ready, 1)

            pool.wait_ge(consts_set, 3)
            for p in phases:
                squares(NORM[p])
                if NORM[p] == 0:
                    pool.wait_ge(params_in, 16)
                    pool.wait_ge(tables_in, 32)
                    s5_tables()
                if p == 'mix0':
                    even_mixer()
                if p == phases[phases.index('mix1') - 1] if 'mix1' in phases else False:
                    pool.dma_start(oc, odd_consts).then_inc(odd_in, 16)
                    pool.dma_start(t5_onehot[0:BUCKETS + 1, :], onehot).then_inc(odd_in, 16)
                if p == 'mix1':
                    odd_mixer()


def odd_unit_arrays(a, by_k):
    import numpy as np

    w = a['l1_w_in']
    starts = np.cumsum([0, Q_RANK, KV_RANK, ROPE, 512, 128, 128, 128, 128, 128, 128])
    c_q, c_kv, k_rope, q_n, k_c, v_c, k_s, v_s, k_w, v_w, g = np.split(w, starts[1:], 1)
    half = ROPE // 2
    swapped = np.concatenate([k_rope[:, half:], k_rope[:, :half]], 1)
    krg = np.zeros((1, P, D), np.float32)
    kr = np.concatenate([k_rope, swapped], 1).reshape(KD, P, 2 * ROPE).transpose(1, 0, 2).reshape(P, -1)
    krg[0, :, :kr.shape[1]] = kr
    krg[0, :, kr.shape[1]:kr.shape[1] + 24 * KD] = g.reshape(KD, P, 24).transpose(1, 0, 2).reshape(P, -1)
    pair = [h for r in range(REP) for h in (r, REP + r)]
    nq = q_n.reshape(D, HEADS, DH)[:, pair].reshape(D, HEADS * DH)
    units = [by_k(c_q), by_k(c_kv), krg, by_k(nq), by_k(np.concatenate([k_c, v_c, k_s, k_w], 1))]
    units.append(np.concatenate([v_s, v_w], 1).reshape(2, 4, P, 2 * P).transpose(0, 2, 1, 3))
    uq = a['l1_mla_w_uq'].reshape(Q_RANK, HEADS, DH + ROPE)
    uq = np.concatenate([uq, uq[:, :, DH + half:], uq[:, :, DH:DH + half]], 2)
    uq4 = np.zeros((4, P, D), np.float32)
    uq4[:, :, :QB * 2 * P] = uq.reshape(QB, P, 4, 2 * P).transpose(2, 1, 0, 3).reshape(4, P, -1)
    units.append(uq4)
    ukv = a['l1_mla_w_ukv'].reshape(KVB, P, HEADS, 2, DH).transpose(3, 1, 0, 2, 4)
    units.append(ukv)
    units += [a['l1_nsa_cmp_' + c + '_w1'].reshape(2, CMP_PAIRS // 2, P, P).transpose(0, 2, 1, 3) for c in 'kv']
    w_out = a['l1_w_out']
    units.append(w_out[:512].reshape(4, P, D))
    units.append(w_out[512:].reshape(HEADS, DH, D)[pair].reshape(4, P, D))
    return [u.reshape(-1, P, D) for u in units]


def odd_constants():
    import numpy as np

    f32 = np.float32
    oc = np.zeros((P, N_OC), f32)
    half = ROPE // 2
    freqs = (f32(10000.0) ** (-np.arange(half, dtype=f32) / f32(half))).astype(f32)
    ang = np.arange(SEQ, dtype=f32)[None, :] * freqs[:, None]
    cos, sin = np.cos(ang).astype(f32), np.sin(ang).astype(f32)
    oc[:, OC['rope']] = np.concatenate([np.ones((DH, SEQ), f32), cos, cos, -sin, sin])
    oc[DH:, OC['sel']] = np.tile(np.eye(ROPE, dtype=f32), (2, 2))
    ends = np.arange(N_CMP) * CMP_STRIDE + CMP_LEN - 1
    pos = np.arange(SEQ).reshape(TT, P).T
    mask = np.zeros((P, TT, 16), f32)
    mask[:, :, :N_CMP] = ends[None, None, :] <= pos[:, :, None]
    oc[:, OC['mask']] = mask.reshape(P, -1)
    oc[:, OC['block']] = 0.5 * np.repeat(np.eye(HEADS, dtype=f32), 16, 0)
    dist = 2 * P - 1 - np.arange(512)
    exact = BUCKETS // 2
    far = exact + (np.log(np.maximum(dist, exact).astype(f32) / f32(exact)) / f32(math.log(128 / exact))
                   * f32(BUCKETS - exact)).astype(np.int32)
    bucket = np.where(dist < exact, dist, np.minimum(far, BUCKETS - 1))
    bucket = np.where(dist < 0, BUCKETS, bucket)
    return oc, (np.arange(BUCKETS + 1)[:, None] == bucket[None, :]).astype(f32)


def kernel(**inputs):
    import ml_dtypes
    import numpy as np
    import concourse.bacc as bacc
    from concourse.bass_utils import run_bass_kernel_spmd as run

    nc = bacc.Bacc("TRN2", target_bir_lowering=False, num_devices=1)
    a = {k: np.asarray(v) for k, v in inputs.items()}
    ffns = [{'ffn0': 'l0_ffn1', 'ffn1': 'l0_ffn2', 'ffn2': 'l1_ffn1', 'ffn3': 'l1_ffn2'}[p] for p in PHASES if p[0:3] == 'ffn']

    def by_k(w):
        k, n = w.shape
        return w.reshape(k // P, P, n // P, P).transpose(2, 1, 0, 3)

    w_gu = np.concatenate([np.stack([by_k(a[f + '_w_gate']), by_k(a[f + '_w_up'])], 2) for f in ffns])
    w_d = np.concatenate([a[f + '_w_down'].reshape(CH, P, D) for f in ffns])
    norms = {'ffn0': 'l0_ffn1_norm', 'mix0': 'l0_mix_norm', 'ffn1': 'l0_ffn2_norm', 'ffn2': 'l1_ffn1_norm',
             'mix1': 'l1_mix_norm', 'ffn3': 'l1_ffn2_norm', 'final': 'final_norm'}
    par = np.zeros((P, N_PARAMS), np.float32)

    def lanes(w):
        return w.reshape(SG, P, *w.shape[2:]).swapaxes(0, 1)

    def put(name, w):
        w = np.asarray(w)
        par[:w.shape[0], PARAMS[name]] = w.reshape(w.shape[0], -1)

    put('gain', np.stack([a[norms[p]].reshape(KD, P).T for p in PHASES], 1))
    put('lam_re', lanes(a['l0_s5_lambda_re']))
    put('lam_im', lanes(a['l0_s5_lambda_im']))
    put('log_dt', lanes(np.repeat(a['l0_s5_log_dt'][:, None], S5_STATE, 1)))
    put('d_skip', a['l0_s5_d'].reshape(UB, P).T)
    put('b_glu', a['l0_s5_b_glu'].reshape(UB, P).T)
    for r in (0, 64):
        par[r:r + 8, PARAMS['b_f']] = par[r + 32:r + 40, PARAMS['b_f']] = a['l0_fox_b_f'][:, None]
        par[r:r + 8, PARAMS['fox_a']] = -8 * np.eye(8, dtype=np.float32)
        par[r + 32:r + 40, PARAMS['fox_b']] = np.eye(8, dtype=np.float32)
        par[r:r + 32, PARAMS['fox_l']] = np.array([0, 1], np.float32)
        par[r + 32:r + 40, PARAMS['fox_l']] = np.array([8, 0], np.float32)
    s5_bc = np.stack([lanes(a['l0_s5_b_re']), lanes(a['l0_s5_b_im']), lanes(a['l0_s5_c_re'].swapaxes(1, 2)),
                      lanes(a['l0_s5_c_im'].swapaxes(1, 2))], 1)
    w_in = a['l0_w_in']
    blocks = by_k(w_in[:, :2048]).reshape(16, P, D)
    w_f = np.zeros((KD, P, F_ROWS), np.float32)
    for r in (0, 32, 64, 96):
        w_f[:, :, r:r + 8] = w_in[:, 2048:].reshape(KD, P, 8)
    f_unit = np.zeros((1, P, D), np.float32)
    f_unit[0, :, :KD * F_ROWS] = w_f.transpose(1, 0, 2).reshape(P, KD * F_ROWS)
    qk = blocks[4:12].reshape(2, 4, P, D).swapaxes(0, 1).reshape(8, P, D)
    w_v = w_in[:, 1536:2048].reshape(4, 2, P, 512).transpose(0, 2, 1, 3).reshape(4, P, D)
    w_out = a['l0_w_out'].reshape(8, P, D)
    glu = by_k(a['l0_s5_w_glu']).reshape(2, 2, P, 4 * P).transpose(0, 2, 1, 3).reshape(2, P, D)
    units = [blocks[:4], f_unit, qk, w_v, w_out[4:], glu, w_out[:4]]
    if 'mix0' not in PHASES:
        units = []
    if 'mix1' in PHASES:
        put('q_norm', a['l1_mla_q_norm'].reshape(QB, P).T)
        put('kv_norm', a['l1_mla_kv_norm'].reshape(KVB, P).T)
        par[:, PARAMS['b_gate']] = a['l1_nsa_b_gate'][None, :]
        put('pe', np.concatenate([a['l1_nsa_cmp_pe_' + c].reshape(CMP_PAIRS, P).T for c in 'kv'], 1))
        put('w2', np.concatenate([a['l1_nsa_cmp_k_w2'], a['l1_nsa_cmp_v_w2']], 1))
        put('rel', a['rel_bias'])
        par[BUCKETS, PARAMS['rel']] = MASKED / 8
        units += odd_unit_arrays(a, by_k)
    rows, cols = np.arange(P)[:, None], np.arange(P)[None, :]
    tri = np.where(cols <= rows, 0, MASKED).astype(np.float32)
    oc, onehot = odd_constants()
    arrays = {
        'x_t': a['x'][0].T.reshape(KD, P, SEQ).transpose(1, 0, 2),
        'w_gate_up': w_gu.reshape(-1, P, 2 * KD * P),
        'w_down': w_d,
        'params': par,
        's5_bc': s5_bc.reshape(P, -1),
        'mix_units': np.concatenate(units),
        'ident_in': np.eye(P, dtype=np.float32),
        'odd_consts': oc,
        'onehot': onehot,
        'causal_in': np.concatenate([tri, np.zeros_like(tri), tri], 1).astype(ml_dtypes.bfloat16),
    }
    order = ['x_t', 'w_gate_up', 'w_down', 'params', 's5_bc', 'mix_units', 'ident_in', 'causal_in', 'odd_consts', 'onehot']
    arrays = {k: np.ascontiguousarray(arrays[k]) for k in order}
    args = [nc.dram_tensor(k, v.shape, mybir.dt.from_np(v.dtype), kind="ExternalInput").ap() for k, v in arrays.items()]
    out = nc.dram_tensor('out', (SEQ, D), F32, kind="ExternalOutput").ap()
    t5_rows = nc.dram_tensor('t5_rows', (HEADS, P, 512), F32, kind="Internal").ap()
    trunk(nc, *args, t5_rows, out)
    r = run(nc, [arrays], core_ids=[0])
    return r.results[0]['out'].reshape(1, SEQ, D)
```

```python
import math
from contextlib import ExitStack

import concourse.bass as bass
from concourse import mybir

F32 = mybir.dt.float32
F32R = mybir.dt.float32r
ALU = mybir.AluOpType
ACT = mybir.ActivationFunctionType
AX = mybir.AxisListType

P = 128
D = 1024
SEQ = 256
KD = D // P
TT = SEQ // P
D_FF = 2816
CH = D_FF // P
EPS = 1e-6
PHASES = ['ffn0', 'mix0', 'ffn1', 'ffn2', 'mix1', 'ffn3', 'final']

S5_WIDTH = D // 2
S5_GROUP = 16
S5_STATE = 64
SG = S5_WIDTH // S5_GROUP // 2
UB = S5_WIDTH // P
PER = SG // UB
GC = 2 * S5_GROUP
HEADS = 8
DH = 64
PAIRS = HEADS // 2
F_ROWS = 104
MASKED = -1e30
ARENA = 15360
RING = 3
ATT_COLS = 3 * P
WARM_UP = 20
KEYS = [slice(0, P), slice(P, 3 * P)]

Q_RANK = 384
KV_RANK = 256
QB = Q_RANK // P
KVB = KV_RANK // P
LB = QB + KVB
ROPE = 32
GROUPS = 2
REP = HEADS // GROUPS
CMP_LEN = 32
CMP_STRIDE = 16
N_CMP = (SEQ - CMP_LEN) // CMP_STRIDE + 1
CMP_PAIRS = CMP_LEN // 2
T5_COLS = 3 * P
BUCKETS = 32
GATES_AT = DH + KD * 2 * ROPE
OC = {'rope': slice(0, 256), 'sel': slice(256, 320), 'mask': slice(320, 352), 'block': slice(352, 360)}
N_OC = 360

PARAMS = {}
_at = 0
for _name, _n in [('gain', len(PHASES) * KD), ('lam_re', SG), ('lam_im', SG), ('log_dt', SG), ('d_skip', UB), ('b_glu', UB),
                  ('b_f', 1), ('fox_a', PAIRS), ('fox_b', PAIRS), ('fox_l', 2), ('q_norm', 3), ('kv_norm', 2),
                  ('b_gate', 24), ('pe', 32), ('w2', 128), ('rel', 8)]:
    PARAMS[_name] = slice(_at, _at + _n)
    _at += _n
N_PARAMS = _at

MAG = 1
MAGIC = 12582912.0
TWO_PI = (6.28125, 1.93500518798828125e-3, 3.01991598196765e-7)
LN2 = (0.693359375, -2.12194440e-4)
NORM = {p: m for m, p in enumerate(PHASES)}
ODD_HEADS = 3 * HEADS


def even_order():
    order = [('u', 0), ('u', 1), ('squares', 0), ('v', 0), ('spread', 0), ('b_t', 0), ('u', 2), ('u', 3), ('f', 0)]
    inputs = [(x, i) for i in range(PAIRS) for x in 'qk'] + [('v', i) for i in range(1, 4)]
    att = [('fox', s) for s in range(HEADS + 3)]
    for j in range(SG + 3):
        order.append(inputs.pop(0) if inputs else att.pop(0))
        if j == 0:
            order.append(('f_end', 0))
        order.append(('s5', j))
        b, step = divmod(j - 2 - PER, PER)
        if 0 <= b < UB - 1:
            order.append((('gelu', 'gelu_square', 'gelu_inner', 'gelu_tanh')[step], b))
    order += [('gelu_end', UB - 2), ('gelu', UB - 1), att[0], ('gelu_square', UB - 1), ('out', 0), ('gelu_inner', UB - 1), att[1],
              ('gelu_tanh', UB - 1), ('out', 1), ('gelu_end', UB - 1), att[2], ('gelu_split', 0), ('out', 2)]
    return order + [('glu', i) for i in range(4)] + [('out', i) for i in range(3, KD)]


def odd_order():
    order = [('t5', 0), ('cq', 0), ('cq', 1), ('squares', 0), ('vsw', 0), ('spread', 0), ('cq', 2), ('ckv', 0), ('ckv', 1),
             ('krg', 0), ('nq', 0), ('lat_squares', 0), ('nq', 1), ('sel', 0), ('nq', 2), ('lat_spread', 0), ('nq', 3)]
    order += [('kv', i) for i in range(4)] + [('vsw', 1)] + [('uq', i) for i in range(HEADS)]
    order += [('uk', i) for i in range(HEADS)] + [('w1', 0), ('uv', 0), ('w1', 1)]
    between = {1: ('w1', 2), 2: ('w1', 3), 3: ('hidden', 0), 5: ('compress', 0), 6: ('cmp_scores', 0), 8: ('cmp_softmax', 0),
               10: ('cmp_weights', 0), 12: ('cmp_turn', 0)}
    for s in range(ODD_HEADS + 4):
        order.append(('att', s))
        if s in between:
            order.append(between[s])
    return order + [('out', i) for i in range(KD)]


SPLIT_KINDS = ('u', 'f', 'q', 'k', 'v', 'glu', 'out', 'cq', 'ckv', 'krg', 'nq', 'kv', 'vsw')
PLAIN_KINDS = ('uq', 'uk', 'uv', 'w1')
USES = {'glu': 2, 'uq': 2, 'uk': HEADS}
UNIT = {}
SPLIT_SLOT = {}
SPLIT_BEFORE = {}
SLOT_FREE = {}
ORDER = {}
AHEAD = 3
SPLIT_AT = {('mix0', 'out', 0): ('fox', 6),
            ('mix0', 'out', 1): ('fox', 8), ('mix0', 'out', 2): ('fox', 9),
            ('mix1', 'out', 0): ('att', 14), ('mix1', 'out', 1): ('att', 17), ('mix1', 'out', 2): ('att', 20),
            ('mix1', 'out', 3): ('att', 23)}


def lay_out_units():
    at = 0
    total = 0
    for mixer, order in (('mix0', even_order()), ('mix1', odd_order())):
        first = at
        kinds = []
        for what, i in order:
            if what in SPLIT_KINDS or what in PLAIN_KINDS:
                key = (mixer, what, i // USES.get(what, 1))
                if key not in UNIT:
                    UNIT[key] = at
                    kinds.append(what)
                    at += 1
        split = [first + n for n, what in enumerate(kinds) if what in SPLIT_KINDS]
        holder = {}
        for n, u in enumerate(split):
            slot = n % 4 if n < len(split) - 4 else (4, 2, 3, 4)[n - len(split) + 4]
            SPLIT_SLOT[u], SPLIT_BEFORE[u], SLOT_FREE[u] = slot, total, holder.get(slot)
            holder[slot] = u
            total += 1
        seen = first - 1
        to_split = split[AHEAD:]
        out = []
        rests = []
        held = {UNIT[key]: place for key, place in SPLIT_AT.items() if key[0] == mixer}
        for what, i in order:
            u = UNIT.get((mixer, what, i // USES.get(what, 1)))
            new = []
            if u is not None and u > seen:
                seen = u
                while to_split and to_split[0] not in held and to_split[0] <= u + AHEAD and u > (SLOT_FREE[to_split[0]] or 0):
                    new.append(to_split.pop(0))
            out += [('split_hi', n) for n in new]
            out.append((what, i))
            out += [('split_lo', n) for n in rests]
            rests = new
            if to_split and held.get(to_split[0]) == (what, i):
                rests = rests + [to_split.pop(0)]
                out.append(('split_hi', rests[-1]))
            if not to_split and not rests and ('next_gate_up', 0) not in out:
                out.append(('next_gate_up', 0))
        ORDER[mixer] = out
        ORDER[mixer, 'first'] = first
        ORDER[mixer, 'end'] = at
    return at


N_UNITS = lay_out_units()


def trunk(nc, x_t, w_gate_up, w_down, params, s5_bc, mix_units, ident_in, causal_in, odd_consts, onehot, t5_rows, out):
    with ExitStack() as ctx:
        def sb(name, shape, dt=F32):
            return ctx.enter_context(nc.sbuf_tensor(name, shape, dt))

        def sem(name):
            return ctx.enter_context(nc.semaphore(name))

        h = sb('h', [P, KD, SEQ])
        xh = sb('xh', [P, KD, SEQ], F32R)
        xl = sb('xl', [P, KD, SEQ], F32R)
        sq = sb('sq', [P, KD, SEQ])
        raw_gu = sb('raw_gu', [P, 2, 2 * KD * P])
        raw_d = sb('raw_d', [P, 2, D])
        hi_gu = sb('hi_gu', [P, 2, 2 * KD * P], F32R)
        lo_gu = sb('lo_gu', [P, 2, 2 * KD * P], F32R)
        hi_d = sb('hi_d', [P, 2, D], F32R)
        lo_d = sb('lo_d', [P, 2, D], F32R)
        scratch = sb('scratch', [P, 10 * SEQ])
        gs = scratch[:, 0:4 * SEQ].rearrange('p (s a t) -> p s a t', s=2, a=2)
        th = scratch[:, 4 * SEQ:6 * SEQ].rearrange('p (s t) -> p s t', s=2)
        ga = scratch[:, 6 * SEQ:8 * SEQ].rearrange('p (s t) -> p s t', s=2)
        diag = scratch[:, 0:TT * P].rearrange('p (t n) -> p t n', t=TT)
        prod = scratch[:, 8 * SEQ:10 * SEQ].rearrange('p (s t) -> p s t', s=2)
        ph = sb('ph', [P, 2, SEQ], F32R)
        pl = sb('pl', [P, 2, SEQ], F32R)
        par = sb('par', [P, N_PARAMS])
        gain = par[:, PARAMS['gain']].rearrange('p (m k) -> p m k', k=KD)
        ring = sb('ring', [P, RING, D])
        spare_hi = sb('spare_hi', [P, D], F32R)
        spare_lo = sb('spare_lo', [P, D], F32R)
        causal = sb('causal', [P, ATT_COLS], mybir.dt.bfloat16)
        arena = sb('arena', [P, ARENA])
        ident = sb('ident', [P, P])
        ones = sb('ones', [P, P])
        halves = sb('halves', [P, 4])
        ms = sb('ms', [P, TT])
        rstd = sb('rstd', [P, TT])
        rbc = sb('rbc', [P, SEQ])
        o_sb = raw_gu[:, :, 0:D]

        out_hi = [hi_d[:, i, :].rearrange('p (b t) -> p b t', b=4) for i in range(2)]
        out_lo = [lo_d[:, i, :].rearrange('p (b t) -> p b t', b=4) for i in range(2)]
        xf = arena[:, 0:KD * SEQ].rearrange('p (k t) -> p k t', k=KD)

        def unit_hi_lo(u):
            slot = SPLIT_SLOT[u]
            if slot == 4:
                return spare_hi[:], spare_lo[:]
            w = slice(slot % 2 * D, (slot % 2 + 1) * D)
            return hi_gu[:, slot // 2, w], lo_gu[:, slot // 2, w]

        at = 0

        def region(n):
            nonlocal at
            at += n
            assert at <= ARENA
            return arena[:, at - n:at]

        cos_t = region(SG * SEQ).rearrange('p (j t) -> p j t', j=SG)
        sin_t = region(SG * SEQ).rearrange('p (j t) -> p j t', j=SG)
        u_t = region(UB * SEQ).rearrange('p (b t) -> p b t', b=UB)
        q_t = region(PAIRS * SEQ).rearrange('p (b t) -> p b t', b=PAIRS)
        k_t = region(PAIRS * SEQ).rearrange('p (b t) -> p b t', b=PAIRS)
        v_n = region(TT * HEADS * DH).rearrange('p (t n) -> p t n', t=TT)
        b_t = region(2 * UB * P).rearrange('p (c b n) -> p c b n', c=2, b=UB)
        c_d = region(2 * SG * GC).rearrange('p (c j n) -> p c j n', c=2, j=SG)
        cum = region(SEQ)
        fox_lhs = region(SEQ)
        fox_rhs = region(2 * SEQ).rearrange('p (s t) -> p s t', s=2)
        s5z = sb('s5z', [P, 4 * SEQ])
        small = sb('small', [P, 13, SG])
        s5_out = arena[:, 0:UB * SEQ].rearrange('p (b t) -> p b t', b=UB)
        quarter = arena[:, UB * SEQ:2 * UB * SEQ].rearrange('p (b t) -> p b t', b=UB)
        at = 0
        t5 = region(HEADS * T5_COLS).rearrange('p (h x) -> p h x', h=HEADS)
        lat = region(LB * SEQ).rearrange('p (b t) -> p b t', b=LB)
        mq = region(HEADS * SEQ).rearrange('p (h t) -> p h t', h=HEADS)
        mk = region(HEADS * SEQ).rearrange('p (h t) -> p h t', h=HEADS)
        mv = region(TT * HEADS * DH).rearrange('p (t n) -> p t n', t=TT)
        nq = region(REP * SEQ).rearrange('p (r t) -> p r t', r=REP)
        kv_raw = region(2 * SEQ).rearrange('p (c t) -> p c t', c=2)
        ksw = region(2 * SEQ).rearrange('p (c t) -> p c t', c=2)
        vsw = region(TT * 2 * P).rearrange('p (t n) -> p t n', t=TT)
        win = region(4 * SEQ).rearrange('p (c g t) -> p c g t', c=2, g=GROUPS)
        blk = region(2 * CMP_PAIRS * GROUPS * N_CMP).rearrange('p (c i g n) -> p c i g n', c=2, i=CMP_PAIRS, g=GROUPS)
        oc = region(N_OC)
        kr = region(SEQ)
        hid = region(4 * N_CMP).rearrange('p (a n) -> p a n', a=2)
        hid_t = region(4 * N_CMP).rearrange('p (a n) -> p a n', a=2)
        hid_v = region(P)
        rope = oc[:, OC['rope']]
        t5_onehot = mv[:, 0, :]
        t5_row = mv[:, 1, :]
        v_block = s5z[:, 0:HEADS * DH].rearrange('p (h d) -> p h d', h=HEADS)
        pc = s5z[:, 512:768].rearrange('p (t h n) -> p t h n', t=TT, h=HEADS)
        pc_t = s5z[:, 768:1024]
        sflat = small[:].rearrange('p a b -> p (a b)')
        gates = sflat[:, 0:48].rearrange('p (t n) -> p t n', t=TT)
        logits = sflat[:, 48:96].rearrange('p (t n) -> p t n', t=TT)
        kc = sflat[:, 96:96 + N_CMP]
        c_max = sflat[:, 112:128].rearrange('p (t h) -> p t h', t=TT)
        c_sum = sflat[:, 128:144].rearrange('p (t h) -> p t h', t=TT)
        lat_ms = sflat[:, 144:148]
        lat_rstd = sflat[:, 148:152]
        lat_diag = scratch[:, 0:4 * P].rearrange('p (t n) -> p t n', t=4)
        bc_raw = k_t.rearrange('p b t -> p (b t)').rearrange('p (c j n) -> p c j n', c=4, j=SG)
        b_blocks = v_n.rearrange('p t n -> p (t n)').rearrange('p (c j n) -> p c j n', c=2, j=SG)
        tmp1 = arena[:, 2 * SG * SEQ:2 * SG * SEQ + SG * P].rearrange('p (j t) -> p j t', j=SG)
        tmp2 = sq[:].rearrange('p k t -> p (k t)').rearrange('p (j t) -> p j t', j=SG)
        sqf = sq[:].rearrange('p k t -> p (k t)')
        bu = [sqf[:, 2 * i * SEQ:2 * (i + 1) * SEQ].rearrange('p (c t) -> p c t', c=2) for i in range(2)]
        cos_in = sqf[:, 4 * SEQ:6 * SEQ].rearrange('p (c t) -> p c t', c=2)
        sin_in = sqf[:, 6 * SEQ:8 * SEQ].rearrange('p (c t) -> p c t', c=2)
        sin_out = scratch[:, 5 * ATT_COLS:5 * ATT_COLS + 2 * SEQ].rearrange('p (c t) -> p c t', c=2)
        states = [s5z[:, 2 * i * SEQ:2 * (i + 1) * SEQ].rearrange('p (c t) -> p c t', c=2) for i in range(2)]
        probs = [scratch[:, i * ATT_COLS:(i + 1) * ATT_COLS] for i in (0, 1, 2, 5)]

        def slot_of(g):
            return g % 3 if g < HEADS else (g - HEADS) % 4

        probs_t = [scratch[:, (3 + i) * ATT_COLS:(4 + i) * ATT_COLS] for i in range(2)]
        states_tanh = sin_t[:, 0:SG:PER, :]
        minus_one = sb('minus_one', [P, SG])
        half_b = sb('half_b', [P, UB])
        stats = sb('stats', [P, 4, 3, TT])

        bank = [ctx.enter_context(nc.psum_tensor(f'bank{i}', [P, 512], F32)) for i in range(8)]

        def acc(j):
            return bank[j // 2][:, (j % 2) * SEQ:(j % 2 + 1) * SEQ]

        GU = [bank[4], bank[5]]
        misc = bank[7]
        final_bank = [[bank[4], bank[5]], [bank[6], bank[0]]]

        params_in = sem('params_in')
        x_in = [sem('x_in0'), sem('x_in1')]
        first_gate_in = sem('first_gate_in')
        first_hi = sem('first_hi')
        first_lo = sem('first_lo')
        functions_in = sem('functions_in')
        ident_loaded = sem('ident_loaded')
        tables_in = sem('tables_in')
        raw_gu_in = [sem('raw_gu_in0'), sem('raw_gu_in1')]
        raw_d_in = [sem('raw_d_in0'), sem('raw_d_in1')]
        gu_hi = sem('gu_hi')
        gu_lo = sem('gu_lo')
        d_hi = sem('d_hi')
        d_lo = sem('d_lo')
        consts_set = sem('consts_set')
        h_ready = sem('h_ready')
        xf_ready = sem('xf_ready')
        even_squared = sem('even_squared')
        odd_squared = sem('odd_squared')
        sq_ready = sem('sq_ready')
        x_hi = sem('x_hi')
        x_lo = sem('x_lo')
        ss_done = sem('ss_done')
        ms_ready = sem('ms_ready')
        rstd_ready = sem('rstd_ready')
        diag_ready = sem('diag_ready')
        rbc_done = sem('rbc_done')
        rbc_ready = sem('rbc_ready')
        gateup_done = sem('gateup_done')
        gate_scaled = sem('gate_scaled')
        tanh_done = sem('tanh_done')
        a_ready = sem('a_ready')
        prod_ready = sem('prod_ready')
        ph_ready = sem('ph_ready')
        act_lo = sem('act_lo')
        down_done = sem('down_done')
        unit_in = [sem(f'unit_in{i}') for i in range(RING)]
        unit_used = sem('unit_used')
        unit_hi = sem('unit_hi')
        unit_lo = sem('unit_lo')
        out_hi_ready = sem('out_hi_ready')
        out_lo_ready = sem('out_lo_ready')
        s5_prep = sem('s5_prep')
        b_t_done = sem('b_t_done')
        b_t_ready = sem('b_t_ready')
        proj_read = sem('proj_read')
        v_ready = sem('v_ready')
        f_x = sem('f_x')
        f_neg = sem('f_neg')
        f_exp = sem('f_exp')
        f_ln = sem('f_ln')
        f_log = sem('f_log')
        cum_ready = sem('cum_ready')
        fox_lhs_ready = sem('fox_lhs_ready')
        fox_rhs_ready = sem('fox_rhs_ready')
        scores_done = sem('scores_done')
        biased = sem('biased')
        exp_done = sem('exp_done')
        factor = sem('factor')
        gated = sem('gated')
        probs_ready = sem('probs_ready')
        probs_0_ready = sem('probs_0_ready')
        probs_t_done = sem('probs_t_done')
        probs_t_ready = sem('probs_t_ready')
        heads_done = sem('heads_done')
        heads_out = sem('heads_out')
        bu_done = sem('bu_done')
        bu_ready = sem('bu_ready')
        cos_in_ready = sem('cos_in_ready')
        sin_in_ready = sem('sin_in_ready')
        zin_ready = sem('zin_ready')
        scanned = sem('scanned')
        cos_out_ready = sem('cos_out_ready')
        sin_out_ready = sem('sin_out_ready')
        state_re_ready = sem('state_re_ready')
        state_im_ready = sem('state_im_ready')
        gelu_hi_ready = sem('gelu_hi_ready')
        gelu_lo_ready = sem('gelu_lo_ready')
        y_done = sem('y_done')
        y_read = sem('y_read')
        y_square = sem('y_square')
        y_inner = sem('y_inner')
        gelu_tanh = sem('gelu_tanh')
        gelu_ready = sem('gelu_ready')
        quarter_ready = sem('quarter_ready')
        glu_done = sem('glu_done')
        glu_tanh = sem('glu_tanh')
        s5_ready = sem('s5_ready')
        mix_done = sem('mix_done')
        tables_ready = sem('tables_ready')
        t5_copied = sem('t5_copied')
        t5_stored = sem('t5_stored')
        t5_in = sem('t5_in')
        odd_in = sem('odd_in')
        lat_squared = sem('lat_squared')
        lat_ss_done = sem('lat_ss_done')
        lat_ms_ready = sem('lat_ms_ready')
        lat_rstd_ready = sem('lat_rstd_ready')
        lat_diag_ready = sem('lat_diag_ready')
        lat_spread_done = sem('lat_spread_done')
        lat_ready = sem('lat_ready')
        krope_ready = sem('krope_ready')
        krope_done = sem('krope_done')
        krope_copied = sem('krope_copied')
        logits_read = sem('logits_read')
        gate_tanh = sem('gate_tanh')
        gates_ready = sem('gates_ready')
        windows_in = sem('windows_in')
        blocks_ready = sem('blocks_ready')
        hid_read = sem('hid_read')
        hid_square = sem('hid_square')
        hid_inner = sem('hid_inner')
        hid_tanh = sem('hid_tanh')
        hid_ready = sem('hid_ready')
        hid_v_ready = sem('hid_v_ready')
        cmp_made = sem('cmp_made')
        kc_ready = sem('kc_ready')
        v_block_ready = sem('v_block_ready')
        cmp_scored = sem('cmp_scored')
        cmp_step = sem('cmp_step')
        cmp_exp = sem('cmp_exp')
        cmp_ready = sem('cmp_ready')
        cmp_turned = sem('cmp_turned')
        pc_t_ready = sem('pc_t_ready')
        cmp_weighed = sem('cmp_weighed')
        mla_v_ready = sem('mla_v_ready')
        part_done = sem('part_done')
        t5_made = sem('t5_made')
        final_t = sem('final_t')
        scaled_dve = sem('scaled_dve')
        scaled_act = sem('scaled_act')
        stored = sem('stored')

        def pairs(eng, step, n):
            c0 = CH * n
            lead = 1 if n == 0 else 0
            tail = 1 if n != 1 else 0
            if lead:
                step(0, 0, 0)
                step(1, 1, 0)
            with eng.Fori(lead, CH // 2 - tail) as i:
                step(c0 + 2 * i, 0, c0 // 2 + i)
                step(c0 + 2 * i + 1, 1, c0 // 2 + i)
            if tail:
                c = c0 + CH - 2
                mixer = PHASES[NORM[f'ffn{n}'] + 1]
                first = ORDER[mixer, 'first'] if mixer in ORDER else None
                step(c, 0, c // 2, more_gu=False, units=[first, first + 1] if mixer in ORDER else [])
                step(c + 1, 1, c // 2, more_gu=False, more_d=False, units=[first + 2] if mixer in ORDER else [])

        even, odd = ORDER['mix0'], ORDER['mix1']
        v0 = TT
        heads0 = HEADS
        reads0 = UB + 1 + 2 * PAIRS
        out0 = PAIRS
        mixes0 = KD - 1
        glu_bank = [bank[6], bank[7]]
        cmp_scores_in = [bank[0][:, 0:P], bank[1][:, 320:320 + P]]

        def o_bank(b):
            return (bank[7], bank[6])[b % 2]

        def y_bank(b):
            return bank[7] if b == 1 else bank[1]

        small_ps = bank[1]

        def used(mixer, what, i=0):
            return UNIT[mixer, what, i // USES.get(what, 1)] + 1

        def nsa(s):
            return s // 4, s // 2 % 2, s % 2

        block = ctx.enter_context(nc.Block())

        @block.sync
        def _(sp):
            def load_gu(c, s):
                sp.dma_start(raw_gu[:, s, :], w_gate_up[bass.ds(c, 1)].rearrange('o p n -> (o p) n')).then_inc(raw_gu_in[s], 16)

            def load_d(c, s):
                sp.dma_start(raw_d[:, s, :], w_down[bass.ds(c, 1)].rearrange('o p n -> (o p) n')).then_inc(raw_d_in[s], 16)

            def load_pairs(first, count):
                with sp.Fori(first, first + count) as i:
                    for s in range(2):
                        sp.wait_ge(gu_lo, 2 * (2 * i + s - 1))
                        load_gu(2 * i + s, s)
                        sp.wait_ge(d_lo, 2 * i + s - 1)
                        load_d(2 * i + s, s)

            def load_unit(u, slot):
                sp.dma_start(ring[:, slot, :], mix_units[bass.ds(u, 1)].rearrange('o p n -> (o p) n')).then_inc(unit_in[slot], 16)

            def load_units(first, end):
                for u in range(first, end):
                    before = u - RING
                    if before in SPLIT_SLOT:
                        sp.wait_ge(unit_lo, SPLIT_BEFORE[before] + 1)
                    elif before >= 0:
                        sp.wait_ge(unit_used, before + 1)
                    load_unit(u, u % RING)

            sp.dma_start(par[:], params).then_inc(params_in, 16)
            for half in range(2):
                ks = slice(half * KD // 2, (half + 1) * KD // 2)
                sp.dma_start(h[:, ks, :], x_t[:, ks, :]).then_inc(x_in[half], 16)
            sp.dma_start(raw_gu[:, 0, 0:D], w_gate_up[0, :, 0:D]).then_inc(first_gate_in, 16)
            sp.dma_start(raw_gu[:, 0, D:2 * D], w_gate_up[0, :, D:2 * D]).then_inc(raw_gu_in[0], 16)
            sp.dma_start(ident[:], ident_in).then_inc(ident_loaded, 16)
            load_gu(1, 1)
            load_d(0, 0)
            load_d(1, 1)
            sp.dma_start(k_t.rearrange('p b t -> p (b t)'), s5_bc).then_inc(tables_in, 16)
            sp.dma_start(causal[:], causal_in).then_inc(tables_in, 16)
            half = CH // 2
            load_pairs(1, half - 1)
            u = ORDER['mix0', 'first']
            load_units(u, u + RING)
            load_pairs(half, 1)
            load_units(u + RING, ORDER['mix0', 'end'])
            load_pairs(half + 1, 2 * half - 1)
            u = ORDER['mix1', 'first']
            load_units(u, u + RING)
            load_pairs(3 * half, 1)
            load_units(u + RING, ORDER['mix1', 'end'])
            load_pairs(3 * half + 1, half - 1)

            for i in range(2):
                for t, scaled in enumerate((scaled_dve, scaled_act)):
                    cols = slice(i * 512, (i + 1) * 512)
                    sp.wait_ge(scaled, i + 1)
                    sp.dma_start(out[t * P:(t + 1) * P, cols], o_sb[:, t, cols]).then_inc(stored, 16)
            sp.wait_ge(stored, 64)

        @block.tensor
        def _(pe):
            def product3(dst, w_hi, w_lo, x_hi_ap, x_lo_ap, start, stop):
                nc.tensor.matmul(dst, w_hi, x_hi_ap, start=start, stop=False, skip_group_check=True)
                nc.tensor.matmul(dst, w_hi, x_lo_ap, start=False, stop=False, skip_group_check=True)
                return nc.tensor.matmul(dst, w_lo, x_hi_ap, start=False, stop=stop, skip_group_check=True)

            def square_sums(m):
                for t in range(TT):
                    for k in range(0, KD, 2):
                        if t == 0:
                            pe.wait_ge(sq_ready, KD // 2 * m + k // 2 + 1)
                        last = nc.tensor.matmul(misc[:, t:t + 1], sq[:, k, t * P:(t + 1) * P], ones[:, 0:1],
                                                start=(k == 0), stop=(k == KD - 2))
                last.then_inc(ss_done, 1)

            def spread_rstd(m):
                pe.wait_ge(diag_ready, TT * (m + 1))
                for t in range(TT):
                    last = nc.tensor.matmul(misc[:, SEQ + t * P:SEQ + (t + 1) * P], ones[:], diag[:, t, :],
                                            start=True, stop=True)
                last.then_inc(rbc_done, 1)

            def gateup(c, s, first=None, second=None):
                if not (isinstance(c, int) and c < 2):
                    pe.wait_ge(gate_scaled, c - 1)
                if first == 0:
                    pe.wait_ge(first_lo, 1)
                else:
                    pe.wait_ge(gu_lo, 2 * c + 1)
                order = [(half, k) for half in range(2) for k in range(KD)]
                if first:
                    order = [(half, k) for k in range(KD) for half in range(2)]
                for at_, (half, k) in enumerate(order):
                    if first is not None and half == 0:
                        pe.wait_ge(x_lo, KD * norm_of[first] + k + 1)
                    if first == 0 and at_ == KD // 2:
                        pe.wait_ge(gu_lo, 1)
                    if at_ == (1 if first else KD):
                        pe.wait_ge(gu_lo, 2 * c + 2)
                    if second is not None and at_ == KD // 2:
                        spread_rstd(norm_of[second])
                    w = slice((half * KD + k) * P, (half * KD + k + 1) * P)
                    last = product3(GU[s][:, half * SEQ:(half + 1) * SEQ], hi_gu[:, s, w], lo_gu[:, s, w],
                                    xh[:, k, :], xl[:, k, :], at_ == 0, False)
                last.then_inc(gateup_done, 1)
                if first is not None:
                    square_sums(norm_of[first])

            def down(c, s, first=False):
                pe.wait_ge(act_lo, c + 1)
                pe.wait_ge(d_lo, c + 1)
                for j in range(KD):
                    w = slice(j * P, (j + 1) * P)
                    product3(acc(j), hi_d[:, s, w], lo_d[:, s, w], ph[:, s, :], pl[:, s, :],
                             first and j % 2 == 0, False).then_inc(down_done, 1)

            norm_of = [NORM[p] for p in PHASES if p.startswith('ffn')]

            def ffn(n):
                c0 = CH * n
                gateup(c0, 0, first=n)
                gateup(c0 + 1, 1, second=n)
                down(c0, 0, first=True)
                with pe.Fori(0, CH // 2 - 1) as i:
                    gateup(c0 + 2 * i + 2, 0)
                    down(c0 + 2 * i + 1, 1)
                    gateup(c0 + 2 * i + 3, 1)
                    down(c0 + 2 * i + 2, 0)
                down(c0 + CH - 1, 1)

            def final():
                m = NORM['final']
                for k in range(KD):
                    pe.wait_ge(xf_ready, k + 1)
                    for t in range(TT):
                        last = nc.tensor.transpose(final_bank[k // 4][t][:, (k % 4) * P:(k % 4 + 1) * P],
                                                   xf[:, k, t * P:(t + 1) * P], ident[:])
                    if k % 4 == 3:
                        last.then_inc(final_t, 1)
                square_sums(m)

            def plain(mixer, what, i=0):
                u = UNIT[mixer, what, i // USES.get(what, 1)]
                pe.wait_ge(unit_in[u % RING], 16 * (u // RING) + 16)
                return ring[:, u % RING, :]

            def halves_of(mixer, what, i=0):
                u = UNIT[mixer, what, i]
                pe.wait_ge(unit_lo, SPLIT_BEFORE[u] + 1)
                return unit_hi_lo(u)

            def project(w, it, rows=P, step=None, ks=range(KD)):
                hi, lo = w
                for k in ks:
                    c = slice(k * (step or rows), k * (step or rows) + rows)
                    last = product3(GU[it % 2][0:rows, 0:SEQ], hi[:, c], lo[:, c], xh[:, k, :], xl[:, k, :],
                                    k == 0, k == KD - 1)
                return last

            def first_two(mixer, what):
                m = NORM[mixer]
                ws = [halves_of(mixer, what, b) for b in range(2)]
                for k in range(KD):
                    pe.wait_ge(x_lo, KD * m + k + 1)
                    for b in range(2):
                        last = project(ws[b], b, ks=[k])
                        if k == KD - 1:
                            last.then_inc(unit_used, 1)

            def by_token(w, k, c, n, start, stop):
                hi, lo = w
                for t in range(TT):
                    dst = bank[2 + t][:, 0:n]
                    tok = slice(t * P, (t + 1) * P)
                    nc.tensor.matmul(dst, xh[:, k, tok], hi[:, c:c + n], start=start, stop=False, skip_group_check=True)
                    nc.tensor.matmul(dst, xh[:, k, tok], lo[:, c:c + n], start=False, stop=False, skip_group_check=True)
                    last = nc.tensor.matmul(dst, xl[:, k, tok], hi[:, c:c + n], start=False, stop=stop, skip_group_check=True)
                return last

            def scores(g, q, k, more=None):
                if g >= 2:
                    pe.wait_ge(biased, 2 * (g - 1))
                for t in range(TT):
                    dst = bank[2 + g % 2][:, KEYS[t]]
                    nk = (t + 1) * P
                    last = nc.tensor.matmul(dst, q[:, t * P:(t + 1) * P], k[:, 0:nk], start=True, stop=more is None)
                    if more is not None:
                        last = nc.tensor.matmul(dst, more[0][:, t * P:(t + 1) * P], more[1][:, 0:nk], start=False, stop=True)
                return last.then_inc(scores_done, 1)

            def turn_probs(g):
                if g < HEADS:
                    pe.wait_ge(probs_ready, 2 * (g + 1))
                else:
                    pe.wait_ge(probs_ready, HEADS + g + 1)
                    pe.wait_ge(probs_0_ready, g - HEADS + 1)
                if g >= 2:
                    pe.wait_ge(probs_t_ready, g - 1)
                src = probs[slot_of(g)]
                for i in range(3):
                    last = nc.tensor.transpose(GU[g % 2][:, i * P:(i + 1) * P], src[:, i * P:(i + 1) * P], ident[:])
                last.then_inc(probs_t_done, 1)

            def weigh_values(g, dst, v, start=True, stop=True):
                pe.wait_ge(probs_t_ready, g + 1)
                src = probs_t[g % 2]
                nc.tensor.matmul(dst, v[0], src[:, 0:SEQ], start=start, stop=False, skip_group_check=True)
                return nc.tensor.matmul(dst[:, P:SEQ], v[1], src[:, SEQ:SEQ + P], start=False, stop=stop,
                                        skip_group_check=True).then_inc(heads_done, 1)

            def mix_out(mixer, i):
                hi, lo = halves_of(mixer, 'out', i)
                half, b = i // 4, i % 4
                pe.wait_ge(out_lo_ready, (KD if mixer == 'mix1' else 0) + i + 1)
                for j in range(KD):
                    c = slice(j * P, (j + 1) * P)
                    last = product3(acc(j), hi[:, c], lo[:, c], out_hi[half][:, b, :], out_lo[half][:, b, :],
                                    i == 0 and j % 2 == 0, False)
                    if i == KD - 1 and j < KD - 1:
                        last.then_inc(mix_done, 1)
                last.then_inc(unit_used, 1)

            def even_mixer(m):
                it = 0
                for what, i in even:
                    if what == 'b_t':
                        pe.wait_ge(tables_ready, 1)
                        for c, dst in enumerate((bank[6], bank[1])):
                            for b in range(UB):
                                last = nc.tensor.transpose(dst[:, b * P:(b + 1) * P],
                                                           b_blocks[:, c, PER * b:PER * (b + 1), :], ident[:])
                            last.then_inc(b_t_done, 1)
                    elif what == 'squares':
                        square_sums(m)
                    elif what == 'spread':
                        spread_rstd(m)
                    elif what in ('u', 'q', 'k'):
                        if (what, i) == ('u', 0):
                            first_two('mix0', 'u')
                        elif (what, i) != ('u', 1):
                            pe.wait_ge(proj_read, it - 1)
                            project(halves_of('mix0', what, i), it).then_inc(unit_used, 1)
                        it += 1
                    elif what == 'f':
                        pe.wait_ge(proj_read, it - 1)
                        project(halves_of('mix0', 'f'), it, rows=F_ROWS).then_inc(unit_used, 1)
                        it += 1
                    elif what == 'v':
                        w = halves_of('mix0', 'v', i)
                        for kk in range(2):
                            last = by_token(w, 2 * i + kk, kk * 512, 512, i + kk == 0, i == 3 and kk == 1)
                        last.then_inc(unit_used, 1)
                    elif what == 's5':
                        if i < SG:
                            if i == 0:
                                pe.wait_ge(proj_read, UB)
                                pe.wait_ge(b_t_ready, 2)
                            if i >= 2:
                                pe.wait_ge(bu_ready, i - 1)
                            r = slice(GC * (i % PER), GC * (i % PER + 1))
                            for c in range(2):
                                last = nc.tensor.matmul((bank[6], bank[0])[i % 2][:, c * SEQ:(c + 1) * SEQ],
                                                        b_t[r, c, i // PER, :], u_t[r, i // PER, :], start=True, stop=True)
                            last.then_inc(bu_done, 1)
                        j = i - 3
                        if j >= 0:
                            pe.wait_ge(state_re_ready, j + 1)
                            pe.wait_ge(state_im_ready, j + 1)
                            if j % PER == 0 and j >= 2 * PER:
                                pe.wait_ge(y_read, j // PER)
                            r = slice(GC * (j % PER), GC * (j % PER + 1))
                            for c in range(2):
                                last = nc.tensor.matmul(y_bank(j // PER)[r, 0:SEQ], c_d[:, c, j, :], states[j % 2][:, c, :],
                                                        start=(c == 0), stop=(c == 1))
                            last.then_inc(y_done, 1)
                    elif what == 'fox':
                        if i < HEADS:
                            if i == 0:
                                pe.wait_ge(proj_read, UB + 1 + 2 * PAIRS)
                                pe.wait_ge(v_ready, TT)
                                pe.wait_ge(fox_lhs_ready, 1)
                            pe.wait_ge(fox_rhs_ready, i // 2 + 1)
                            r = slice(DH * (i % 2), DH * (i % 2 + 1))
                            fr = slice(DH * (i % 2), DH * (i % 2) + 40)
                            scores(i, q_t[r, i // 2, :], k_t[r, i // 2, :], (fox_lhs[fr, :], fox_rhs[fr, i // 2 % 2, :]))
                        if 0 <= i - 2 < HEADS:
                            turn_probs(i - 2)
                        g = i - 3
                        if g >= 0:
                            if g % 2 == 0 and g:
                                pe.wait_ge(heads_out, g // 2)
                            if g == 0:
                                pe.wait_ge(rbc_ready, m + 1)
                            weigh_values(g, misc[DH * (g % 2):DH * (g % 2 + 1), 0:SEQ],
                                         [v_n[:, t, g * DH:(g + 1) * DH] for t in range(TT)])
                    elif what == 'out':
                        if i == 0:
                            pe.wait_ge(y_read, UB)
                            pe.wait_ge(bu_ready, SG)
                            pe.wait_ge(biased, 2 * HEADS)
                        mix_out('mix0', i)
                    elif what == 'glu':
                        hi, lo = halves_of('mix0', 'glu', i // 2)
                        if i == 0:
                            pe.wait_ge(heads_out, PAIRS)
                        if i >= 2:
                            pe.wait_ge(glu_tanh, i - 1)
                        for k in range(UB):
                            pe.wait_ge(gelu_lo_ready, k + 1)
                            c = slice((i % 2 * UB + k) * P, (i % 2 * UB + k + 1) * P)
                            last = product3(glu_bank[i % 2][:, 0:SEQ], hi[:, c], lo[:, c], out_hi[1][:, k, :], out_lo[1][:, k, :],
                                            k == 0, k == UB - 1)
                        last.then_inc(unit_used if i % 2 else glu_done, 1)

            def odd_mixer(m):
                it = 0

                def next_bank():
                    if it >= 2:
                        pe.wait_ge(proj_read, reads0 + it - 1)
                    return GU[it % 2]

                for what, i in odd:
                    if what == 't5':
                        pe.wait_ge(odd_in, 32)
                        nc.tensor.matmul(bank[6][0:HEADS, :], par[0:BUCKETS + 1, PARAMS['rel']], t5_onehot[0:BUCKETS + 1, :],
                                         start=True, stop=True).then_inc(t5_made, 1)
                    elif what == 'squares':
                        square_sums(m)
                    elif what == 'spread':
                        spread_rstd(m)
                    elif what in ('cq', 'ckv', 'nq', 'kv'):
                        if (what, i) == ('cq', 0):
                            first_two('mix1', 'cq')
                        elif (what, i) != ('cq', 1):
                            next_bank()
                            project(halves_of('mix1', what, i), it).then_inc(unit_used, 1)
                        it += 1
                    elif what == 'krg':
                        next_bank()
                        hi, lo = halves_of('mix1', 'krg')
                        project((hi, lo), it, step=2 * ROPE)
                        it += 1
                        pe.wait_ge(rbc_ready, m + 1)
                        for t in range(TT):
                            tok = slice(t * P, (t + 1) * P)
                            for k in range(KD):
                                c = slice(GATES_AT + 24 * k, GATES_AT + 24 * (k + 1))
                                last = product3(misc[:, 8 + 24 * t:32 + 24 * t], xh[:, k, tok], xl[:, k, tok], hi[:, c], lo[:, c],
                                                k == 0, k == KD - 1)
                        last.then_inc(unit_used, 1)
                    elif what == 'lat_squares':
                        pe.wait_ge(lat_squared, LB)
                        pe.wait_ge(logits_read, TT)
                        for c, chunks in enumerate((range(QB), range(QB, LB))):
                            for t in range(TT):
                                for k in chunks:
                                    last = nc.tensor.matmul(misc[:, 64 + 2 * c + t:65 + 2 * c + t], sq[:, k, t * P:(t + 1) * P],
                                                            ones[:, 0:1], start=(k == chunks[0]), stop=(k == chunks[-1]))
                        last.then_inc(lat_ss_done, 1)
                    elif what == 'sel':
                        pe.wait_ge(krope_ready, 1)
                        pe.wait_ge(t5_copied, 1)
                        nc.tensor.matmul(bank[6][DH:P, 0:SEQ], oc[DH:P, OC['sel']], kr[DH:P, :], start=True,
                                         stop=True).then_inc(krope_done, 1)
                    elif what == 'lat_spread':
                        pe.wait_ge(lat_diag_ready, 4)
                        pe.wait_ge(krope_copied, 1)
                        for t in range(4):
                            last = nc.tensor.matmul(bank[6][:, t * P:(t + 1) * P], ones[:], lat_diag[:, t, :], start=True, stop=True)
                        last.then_inc(lat_spread_done, 1)
                    elif what == 'vsw':
                        w = halves_of('mix1', 'vsw', i)
                        for kk in range(4):
                            last = by_token(w, 4 * i + kk, kk * 2 * P, 2 * P, i + kk == 0, i + kk == 4)
                        last.then_inc(unit_used, 1)
                    elif what == 'uq':
                        b = next_bank()
                        it += 1
                        if i == 0:
                            pe.wait_ge(lat_ready, LB)
                        w = plain('mix1', 'uq', i)
                        for k in range(QB):
                            c = (2 * k + i % 2) * P
                            last = nc.tensor.matmul(b[:, 0:SEQ], w[:, c:c + P], lat[:, k, :], start=(k == 0), stop=(k == QB - 1))
                        last.then_inc(unit_used if i % 2 else part_done, 1)
                    elif what == 'uk':
                        b = next_bank()
                        it += 1
                        w = plain('mix1', 'uk', i)
                        for k in range(KVB):
                            c = k * HEADS * DH + i * DH
                            last = nc.tensor.matmul(b[0:DH, 0:SEQ], w[:, c:c + DH], lat[:, QB + k, :], start=(k == 0),
                                                    stop=(k == KVB - 1))
                        last.then_inc(unit_used if i == HEADS - 1 else part_done, 1)
                    elif what == 'uv':
                        w = plain('mix1', 'uv')
                        pe.wait_ge(v_ready, v0 + TT)
                        for t in range(TT):
                            for k in range(KVB):
                                last = nc.tensor.matmul(bank[2 + t][:], lat[:, QB + k, t * P:(t + 1) * P],
                                                        w[:, k * 512:(k + 1) * 512], start=(k == 0), stop=(k == KVB - 1))
                        last.then_inc(unit_used, 1)
                    elif what == 'w1':
                        w = plain('mix1', 'w1', i)
                        pe.wait_ge(blocks_ready, 2)
                        c = i // 2
                        for k in range(CMP_PAIRS // 2):
                            kk = i % 2 * (CMP_PAIRS // 2) + k
                            last = nc.tensor.matmul(small_ps[:, 128 + 32 * c:128 + 32 * c + 2 * N_CMP], w[:, k * P:(k + 1) * P],
                                                    blk[:, c, kk].rearrange('p g n -> p (g n)'), start=(kk == 0),
                                                    stop=(kk == CMP_PAIRS - 1))
                        last.then_inc(unit_used, 1)
                    elif what == 'compress':
                        pe.wait_ge(hid_v_ready, 1)
                        w2 = par[:, PARAMS['w2']]
                        for g in range(GROUPS):
                            nc.tensor.matmul(small_ps[DH * g:DH * (g + 1), 192:192 + N_CMP], w2[:, 0:DH],
                                             hid[:, 0, g * N_CMP:(g + 1) * N_CMP], start=True, stop=True)
                        nc.tensor.matmul(small_ps[:, 256:256 + DH], hid_v, w2[:, DH:2 * DH], start=True, stop=True).then_inc(cmp_made, 1)
                    elif what == 'cmp_scores':
                        pe.wait_ge(kc_ready, 1)
                        pe.wait_ge(v_block_ready, 1)
                        for g in range(GROUPS):
                            rows = slice(DH * g, DH * (g + 1))
                            for t in range(TT):
                                for r in range(REP):
                                    c = (t * REP + r) * 16
                                    last = nc.tensor.matmul(cmp_scores_in[g][:, c:c + N_CMP], nq[rows, r, t * P:(t + 1) * P],
                                                            kc[rows, :], start=True, stop=True)
                        last.then_inc(cmp_scored, 1)
                    elif what == 'cmp_turn':
                        pe.wait_ge(cmp_ready, 1)
                        pe.wait_ge(v_block_ready, 1)
                        for t in range(TT):
                            last = nc.tensor.transpose(bank[1][:, t * P:(t + 1) * P], pc[:, t].rearrange('p h n -> p (h n)'), ident[:])
                        last.then_inc(cmp_turned, 1)
                    elif what == 'att':
                        if i < HEADS:
                            if i == 0:
                                pe.wait_ge(proj_read, reads0 + it)
                                pe.wait_ge(mla_v_ready, TT)
                            scores(heads0 + i, mq[:, i, :], mk[:, i, :])
                        elif i < ODD_HEADS:
                            r, g, w = nsa(i - HEADS)
                            rows = slice(DH * g, DH * (g + 1))
                            scores(heads0 + i, nq[rows, r, :], ksw[rows, w, :])
                        if 0 <= i - 3 < ODD_HEADS:
                            turn_probs(heads0 + i - 3)
                        j = i - 4
                        if 0 <= j < HEADS:
                            if j % 2 == 0:
                                pe.wait_ge(heads_out, out0 + j // 2 - 1)
                            weigh_values(heads0 + j, o_bank(j // 2)[DH * (j % 2):DH * (j % 2 + 1), 0:SEQ],
                                         [mv[:, t, j * DH:(j + 1) * DH] for t in range(TT)])
                        elif j >= 0:
                            r, g, w = nsa(j - HEADS)
                            if g + w == 0:
                                pe.wait_ge(heads_out, out0 + PAIRS + r - 1)
                            dst = o_bank(r)[DH * g:DH * (g + 1), 0:SEQ]
                            weigh_values(heads0 + j, dst, [vsw[:, t, (2 * w + g) * DH:(2 * w + g + 1) * DH] for t in range(TT)],
                                         start=(w == 0), stop=False)
                            if w:
                                pe.wait_ge(pc_t_ready, 1)
                                nc.tensor.matmul(dst, v_block[:, g * REP + r, :], pc_t, start=False, stop=True,
                                                 skip_group_check=True).then_inc(cmp_weighed, 1)
                    elif what == 'out':
                        mix_out('mix1', i)

            pe.wait_ge(consts_set, 3)
            for _ in range(WARM_UP):
                nc.tensor.matmul(bank[6][:, 0:P], ones[:], ones[:], start=True, stop=True)
            pe.wait_ge(ident_loaded, 16)
            n = 0
            for p in PHASES:
                if p.startswith('ffn'):
                    ffn(n)
                    n += 1
                elif p == 'mix0':
                    even_mixer(NORM[p])
                elif p == 'mix1':
                    odd_mixer(NORM[p])
                elif p == 'final':
                    final()

        @block.scalar
        def _(act):
            def split_gu(c, s, c_half, half):
                act.wait_ge(raw_gu_in[s], 16 * c_half + 16)
                if not (isinstance(c, int) and c < 2):
                    act.wait_ge(gateup_done, c - 1)
                w = slice(half * D, (half + 1) * D)
                nc.scalar.copy(hi_gu[:, s, w], raw_gu[:, s, w]).then_inc(gu_hi, 1)

            def split_d(c, s, c_half):
                act.wait_ge(raw_d_in[s], 16 * c_half + 16)
                if not (isinstance(c, int) and c < 2):
                    act.wait_ge(down_done, KD * (c - 1))
                if isinstance(c, int) and c in (CH, 3 * CH):
                    act.wait_ge(unit_used, ORDER['mix0' if c == CH else 'mix1', 'end'])
                nc.scalar.copy(hi_d[:, s, :], raw_d[:, s, :]).then_inc(d_hi, 1)

            def split_unit(u):
                act.wait_ge(unit_in[u % RING], 16 * (u // RING) + 16)
                if SLOT_FREE[u] is not None:
                    act.wait_ge(unit_used, SLOT_FREE[u] + 1)
                nc.scalar.copy(unit_hi_lo(u)[0], ring[:, u % RING, :]).then_inc(unit_hi, 1)

            def next_gate_up(n):
                mixer = PHASES[NORM[f'ffn{n}'] - 1]
                act.wait_ge(unit_used, ORDER[mixer, 'end'] - 4)
                for half in range(2):
                    split_gu(CH * n, 0, CH * n // 2, half)

            def step(c, s, c_half, more_gu=True, more_d=True, units=()):
                act.wait_ge(gate_scaled, c + 1)
                nc.scalar.activation(th[:, s, :], gs[:, s, 0, :], ACT.Tanh, scale=0.5).then_inc(tanh_done, 1)
                act.wait_ge(prod_ready, c + 1)
                nc.scalar.copy(ph[:, s, :], prod[:, s, :]).then_inc(ph_ready, 1)
                if more_gu:
                    split_gu(c + 2, s, c_half + 1, 0)
                if more_d:
                    split_d(c + 1, 1 - s, c_half + s)
                if more_gu:
                    split_gu(c + 2, s, c_half + 1, 1)
                for u in units:
                    if s == 1:
                        act.wait_ge(gateup_done, c + 1)
                    split_unit(u)

            def h_wait(m, k):
                if m == 0:
                    act.wait_ge(x_in[2 * k // KD], 16)
                else:
                    act.wait_ge(h_ready, KD * m + k + 1 - KD)

            def square(k):
                nc.scalar.activation(sq[:, k, :], h[:, k, :], ACT.Square).then_inc(even_squared, 1)

            def norm_inputs(p):
                m = NORM[p]
                if m == 1:
                    act.wait_ge(tables_ready, 1)
                for k in range(KD):
                    h_wait(m, k)
                    g = gain[:, m, k:k + 1]
                    if p != 'final':
                        nc.scalar.activation(xh[:, k, :], h[:, k, :], ACT.Copy, scale=g).then_inc(x_hi, 1)
                    else:
                        nc.scalar.activation(xf[:, k, :], h[:, k, :], ACT.Copy, scale=g).then_inc(xf_ready, 1)
                    if k % 2 == 0 and m > 0:
                        square(k)

            def exp_scores(g):
                for t in range(TT):
                    act.wait_ge(biased, 2 * g + t + 1)
                    nc.scalar.activation(probs[slot_of(g)][:, KEYS[t]], probs[slot_of(g)][:, KEYS[t]], ACT.Exp,
                                         scale=-1.0, bias=stats[:, slot_of(g), 0, t:t + 1], accum_out=stats[:, slot_of(g), 1, t:t + 1]).then_inc(exp_done, 1)

            def copy_probs_t(g):
                act.wait_ge(probs_t_done, g + 1)
                if g >= 2:
                    act.wait_ge(heads_done, g - 1)
                nc.scalar.copy(probs_t[g % 2], GU[g % 2][:, 0:ATT_COLS]).then_inc(probs_t_ready, 1)

            def even_mixer(m):
                for what, i in even:
                    if what == 'split_hi':
                        split_unit(i)
                    elif what == 'next_gate_up':
                        next_gate_up(1)
                    elif what == 'gelu_split':
                        for b in range(UB):
                            act.wait_ge(gelu_ready, b + 1)
                            nc.scalar.copy(out_hi[1][:, b, :], u_t[:, b, :]).then_inc(gelu_hi_ready, 1)
                    elif what == 'out' and i == 3:
                        act.wait_ge(unit_used, used('mix0', 'glu', 3))
                        for b in range(UB):
                            act.wait_ge(s5_ready, b + 1)
                            nc.scalar.copy(out_hi[1][:, b, :], s5_out[:, b, :]).then_inc(out_hi_ready, 1)
                    elif what == 'b_t':
                        for c, src in enumerate((bank[6], bank[1])):
                            act.wait_ge(b_t_done, c + 1)
                            nc.scalar.copy(b_t[:, c, :, :], src[:].rearrange('p (b n) -> p b n', b=UB)).then_inc(b_t_ready, 1)
                    elif what == 'f':
                        act.wait_ge(f_neg, 1)
                        nc.scalar.activation(fox_rhs[0:F_ROWS, 1, :], fox_rhs[0:F_ROWS, 0, :], ACT.Exp).then_inc(f_exp, 1)
                        act.wait_ge(f_exp, 1)
                        nc.scalar.activation(fox_rhs[0:F_ROWS, 0, :], fox_rhs[0:F_ROWS, 1, :], ACT.Ln, bias=1.0).then_inc(f_ln, 1)
                    elif what == 'v' and i == 3:
                        act.wait_ge(unit_used, used('mix0', 'v', 3))
                        act.wait_ge(rstd_ready, m + 1)
                        for t in range(TT):
                            nc.scalar.activation(v_n[:, t, :], bank[2 + t][:], ACT.Copy, scale=rstd[:, t:t + 1]).then_inc(v_ready, 1)
                    elif what == 's5' and i < SG:
                        act.wait_ge(bu_done, i + 1)
                        if i >= 2:
                            act.wait_ge(cos_out_ready, i - 1)
                            act.wait_ge(sin_out_ready, i - 1)
                        nc.scalar.copy(bu[i % 2], (bank[6], bank[0])[i % 2][:].rearrange('p (c t) -> p c t', c=2)).then_inc(bu_ready, 1)
                    elif what == 'fox':
                        if i < HEADS:
                            exp_scores(i)
                        g = i - 1
                        if 0 <= g < HEADS:
                            act.wait_ge(factor, g + 1)
                            for t in range(TT):
                                nc.scalar.activation(probs[slot_of(g)][:, KEYS[t]], probs[slot_of(g)][:, KEYS[t]], ACT.Copy,
                                                     scale=stats[:, slot_of(g), 2, t:t + 1]).then_inc(probs_ready, 1)
                        if 0 <= i - 2 < HEADS:
                            copy_probs_t(i - 2)
                        if i - 3 >= 0 and (i - 3) % 2:
                            act.wait_ge(heads_done, i - 2)
                            b = (i - 3) // 2
                            nc.scalar.copy(q_t[:, b, :], misc[:, 0:SEQ]).then_inc(heads_out, 1)
                            act.wait_ge(heads_out, b + 1)
                            nc.scalar.copy(out_hi[0][:, b, :], q_t[:, b, :]).then_inc(out_hi_ready, 1)
                    elif what == 'gelu_square':
                        act.wait_ge(y_read, i + 1)
                        nc.scalar.activation(states_tanh[:, i, :], u_t[:, i, :], ACT.Square, scale=0.044715 ** 0.5).then_inc(y_square, 1)
                    elif what == 'gelu_tanh':
                        act.wait_ge(y_inner, i + 1)
                        nc.scalar.activation(states_tanh[:, i, :], states_tanh[:, i, :], ACT.Tanh, scale=0.7978845608028654).then_inc(gelu_tanh, 1)
                    elif what == 'glu':
                        if i % 2:
                            act.wait_ge(unit_used, used('mix0', 'glu', i))
                        else:
                            act.wait_ge(glu_done, i // 2 + 1)
                        nc.scalar.activation(k_t[:, i, :], glu_bank[i % 2][:, 0:SEQ], ACT.Tanh, scale=0.25,
                                             bias=half_b[:, i:i + 1]).then_inc(glu_tanh, 1)

            def odd_mixer(m):
                def head_pair_out(b, dst):
                    nc.scalar.copy(dst, o_bank(b)[:, 0:SEQ]).then_inc(heads_out, 1)
                    act.wait_ge(heads_out, out0 + b + 1)
                    nc.scalar.copy(out_hi[b // 4][:, b % 4, :], dst).then_inc(out_hi_ready, 1)

                for what, i in odd:
                    if what == 'split_hi':
                        split_unit(i)
                    elif what == 'next_gate_up':
                        next_gate_up(3)
                    elif what == 't5':
                        act.wait_ge(t5_made, 1)
                        nc.scalar.mul(t5_row[0:HEADS, :], bank[6][0:HEADS, :], 8.0).then_inc(t5_copied, 1)
                    elif what == 'krg':
                        act.wait_ge(logits_read, TT)
                        nc.scalar.activation(gates, logits, ACT.Tanh, scale=0.5).then_inc(gate_tanh, 1)
                    elif what == 'sel':
                        act.wait_ge(krope_done, 1)
                        nc.scalar.copy(mk[DH:P, :, :], bank[6][DH:P, 0:SEQ].unsqueeze(1).broadcast_to([DH, HEADS, SEQ])
                                       ).then_inc(krope_copied, 1)
                    elif what == 'vsw' and i == 1:
                        act.wait_ge(unit_used, used('mix1', 'vsw', 1))
                        act.wait_ge(rstd_ready, m + 1)
                        for t in range(TT):
                            nc.scalar.activation(vsw[:, t, :], bank[2 + t][:, 0:2 * P], ACT.Copy, scale=rstd[:, t:t + 1]).then_inc(v_ready, 1)
                    elif what == 'uv':
                        act.wait_ge(unit_used, used('mix1', 'uv'))
                        act.wait_ge(t5_stored, 16)
                        for t in range(TT):
                            nc.scalar.copy(mv[:, t, :], bank[2 + t][:]).then_inc(mla_v_ready, 1)
                    elif what == 'hidden':
                        act.wait_ge(hid_inner, 1)
                        nc.scalar.activation(hid_t, hid_t, ACT.Tanh, scale=0.7978845608028654).then_inc(hid_tanh, 1)
                    elif what == 'cmp_softmax':
                        act.wait_ge(cmp_step, 5)
                        flat = pc.rearrange('p t h n -> p (t h n)')
                        nc.scalar.activation(flat, flat, ACT.Exp, scale=DH ** -0.5).then_inc(cmp_exp, 1)
                    elif what == 'cmp_turn':
                        act.wait_ge(cmp_turned, 1)
                        nc.scalar.copy(pc_t, bank[1][:, 0:SEQ]).then_inc(pc_t_ready, 1)
                    elif what == 'att':
                        if 0 <= i - 3 < ODD_HEADS:
                            copy_probs_t(heads0 + i - 3)
                        if i < ODD_HEADS:
                            exp_scores(heads0 + i)
                        j = i - 4
                        if 0 <= j < HEADS and j % 2:
                            act.wait_ge(heads_done, heads0 + j + 1)
                            head_pair_out(j // 2, mq[:, j // 2, :])
                        elif j >= HEADS and nsa(j - HEADS)[1:] == (1, 1):
                            r = nsa(j - HEADS)[0]
                            act.wait_ge(cmp_weighed, 2 * (r + 1))
                            head_pair_out(PAIRS + r, nq[:, r, :])

            act.wait_ge(consts_set, 3)
            nc.scalar.activation(th[:, 0, 0:1], halves[:, 0:1], ACT.Tanh).then_inc(functions_in, 1)
            act.wait_ge(functions_in, 1)
            act.wait_ge(params_in, 16)
            n = 0
            for p in PHASES:
                norm_inputs(p)
                if p == 'mix0':
                    even_mixer(NORM[p])
                if p == 'mix1':
                    odd_mixer(NORM[p])
                if p.startswith('ffn'):
                    if n == 0:
                        act.wait_ge(first_gate_in, 16)
                        nc.scalar.copy(hi_gu[:, 0, 0:D // 2], raw_gu[:, 0, 0:D // 2]).then_inc(first_hi, 1)
                        nc.scalar.copy(hi_gu[:, 0, D // 2:D], raw_gu[:, 0, D // 2:D]).then_inc(gu_hi, 1)
                        split_gu(0, 0, 0, 1)
                        for k in range(0, KD, 2):
                            square(k)
                        split_gu(1, 1, 0, 0)
                        split_gu(1, 1, 0, 1)
                        split_d(0, 0, 0)
                    elif n != 2:
                        c = CH * n
                        for half in range(2):
                            split_gu(c + 1, 1, c // 2, half)
                        split_d(c, 0, c // 2)
                    pairs(act, step, n)
                    n += 1
                if p == 'final':
                    act.wait_ge(rstd_ready, NORM[p] + 1)
                    for i in range(2):
                        act.wait_ge(final_t, i + 1)
                        nc.scalar.activation(o_sb[:, 1, i * 512:(i + 1) * 512], final_bank[i][1][:], ACT.Copy,
                                             scale=rstd[:, 1:2]).then_inc(scaled_act, 1)

        @block.vector
        def _(dve):
            def x_rest(m, k):
                dve.wait_ge(x_hi, KD * m + k + 1)
                nc.vector.scalar_tensor_tensor(xl[:, k, :], h[:, k, :], gain[:, m, k:k + 1], xh[:, k, :].bitcast(F32), ALU.mult,
                                               ALU.subtract).then_inc(x_lo, 1)

            def rms(m, meanwhile=lambda: None, then=lambda: None):
                dve.wait_ge(ss_done, m + 1)
                nc.vector.tensor_scalar(ms[:], misc[:, 0:TT], 1.0 / D, EPS, ALU.mult, ALU.add).then_inc(ms_ready, 1)
                meanwhile()
                dve.wait_ge(rstd_ready, m + 1)
                for t in range(TT):
                    nc.vector.tensor_scalar(diag[:, t, :], ident[:], rstd[:, t:t + 1], None,
                                            ALU.mult).then_inc(diag_ready, 1)
                then()
                dve.wait_ge(rbc_done, m + 1)
                nc.vector.tensor_copy(rbc[:], misc[:, SEQ:2 * SEQ]).then_inc(rbc_ready, 1)
                dve.wait_ge(rbc_ready, m + 1)

            def split_gu(c, s, half):
                dve.wait_ge(gu_hi, 2 * c + half + 1)
                w = slice(half * D, (half + 1) * D)
                nc.vector.tensor_tensor(lo_gu[:, s, w], raw_gu[:, s, w], hi_gu[:, s, w].bitcast(F32),
                                        ALU.subtract).then_inc(gu_lo, 1)

            def split_d(c, s):
                dve.wait_ge(d_hi, c + 1)
                nc.vector.tensor_tensor(lo_d[:, s, :], raw_d[:, s, :], hi_d[:, s, :].bitcast(F32),
                                        ALU.subtract).then_inc(d_lo, 1)

            def split_unit(u):
                dve.wait_ge(unit_hi, SPLIT_BEFORE[u] + 1)
                hi, lo = unit_hi_lo(u)
                nc.vector.tensor_tensor(lo, ring[:, u % RING, :], hi.bitcast(F32), ALU.subtract).then_inc(unit_lo, 1)

            def out_rest(mixer, i, src):
                dve.wait_ge(out_hi_ready, (KD if mixer == 'mix1' else 0) + i + 1)
                nc.vector.tensor_tensor(out_lo[i // 4][:, i % 4, :], src, out_hi[i // 4][:, i % 4, :].bitcast(F32),
                                        ALU.subtract).then_inc(out_lo_ready, 1)

            def step(c, s, c_half, more_gu=True, more_d=True, units=()):
                dve.wait_ge(gateup_done, c + 1)
                nc.vector.tensor_tensor(gs[:, s, :, :], GU[s][:].rearrange('p (a t) -> p a t', a=2),
                                        rbc[:].unsqueeze(1).broadcast_to([P, 2, SEQ]), ALU.mult).then_inc(gate_scaled, 1)
                dve.wait_ge(tanh_done, c + 1)
                nc.vector.scalar_tensor_tensor(ga[:, s, :], th[:, s, :], 1.0, gs[:, s, 0, :], ALU.add,
                                               ALU.mult).then_inc(a_ready, 1)
                dve.wait_ge(a_ready, c + 1)
                nc.vector.tensor_tensor(prod[:, s, :], ga[:, s, :], gs[:, s, 1, :], ALU.mult).then_inc(prod_ready, 1)
                dve.wait_ge(ph_ready, c + 1)
                nc.vector.tensor_tensor(pl[:, s, :], prod[:, s, :], ph[:, s, :].bitcast(F32),
                                        ALU.subtract).then_inc(act_lo, 1)
                if more_gu:
                    split_gu(c + 2, s, 0)
                if more_d:
                    split_d(c + 1, 1 - s)
                if more_gu:
                    split_gu(c + 2, s, 1)
                for u in units:
                    split_unit(u)

            def stat_rows(g, bias, scale):
                dve.wait_ge(scores_done, g + 1)
                if g >= 3:
                    dve.wait_ge(probs_t_done, g - (2 if g < HEADS else 3))
                for t in range(TT):
                    nc.vector.tensor_tensor_reduce(probs[slot_of(g)][:, KEYS[t]], bank[2 + g % 2][:, KEYS[t]], bias[t], -scale, 3e38,
                                                   ALU.add, ALU.min, stats[:, slot_of(g), 0, t:t + 1]).then_inc(biased, 1)

            def normalise(g, gate=None):
                dve.wait_ge(exp_done, 2 * (g + 1))
                nc.vector.reciprocal(stats[:, slot_of(g), 2, :], stats[:, slot_of(g), 1, :]).then_inc(factor, 1)
                dve.wait_ge(factor, g + 1)
                if gate is not None:
                    dve.wait_ge(gates_ready, 1)
                    nc.vector.tensor_tensor(stats[:, slot_of(g), 2, :], stats[:, slot_of(g), 2, :], gate, ALU.mult).then_inc(gated, 1)
                    dve.wait_ge(gated, g + 1 - heads0 - HEADS)
                nc.vector.tensor_scalar(probs[slot_of(g)][:, KEYS[1]], probs[slot_of(g)][:, KEYS[1]], stats[:, slot_of(g), 2, 1:2], None,
                                        ALU.mult).then_inc(probs_ready, 1)

            def even_mixer(m):
                it = 0
                for what, i in even:
                    if what == 'split_lo':
                        split_unit(i)
                    elif what == 'next_gate_up':
                        for half in range(2):
                            split_gu(CH, 0, half)
                    elif what == 'out' and i == 2:
                        out_rest('mix0', PAIRS - 1, q_t[:, PAIRS - 1, :])
                    elif what == 'gelu_split':
                        for b in range(UB):
                            dve.wait_ge(gelu_hi_ready, b + 1)
                            nc.vector.tensor_tensor(out_lo[1][:, b, :], u_t[:, b, :], out_hi[1][:, b, :].bitcast(F32),
                                                    ALU.subtract).then_inc(gelu_lo_ready, 1)
                    elif what == 'out' and i == 3:
                        for b in range(UB):
                            out_rest('mix0', 4 + b, s5_out[:, b, :])
                    elif what == 'spread':
                        rms(m)
                        for b in range(2):
                            dve.wait_ge(unit_used, used('mix0', 'u', b))
                            nc.vector.tensor_tensor(u_t[:, b, :], GU[b % 2][:, 0:SEQ], rbc[:], ALU.mult).then_inc(proj_read, 1)
                        it = 2
                    elif what in ('u', 'q', 'k'):
                        if what == 'u' and i < 2:
                            continue
                        dve.wait_ge(unit_used, used('mix0', what, i))
                        dst = {'u': u_t, 'q': q_t, 'k': k_t}[what][:, i, :]
                        nc.vector.tensor_tensor(dst, GU[it % 2][:, 0:SEQ], rbc[:], ALU.mult).then_inc(proj_read, 1)
                        it += 1
                    elif what == 'f':
                        dve.wait_ge(unit_used, used('mix0', 'f'))
                        rows = slice(0, F_ROWS)
                        nc.vector.tensor_tensor(fox_lhs[rows, :], GU[it % 2][rows, 0:SEQ], rbc[rows, :], ALU.mult).then_inc(proj_read, 1)
                        it += 1
                        dve.wait_ge(proj_read, it)
                        nc.vector.tensor_scalar(fox_lhs[rows, :], fox_lhs[rows, :], par[rows, PARAMS['b_f']], None, ALU.add).then_inc(f_x, 1)
                        dve.wait_ge(f_x, 1)
                        nc.vector.scalar_tensor_tensor(fox_rhs[rows, 0, :], fox_lhs[rows, :], -1.0, fox_lhs[rows, :], ALU.mult,
                                                       ALU.min).then_inc(f_neg, 1)
                    elif what == 'f_end':
                        dve.wait_ge(f_ln, 1)
                        nc.vector.scalar_tensor_tensor(fox_rhs[rows, 1, :], fox_lhs[rows, :], 0.0, fox_rhs[rows, 0, :], ALU.min,
                                                       ALU.subtract).then_inc(f_log, 1)
                        dve.wait_ge(f_log, 1)
                        nc.vector.tensor_tensor_scan(cum[rows, :], ones[rows, 0:1].broadcast_to([F_ROWS, SEQ]), fox_rhs[rows, 1, :],
                                                     0.0, ALU.mult, ALU.add).then_inc(cum_ready, 1)
                    elif what == 's5':
                        cos2 = [cos_t[:, j, :].unsqueeze(1).broadcast_to([P, 2, SEQ]) for j in range(SG)]
                        j = i - 1
                        if 0 <= j < SG:
                            dve.wait_ge(sin_in_ready, j + 1)
                            dve.wait_ge(cos_in_ready, j + 1)
                            nc.vector.tensor_tensor(cos_in[:, 0, :], cos_in[:, 0, :], sin_in[:, 1, :], ALU.add).then_inc(zin_ready, 1)
                            nc.vector.tensor_tensor(cos_in[:, 1, :], cos_in[:, 1, :], sin_in[:, 0, :], ALU.subtract).then_inc(zin_ready, 1)
                            mag = small[:, MAG, j:j + 1].broadcast_to([P, SEQ])
                            for c in range(2):
                                dve.wait_ge(zin_ready, 2 * j + c + 1)
                                nc.vector.tensor_tensor_scan(bu[j % 2][:, c, :], mag, cos_in[:, c, :], 0.0, ALU.mult,
                                                             ALU.add).then_inc(scanned, 1)
                        e = i - 2
                        if 0 <= e < SG:
                            dve.wait_ge(sin_out_ready, e + 1)
                            dve.wait_ge(cos_out_ready, e + 1)
                            nc.vector.tensor_tensor(states[e % 2][:, 0, :], states[e % 2][:, 0, :], sin_out[:, 1, :],
                                                    ALU.subtract).then_inc(state_re_ready, 1)
                        if i < SG:
                            dve.wait_ge(bu_ready, i + 1)
                            if i >= 1:
                                dve.wait_ge(scanned, 2 * i)
                            nc.vector.tensor_tensor(cos_in, bu[i % 2], cos2[i], ALU.mult).then_inc(cos_in_ready, 1)
                        if 0 <= j < SG:
                            if j >= 2:
                                dve.wait_ge(y_done, j - 1)
                            dve.wait_ge(scanned, 2 * (j + 1))
                            nc.vector.tensor_tensor(states[j % 2], bu[j % 2], cos2[j], ALU.mult).then_inc(cos_out_ready, 1)
                    elif what == 'gelu':
                        dve.wait_ge(y_done, PER * (i + 1))
                        nc.vector.scalar_tensor_tensor(u_t[:, i, :], u_t[:, i, :], par[:, PARAMS['d_skip']][:, i:i + 1],
                                                       y_bank(i)[:, 0:SEQ], ALU.mult, ALU.add).then_inc(y_read, 1)
                        if 1 <= i < UB - 1:
                            gelu_end(i - 1)
                    elif what == 'gelu_inner':
                        dve.wait_ge(y_square, i + 1)
                        nc.vector.scalar_tensor_tensor(states_tanh[:, i, :], states_tanh[:, i, :], 1.0, u_t[:, i, :], ALU.add,
                                                       ALU.mult).then_inc(y_inner, 1)
                    elif what == 'gelu_end':
                        gelu_end(i)
                    elif what == 'fox':
                        if i < HEADS:
                            stat_rows(i, [causal[:, KEYS[t]] for t in range(TT)], DH ** -0.5)
                        if 0 <= i - 1 < HEADS:
                            g = i - 1
                            dve.wait_ge(exp_done, 2 * (g + 1))
                            nc.vector.reciprocal(stats[:, slot_of(g), 2, :], stats[:, slot_of(g), 1, :]).then_inc(factor, 1)
                        if i - 4 >= 0 and i % 2 == 1:
                            out_rest('mix0', (i - 5) // 2, q_t[:, (i - 5) // 2, :])
                    elif what == 'glu':
                        dve.wait_ge(glu_tanh, i + 1)
                        dve.wait_ge(quarter_ready, UB)
                        nc.vector.scalar_tensor_tensor(s5_out[:, i, :], k_t[:, i, :], 1.0, quarter[:, i, :], ALU.add,
                                                       ALU.mult).then_inc(s5_ready, 1)

            def odd_mixer(m):
                it = 0

                def scaled(dst, n, rows=slice(0, P), by=None):
                    dve.wait_ge(unit_used, n)
                    return nc.vector.tensor_tensor(dst, GU[it % 2][rows, 0:SEQ], (rbc if by is None else by)[rows, :],
                                                   ALU.mult).then_inc(proj_read, 1)

                for what, i in odd:
                    key = ('mix1', what, i)
                    n = UNIT.get(key, 0) + 1
                    if what == 'split_lo':
                        split_unit(i)
                    elif what == 'next_gate_up':
                        for half in range(2):
                            split_gu(3 * CH, 0, half)
                    elif what == 'out' and i == 0:
                        out_rest('mix1', KD - 1, nq[:, REP - 1, :])
                    elif what == 'spread':
                        rms(m)
                        for j in range(2):
                            scaled(lat[:, j, :], used('mix1', 'cq', j))
                            it += 1
                    elif what == 'cq' and i < 2:
                        continue
                    elif what in ('cq', 'ckv'):
                        scaled(lat[:, i + (QB if what == 'ckv' else 0), :], n)
                        it += 1
                    elif what == 'nq':
                        scaled(nq[:, i, :], n)
                        it += 1
                    elif what == 'kv':
                        scaled(kv_raw[:, i, :] if i < 2 else ksw[:, i - 2, :], n)
                        it += 1
                    elif what == 'krg':
                        rows = slice(DH, P)
                        scaled(kr[rows, :], n, rows)
                        it += 1
                        dve.wait_ge(proj_read, reads0 + it)
                        nc.vector.tensor_tensor(kr[rows, :], kr[rows, :], rope[rows, :], ALU.mult).then_inc(krope_ready, 1)
                        for t in range(TT):
                            nc.vector.scalar_tensor_tensor(logits[:, t, :], misc[:, 8 + 24 * t:32 + 24 * t], rstd[:, t:t + 1],
                                                           par[:, PARAMS['b_gate']], ALU.mult, ALU.add).then_inc(logits_read, 1)
                        dve.wait_ge(gate_tanh, 1)
                        nc.vector.tensor_scalar(gates, gates, 0.5, 0.5, ALU.mult, ALU.add).then_inc(gates_ready, 1)
                    elif what == 'lat_squares':
                        dve.wait_ge(lat_ss_done, 1)
                        nc.vector.tensor_scalar(lat_ms[:, 0:2], misc[:, 64:66], 1.0 / Q_RANK, EPS, ALU.mult, ALU.add).then_inc(lat_ms_ready, 1)
                        nc.vector.tensor_scalar(lat_ms[:, 2:4], misc[:, 66:68], 1.0 / KV_RANK, EPS, ALU.mult, ALU.add).then_inc(lat_ms_ready, 1)
                        dve.wait_ge(lat_rstd_ready, 1)
                        for t in range(4):
                            nc.vector.tensor_scalar(lat_diag[:, t, :], ident[:], lat_rstd[:, t:t + 1], None,
                                                    ALU.mult).then_inc(lat_diag_ready, 1)
                    elif what == 'lat_spread':
                        dve.wait_ge(lat_spread_done, 1)
                        for k in range(LB):
                            c = 0 if k < QB else 1
                            g_ = par[:, PARAMS['q_norm']][:, k:k + 1] if k < QB else par[:, PARAMS['kv_norm']][:, k - QB:k - QB + 1]
                            nc.vector.scalar_tensor_tensor(lat[:, k, :], lat[:, k, :], g_, bank[6][:, c * SEQ:(c + 1) * SEQ], ALU.mult,
                                                           ALU.mult).then_inc(lat_ready, 1)
                    elif what == 'uq':
                        dve.wait_ge(*((unit_used, used('mix1', 'uq', i)) if i % 2 else (part_done, i // 2 + 1)))
                        nc.vector.tensor_tensor(mq[:, i, :], GU[it % 2][:, 0:SEQ], rope, ALU.mult).then_inc(proj_read, 1)
                        it += 1
                    elif what == 'uk':
                        dve.wait_ge(*((unit_used, used('mix1', 'uk')) if i == HEADS - 1 else (part_done, HEADS // 2 + i + 1)))
                        nc.vector.tensor_copy(mk[0:DH, i, :], GU[it % 2][0:DH, 0:SEQ]).then_inc(proj_read, 1)
                        it += 1
                        if i == 0:
                            dve.wait_ge(windows_in, 64)
                            for c in range(2):
                                shape = [P, CMP_PAIRS, N_CMP]
                                for g in range(GROUPS):
                                    w_ap = win[:, c, g, :]
                                    src = bass.AP(w_ap.tensor, w_ap.offset, [w_ap.ap[0], (2, CMP_PAIRS), (CMP_STRIDE, N_CMP)])
                                    pe_ = par[:, PARAMS['pe']][:, c * CMP_PAIRS:(c + 1) * CMP_PAIRS].unsqueeze(2).broadcast_to(shape)
                                    ins = nc.vector.tensor_tensor(blk[:, c, :, g, :], src, pe_, ALU.add)
                                ins.then_inc(blocks_ready, 1)
                    elif what == 'hidden':
                        dve.wait_ge(unit_used, used('mix1', 'w1', 3))
                        nc.vector.tensor_copy(hid, small_ps[:, 128:192].rearrange('p (a n) -> p a n', a=2)[:, :, 0:2 * N_CMP]
                                              ).then_inc(hid_read, 1)
                    elif what == 'compress':
                        dve.wait_ge(hid_tanh, 1)
                        nc.vector.scalar_tensor_tensor(hid, hid_t, 1.0, hid, ALU.add, ALU.mult).then_inc(hid_ready, 1)
                        nc.vector.memset(hid_v, 0.0).then_inc(hid_ready, 1)
                        dve.wait_ge(hid_ready, 2)
                        nc.vector.tensor_copy(hid_v.rearrange('p (g r n) -> p g r n', g=GROUPS, r=REP)[:, :, :, 0:N_CMP],
                                              hid[:, 1, :].rearrange('p (g n) -> p g n', g=GROUPS).unsqueeze(2).broadcast_to(
                                                  [P, GROUPS, REP, N_CMP])).then_inc(hid_v_ready, 1)
                        dve.wait_ge(cmp_made, 1)
                        nc.vector.tensor_scalar(kc, small_ps[:, 192:192 + N_CMP], 0.5, None, ALU.mult).then_inc(kc_ready, 1)
                        nc.vector.tensor_tensor(v_block, small_ps[:, 256:256 + DH].unsqueeze(1).broadcast_to([P, HEADS, DH]),
                                                oc[:, OC['block']].unsqueeze(2).broadcast_to([P, HEADS, DH]), ALU.mult
                                                ).then_inc(v_block_ready, 1)
                    elif what == 'cmp_softmax':
                        dve.wait_ge(cmp_scored, 1)
                        dve.wait_ge(t5_in, 16)
                        nc.vector.memset(s5z[:, 512:768], 0.0).then_inc(cmp_step, 1)
                        dve.wait_ge(cmp_step, 1)
                        for g in range(GROUPS):
                            sc = cmp_scores_in[g].rearrange('p (t r n) -> p t r n', t=TT, r=REP)
                            for t in range(TT):
                                first = CMP_LEN - 1 + (P if t == 0 else 0)
                                bias = t5[:, g * REP:(g + 1) * REP, first:first + CMP_STRIDE * (N_CMP - 1) + 1:CMP_STRIDE]
                                last = nc.vector.tensor_tensor(pc[:, t, g * REP:(g + 1) * REP, 0:N_CMP], sc[:, t, :, 0:N_CMP],
                                                               bias, ALU.add)
                            last.then_inc(cmp_step, 1)
                        dve.wait_ge(cmp_step, 3)
                        th_ = pc.rearrange('p t h n -> p (t h) n')[:, :, 0:N_CMP]
                        flat_max, flat_sum = c_max.rearrange('p t h -> p (t h)'), c_sum.rearrange('p t h -> p (t h)')
                        wide = [P, TT * HEADS, N_CMP]
                        nc.vector.tensor_reduce(flat_max, th_, AX.X, ALU.max).then_inc(cmp_step, 1)
                        dve.wait_ge(cmp_step, 4)
                        nc.vector.tensor_tensor(th_, th_, flat_max.unsqueeze(2).broadcast_to(wide), ALU.subtract).then_inc(cmp_step, 1)
                    elif what == 'cmp_weights':
                        th_ = pc.rearrange('p t h n -> p (t h) n')[:, :, 0:N_CMP]
                        flat_max, flat_sum = c_max.rearrange('p t h -> p (t h)'), c_sum.rearrange('p t h -> p (t h)')
                        wide = [P, TT * HEADS, N_CMP]
                        dve.wait_ge(cmp_exp, 1)
                        mask = oc[:, OC['mask']].rearrange('p (t n) -> p t n', t=TT)[:, :, 0:N_CMP]
                        for t in range(TT):
                            nc.vector.tensor_tensor(pc[:, t, :, 0:N_CMP], pc[:, t, :, 0:N_CMP],
                                                    mask[:, t, :].unsqueeze(1).broadcast_to([P, HEADS, N_CMP]), ALU.mult).then_inc(cmp_step, 1)
                        dve.wait_ge(cmp_step, 7)
                        nc.vector.tensor_reduce(flat_sum, th_, AX.X, ALU.add).then_inc(cmp_step, 1)
                        dve.wait_ge(cmp_step, 8)
                        nc.vector.tensor_scalar(flat_sum, flat_sum, 1e-30, None, ALU.max).then_inc(cmp_step, 1)
                        dve.wait_ge(cmp_step, 9)
                        nc.vector.reciprocal(flat_max, flat_sum).then_inc(cmp_step, 1)
                        dve.wait_ge(cmp_step, 10)
                        nc.vector.tensor_tensor(c_sum, c_max, gates[:, :, 0::3], ALU.mult).then_inc(cmp_step, 1)
                        dve.wait_ge(cmp_step, 11)
                        nc.vector.tensor_tensor(th_, th_, flat_sum.unsqueeze(2).broadcast_to(wide), ALU.mult).then_inc(cmp_ready, 1)
                    elif what == 'att':
                        if i < ODD_HEADS:
                            if i < HEADS:
                                stat_rows(heads0 + i, [causal[:, KEYS[t]] for t in range(TT)], (DH + ROPE) ** -0.5)
                            else:
                                r, g, w = nsa(i - HEADS)
                                dve.wait_ge(t5_in, 16)
                                stat_rows(heads0 + i, [t5[:, g * REP + r, P:2 * P], t5[:, g * REP + r, 0:SEQ]], DH ** -0.5)
                        j = i - 1
                        if 0 <= j < HEADS:
                            normalise(heads0 + j)
                        elif HEADS <= j < ODD_HEADS:
                            r, g, w = nsa(j - HEADS)
                            normalise(heads0 + j, gates[:, :, 3 * (g * REP + r) + 1 + w])
                        j = i - 5
                        if 0 <= j < HEADS and j % 2:
                            out_rest('mix1', j // 2, mq[:, j // 2, :])
                        elif j >= HEADS and nsa(j - HEADS)[1:] == (1, 1):
                            r = nsa(j - HEADS)[0]
                            out_rest('mix1', PAIRS + r, nq[:, r, :])

            def gelu_end(b):
                dve.wait_ge(gelu_tanh, b + 1)
                nc.vector.scalar_tensor_tensor(u_t[:, b, :], states_tanh[:, b, :], 1.0, u_t[:, b, :], ALU.add,
                                               ALU.mult).then_inc(gelu_ready, 1)

            def residual(p, k):
                if p.startswith('ffn'):
                    n = int(p[3])
                    dve.wait_ge(down_done, KD * (CH * (n + 1) - 1) + (k | 1) + 1)
                    nc.vector.scalar_tensor_tensor(h[:, k, :], acc(k), 0.25, h[:, k, :], ALU.mult, ALU.add).then_inc(h_ready, 1)
                    return
                if k < KD - 2:
                    dve.wait_ge(mix_done, (mixes0 if p == 'mix1' else 0) + (k | 1) + 1)
                else:
                    dve.wait_ge(unit_used, ORDER[p, 'end'])
                nc.vector.tensor_tensor(h[:, k, :], acc(k), h[:, k, :], ALU.add).then_inc(h_ready, 1)

            def sum_squares(m, k):
                n = KD // 2 * m + k // 2 + 1
                dve.wait_ge(h_ready, KD * m + k + 1 - KD)
                nc.vector.tensor_tensor(sq[:, k, :], h[:, k, :], h[:, k, :], ALU.mult).then_inc(odd_squared, 1)
                dve.wait_ge(even_squared, n)
                dve.wait_ge(odd_squared, n)
                nc.vector.tensor_tensor(sq[:, k - 1, :], sq[:, k - 1, :], sq[:, k, :], ALU.add).then_inc(sq_ready, 1)

            nc.vector.memset(ones[:], 1.0).then_inc(consts_set, 1)
            nc.vector.memset(halves[:], -0.5).then_inc(consts_set, 1)
            nc.vector.memset(minus_one[:], -1.0).then_inc(consts_set, 1)
            dve.wait_ge(params_in, 16)
            n = 0
            for m, p in enumerate(PHASES):
                for k in range(KD + 1):
                    if m and k < KD:
                        residual(PHASES[m - 1], k)
                    if p == 'final' and k < KD and k % 2:
                        sum_squares(m, k)
                    if p != 'final' and k:
                        x_rest(m, k - 1)
                if p.startswith('ffn'):
                    if n == 0:
                        for sem_hi, sem_lo, w in ((first_hi, first_lo, slice(0, D // 2)), (gu_hi, gu_lo, slice(D // 2, D))):
                            dve.wait_ge(sem_hi, 1)
                            nc.vector.tensor_tensor(lo_gu[:, 0, w], raw_gu[:, 0, w], hi_gu[:, 0, w].bitcast(F32),
                                                    ALU.subtract).then_inc(sem_lo, 1)
                        split_gu(0, 0, 1)
                        for half in range(2):
                            split_gu(1, 1, half)
                        split_d(0, 0)
                        dve.wait_ge(ident_loaded, 16)
                    if n in (1, 3):
                        split_gu(CH * n + 1, 1, 0)
                        rms(m, lambda: split_gu(CH * n + 1, 1, 1), lambda: split_d(CH * n, 0))
                    else:
                        rms(m)
                    pairs(dve, step, n)
                    n += 1
                elif p == 'mix0':
                    dve.wait_ge(tables_in, 32)
                    even_mixer(m)
                elif p == 'mix1':
                    odd_mixer(m)
                elif p == 'final':
                    dve.wait_ge(ss_done, m + 1)
                    nc.vector.tensor_scalar(ms[:], misc[:, 0:TT], 1.0 / D, EPS, ALU.mult, ALU.add).then_inc(ms_ready, 1)
                    dve.wait_ge(rstd_ready, m + 1)
                    for i in range(2):
                        dve.wait_ge(final_t, i + 1)
                        nc.vector.tensor_scalar(o_sb[:, 0, i * 512:(i + 1) * 512], final_bank[i][0][:], rstd[:, 0:1],
                                                None, ALU.mult).then_inc(scaled_dve, 1)

        @block.gpsimd
        def _(pool):
            def squares(m):
                for k in range(1, KD, 2) if m < NORM['final'] else ():
                    if m == 0:
                        pool.wait_ge(x_in[2 * k // KD], 16)
                    else:
                        pool.wait_ge(h_ready, KD * m + k + 1 - KD)
                    n = KD // 2 * m + k // 2 + 1
                    nc.gpsimd.tensor_tensor(sq[:, k, :], h[:, k, :], h[:, k, :], ALU.mult).then_inc(odd_squared, 1)
                    pool.wait_ge(even_squared, n)
                    pool.wait_ge(odd_squared, n)
                    nc.gpsimd.tensor_tensor(sq[:, k - 1, :], sq[:, k - 1, :], sq[:, k, :], ALU.add).then_inc(sq_ready, 1)
                pool.wait_ge(ms_ready, m + 1)
                nc.gpsimd.tensor_tensor(rstd[:], ms[:], halves[:, 0:TT], ALU.pow).then_inc(rstd_ready, 1)

            steps = [0]

            def link(ins):
                steps[0] += 1
                ins.then_inc(s5_prep, 1)
                pool.wait_ge(s5_prep, steps[0])

            def tt(dst, a, b, op):
                link(nc.gpsimd.tensor_tensor(dst, a, b, op))

            def ts(dst, a, s1, op1, s2=None, op2=None):
                if op2 is None:
                    link(nc.gpsimd.tensor_scalar(dst, a, s1, None, op1))
                else:
                    link(nc.gpsimd.tensor_scalar(dst, a, s1, s2, op1, op2))

            S = [small[:, i, :] for i in range(13)]

            def series(dst, x, coeffs):
                ts(dst, x, coeffs[0], ALU.mult, coeffs[1], ALU.add)
                for c in coeffs[2:]:
                    tt(dst, dst, x, ALU.mult)
                    ts(dst, dst, c, ALU.add)

            def exponential(dst, x, k, r):
                ts(k, x, 1 / math.log(2), ALU.mult)
                ts(k, k, 126.0, ALU.min, -126.0, ALU.max)
                ts(k, k, MAGIC, ALU.add)
                ts(k, k, MAGIC, ALU.subtract)
                ts(r, k, LN2[0], ALU.mult)
                tt(r, x, r, ALU.subtract)
                ts(dst, k, LN2[1], ALU.mult)
                tt(r, r, dst, ALU.subtract)
                series(dst, r, [1 / 5040, 1 / 720, 1 / 120, 1 / 24, 1 / 6, 0.5, 1.0, 1.0])
                ts(k, k, 127.0, ALU.add, 8388608.0, ALU.mult)
                link(nc.gpsimd.tensor_copy(r.bitcast(mybir.dt.int32), k))
                tt(dst, dst, r, ALU.mult)

            def sine_cosine(sn, cs, x, k, sq_):
                ts(k, x, 1 / (2 * math.pi), ALU.mult)
                ts(k, k, MAGIC, ALU.add)
                ts(k, k, MAGIC, ALU.subtract)
                for part in TWO_PI:
                    ts(sn, k, part, ALU.mult)
                    tt(x, x, sn, ALU.subtract)
                ts(x, x, 0.25, ALU.mult)
                tt(sq_, x, x, ALU.mult)
                series(sn, sq_, [1 / 362880, -1 / 5040, 1 / 120, -1 / 6, 1.0])
                tt(sn, sn, x, ALU.mult)
                series(cs, sq_, [-1 / 3628800, 1 / 40320, -1 / 720, 1 / 24, -0.5, 1.0])
                for _ in range(2):
                    tt(cs, cs, sn, ALU.mult)
                    tt(sq_, sn, sn, ALU.mult)
                    ts(sn, cs, 2.0, ALU.mult)
                    ts(cs, sq_, -2.0, ALU.mult, 1.0, ALU.add)

            def s5_tables():
                lr, li = par[:, PARAMS['lam_re']], par[:, PARAMS['lam_im']]
                dt, mag, th_, sn, cs, k, r, q, ar, ai, fr, fi, den = [S[i] for i in range(13)]
                exponential(dt, par[:, PARAMS['log_dt']], k, r)
                tt(th_, lr, dt, ALU.mult)
                exponential(mag, th_, k, r)
                tt(th_, li, dt, ALU.mult)
                sine_cosine(sn, cs, th_, k, q)
                tt(ar, mag, cs, ALU.mult)
                ts(ar, ar, -1.0, ALU.add)
                tt(ai, mag, sn, ALU.mult)
                tt(den, lr, lr, ALU.mult)
                tt(q, li, li, ALU.mult)
                tt(den, den, q, ALU.add)
                tt(den, den, minus_one[:, 0:SG], ALU.pow)
                tt(fr, ar, lr, ALU.mult)
                tt(q, ai, li, ALU.mult)
                tt(fr, fr, q, ALU.add)
                tt(fr, fr, den, ALU.mult)
                tt(fi, ai, lr, ALU.mult)
                tt(q, ar, li, ALU.mult)
                tt(fi, fi, q, ALU.subtract)
                tt(fi, fi, den, ALU.mult)
                link(nc.gpsimd.memset(b_blocks, 0.0))
                link(nc.gpsimd.memset(c_d, 0.0))
                wide = [P, SG, S5_GROUP]
                p1 = tmp1[:, :, 0:S5_GROUP]
                p2 = tmp1[:, :, S5_GROUP:2 * S5_GROUP]
                for c in range(2):
                    tt(p1, bc_raw[:, c], fr.unsqueeze(2).broadcast_to(wide), ALU.mult)
                    tt(p2, bc_raw[:, 1 - c], fi.unsqueeze(2).broadcast_to(wide), ALU.mult)
                    for g in range(2):
                        lanes = slice(S5_STATE * g, S5_STATE * (g + 1))
                        cols = slice(S5_GROUP * g, S5_GROUP * (g + 1))
                        tt(b_blocks[lanes, c, :, cols], p1[lanes], p2[lanes], ALU.add if c else ALU.subtract)
                        ts(c_d[lanes, c, :, cols], bc_raw[lanes, 2 + c], -1.0 if c else 1.0, ALU.mult)
                pool.wait_ge(ss_done, 1)
                link(nc.gpsimd.memset(cos_t[:, :, 0:1], 1.0))
                link(nc.gpsimd.memset(sin_t[:, :, 0:1], 0.0))
                n = 1
                while n < SEQ:
                    w = [P, SG, n]
                    wc, ws = cs.unsqueeze(2).broadcast_to(w), sn.unsqueeze(2).broadcast_to(w)
                    c0, s0 = cos_t[:, :, 0:n], sin_t[:, :, 0:n]
                    c1, s1 = cos_t[:, :, n:2 * n], sin_t[:, :, n:2 * n]
                    p1, p2 = tmp1[:, :, 0:n], tmp2[:, :, 0:n]
                    tt(p1, c0, wc, ALU.mult)
                    tt(p2, s0, ws, ALU.mult)
                    tt(c1, p1, p2, ALU.subtract)
                    tt(p1, c0, ws, ALU.mult)
                    tt(p2, s0, wc, ALU.mult)
                    tt(s1, p1, p2, ALU.add)
                    tt(k, cs, sn, ALU.mult)
                    tt(r, sn, sn, ALU.mult)
                    ts(sn, k, 2.0, ALU.mult)
                    ts(cs, r, -2.0, ALU.mult, 1.0, ALU.add)
                    n *= 2
                ts(half_b[:], par[:, PARAMS['b_glu']], 0.5, ALU.mult)
                pool.nop().then_inc(tables_ready, 1)

            def odd_mixer():
                for what, i in odd:
                    if what == 't5':
                        pool.wait_ge(t5_copied, 1)
                        pool.dma_start(t5_rows, t5_row[0:HEADS, :].unsqueeze(1).broadcast_to([HEADS, P, 512])).then_inc(t5_stored, 16)
                        pool.wait_ge(t5_stored, 16)
                        overlapping = bass.AP(t5_rows.tensor, P - 1, [(511, P), (512 * P, HEADS), (1, T5_COLS)])
                        pool.dma_start(t5, overlapping).then_inc(t5_in, 16)
                    elif what in ('cq', 'ckv'):
                        k = i + (QB if what == 'ckv' else 0)
                        pool.wait_ge(proj_read, reads0 + k + 1)
                        if k == 0:
                            pool.wait_ge(ss_done, NORM['mix1'] + 1)
                        nc.gpsimd.tensor_tensor(sq[:, k, :], lat[:, k, :], lat[:, k, :], ALU.mult).then_inc(lat_squared, 1)
                    elif what == 'lat_squares':
                        pool.wait_ge(lat_ms_ready, 2)
                        nc.gpsimd.tensor_tensor(lat_rstd, lat_ms, halves[:], ALU.pow).then_inc(lat_rstd_ready, 1)
                    elif what == 'kv' and i == 1:
                        pool.wait_ge(proj_read, reads0 + LB + 1 + REP + 2)
                        for g in range(GROUPS):
                            rows = slice(DH * g, DH * (g + 1))
                            pool.dma_start(win[0:DH, :, g, :], kv_raw[rows, :, :]).then_inc(windows_in, 16)
                            pool.dma_start(win[DH:P, :, g, 0:SEQ - 1], kv_raw[rows, :, 1:SEQ]).then_inc(windows_in, 16)
                    elif what == 'att' and 0 <= i - 1 < ODD_HEADS:
                        g = heads0 + i - 1
                        pool.wait_ge(*((factor, g + 1) if i - 1 < HEADS else (gated, i - HEADS)))
                        nc.gpsimd.tensor_scalar(probs[slot_of(g)][:, KEYS[0]], probs[slot_of(g)][:, KEYS[0]], stats[:, slot_of(g), 2, 0:1], None,
                                                ALU.mult).then_inc(probs_0_ready, 1)
                    elif what == 'hidden':
                        pool.wait_ge(hid_read, 1)
                        nc.gpsimd.tensor_tensor(hid_t, hid, hid, ALU.mult).then_inc(hid_square, 1)
                        pool.wait_ge(hid_square, 1)
                        nc.gpsimd.tensor_scalar(hid_t, hid_t, 0.044715, 1.0, ALU.mult, ALU.add).then_inc(hid_square, 1)
                        pool.wait_ge(hid_square, 2)
                        nc.gpsimd.tensor_tensor(hid_t, hid_t, hid, ALU.mult).then_inc(hid_inner, 1)

            def even_mixer():
                rows = slice(0, F_ROWS)

                def fox_right(pair):
                    if pair >= 2:
                        pool.wait_ge(scores_done, 2 * pair - 2)
                    fa, fb = par[rows, PARAMS['fox_a']], par[rows, PARAMS['fox_b']]
                    nc.gpsimd.tensor_scalar(fox_rhs[rows, pair % 2, :], cum[rows, :], fa[:, pair:pair + 1], fb[:, pair:pair + 1],
                                            ALU.mult, ALU.add).then_inc(fox_rhs_ready, 1)

                for what, i in even:
                    if what == 's5':
                        sin2 = [sin_t[:, j, :].unsqueeze(1).broadcast_to([P, 2, SEQ]) for j in range(SG)]
                        j = i - 1
                        if i < SG:
                            pool.wait_ge(bu_ready, i + 1)
                            if i >= 1:
                                pool.wait_ge(zin_ready, 2 * i)
                            nc.gpsimd.tensor_tensor(sin_in, bu[i % 2], sin2[i], ALU.mult).then_inc(sin_in_ready, 1)
                        if 0 <= j - 1 < SG:
                            e = j - 1
                            pool.wait_ge(cos_out_ready, e + 1)
                            pool.wait_ge(sin_out_ready, e + 1)
                            nc.gpsimd.tensor_tensor(states[e % 2][:, 1, :], states[e % 2][:, 1, :], sin_out[:, 0, :],
                                                    ALU.add).then_inc(state_im_ready, 1)
                        if 0 <= j < SG:
                            pool.wait_ge(scanned, 2 * (j + 1))
                            if j >= 1:
                                pool.wait_ge(state_re_ready, j)
                                pool.wait_ge(state_im_ready, j)
                            nc.gpsimd.tensor_tensor(sin_out, bu[j % 2], sin2[j], ALU.mult).then_inc(sin_out_ready, 1)
                    elif what == 'f_end':
                        pool.wait_ge(cum_ready, 1)
                        fl = par[rows, PARAMS['fox_l']]
                        nc.gpsimd.tensor_scalar(fox_lhs[rows, :], cum[rows, :], fl[:, 0:1], fl[:, 1:2], ALU.mult,
                                                ALU.add).then_inc(fox_lhs_ready, 1)
                        fox_right(0)
                        fox_right(1)
                    elif what == 'fox' and i in (2, 4):
                        fox_right(i // 2 + 1)
                    elif what == 'glu':
                        pool.wait_ge(gelu_ready, UB)
                        nc.gpsimd.tensor_scalar(quarter[:, i, :], u_t[:, i, :], 0.25, None, ALU.mult).then_inc(quarter_ready, 1)

            pool.wait_ge(consts_set, 3)
            for p in PHASES:
                squares(NORM[p])
                if NORM[p] == 0:
                    pool.wait_ge(params_in, 16)
                    pool.wait_ge(tables_in, 32)
                    s5_tables()
                if p == 'mix0':
                    even_mixer()
                if p == 'ffn2':
                    pool.dma_start(oc, odd_consts).then_inc(odd_in, 16)
                    pool.dma_start(t5_onehot[0:BUCKETS + 1, :], onehot).then_inc(odd_in, 16)
                if p == 'mix1':
                    odd_mixer()


def odd_unit_arrays(a, by_k):
    import numpy as np

    w = a['l1_w_in']
    starts = np.cumsum([0, Q_RANK, KV_RANK, ROPE, 512, 128, 128, 128, 128, 128, 128])
    c_q, c_kv, k_rope, q_n, k_c, v_c, k_s, v_s, k_w, v_w, g = np.split(w, starts[1:], 1)
    half = ROPE // 2
    swapped = np.concatenate([k_rope[:, half:], k_rope[:, :half]], 1)
    krg = np.zeros((1, P, D), np.float32)
    kr = np.concatenate([k_rope, swapped], 1).reshape(KD, P, 2 * ROPE).transpose(1, 0, 2).reshape(P, -1)
    krg[0, :, DH:GATES_AT] = kr
    krg[0, :, GATES_AT:GATES_AT + 24 * KD] = g.reshape(KD, P, 24).transpose(1, 0, 2).reshape(P, -1)
    pair = [h for r in range(REP) for h in (r, REP + r)]
    nq = q_n.reshape(D, HEADS, DH)[:, pair].reshape(D, HEADS * DH)
    units = {'cq': by_k(c_q), 'ckv': by_k(c_kv), 'krg': krg, 'nq': by_k(nq), 'kv': by_k(np.concatenate([k_c, v_c, k_s, k_w], 1)),
             'vsw': np.concatenate([v_s, v_w], 1).reshape(2, 4, P, 2 * P).transpose(0, 2, 1, 3)}
    uq = a['l1_mla_w_uq'].reshape(Q_RANK, HEADS, DH + ROPE)
    uq = np.concatenate([uq, uq[:, :, DH + half:], uq[:, :, DH:DH + half]], 2)
    uq4 = np.zeros((4, P, D), np.float32)
    uq4[:, :, :QB * 2 * P] = uq.reshape(QB, P, 4, 2 * P).transpose(2, 1, 0, 3).reshape(4, P, -1)
    units['uq'] = uq4
    ukv = a['l1_mla_w_ukv'].reshape(KVB, P, HEADS, 2, DH).transpose(3, 1, 0, 2, 4)
    units['uk'], units['uv'] = ukv
    units['w1'] = np.stack([a['l1_nsa_cmp_' + c + '_w1'].reshape(2, CMP_PAIRS // 2, P, P).transpose(0, 2, 1, 3) for c in 'kv'])
    w_out = a['l1_w_out']
    units['out'] = np.concatenate([w_out[:512], w_out[512:].reshape(HEADS, DH, D)[pair].reshape(512, D)])
    return units


def odd_constants():
    import numpy as np

    f32 = np.float32
    oc = np.zeros((P, N_OC), f32)
    half = ROPE // 2
    freqs = (f32(10000.0) ** (-np.arange(half, dtype=f32) / f32(half))).astype(f32)
    ang = np.arange(SEQ, dtype=f32)[None, :] * freqs[:, None]
    cos, sin = np.cos(ang).astype(f32), np.sin(ang).astype(f32)
    oc[:, OC['rope']] = np.concatenate([np.ones((DH, SEQ), f32), cos, cos, -sin, sin])
    oc[DH:, OC['sel']] = np.tile(np.eye(ROPE, dtype=f32), (2, 2))
    ends = np.arange(N_CMP) * CMP_STRIDE + CMP_LEN - 1
    pos = np.arange(SEQ).reshape(TT, P).T
    mask = np.zeros((P, TT, 16), f32)
    mask[:, :, :N_CMP] = ends[None, None, :] <= pos[:, :, None]
    oc[:, OC['mask']] = mask.reshape(P, -1)
    oc[:, OC['block']] = 0.5 * np.repeat(np.eye(HEADS, dtype=f32), 16, 0)
    dist = 2 * P - 1 - np.arange(512)
    exact = BUCKETS // 2
    far = exact + (np.log(np.maximum(dist, exact).astype(f32) / f32(exact)) / f32(math.log(128 / exact))
                   * f32(BUCKETS - exact)).astype(np.int32)
    bucket = np.where(dist < exact, dist, np.minimum(far, BUCKETS - 1))
    bucket = np.where(dist < 0, BUCKETS, bucket)
    return oc, (np.arange(BUCKETS + 1)[:, None] == bucket[None, :]).astype(f32)


def kernel(**inputs):
    import ml_dtypes
    import numpy as np
    import concourse.bacc as bacc
    from concourse.bass_utils import run_bass_kernel_spmd as run

    nc = bacc.Bacc("TRN2", target_bir_lowering=False, num_devices=1)
    a = {k: np.asarray(v) for k, v in inputs.items()}
    ffns = ['l0_ffn1', 'l0_ffn2', 'l1_ffn1', 'l1_ffn2']

    def by_k(w):
        k, n = w.shape
        return w.reshape(k // P, P, n // P, P).transpose(2, 1, 0, 3)

    w_gu = np.concatenate([np.stack([by_k(a[f + '_w_gate']), by_k(a[f + '_w_up'])], 2) for f in ffns])
    w_d = np.concatenate([a[f + '_w_down'].reshape(CH, P, D) for f in ffns])
    norms = {'ffn0': 'l0_ffn1_norm', 'mix0': 'l0_mix_norm', 'ffn1': 'l0_ffn2_norm', 'ffn2': 'l1_ffn1_norm',
             'mix1': 'l1_mix_norm', 'ffn3': 'l1_ffn2_norm', 'final': 'final_norm'}
    par = np.zeros((P, N_PARAMS), np.float32)

    def lanes(w):
        return w.reshape(SG, P, *w.shape[2:]).swapaxes(0, 1)

    def put(name, w):
        w = np.asarray(w)
        par[:w.shape[0], PARAMS[name]] = w.reshape(w.shape[0], -1)

    put('gain', np.stack([a[norms[p]].reshape(KD, P).T for p in PHASES], 1))
    put('lam_re', lanes(a['l0_s5_lambda_re']))
    put('lam_im', lanes(a['l0_s5_lambda_im']))
    put('log_dt', lanes(np.repeat(a['l0_s5_log_dt'][:, None], S5_STATE, 1)))
    put('d_skip', a['l0_s5_d'].reshape(UB, P).T)
    put('b_glu', a['l0_s5_b_glu'].reshape(UB, P).T)
    for r in (0, 64):
        par[r:r + 8, PARAMS['b_f']] = par[r + 32:r + 40, PARAMS['b_f']] = a['l0_fox_b_f'][:, None]
        heads = np.eye(8, dtype=np.float32)[:, r // 64::2]
        par[r:r + 8, PARAMS['fox_a']] = -8 * heads
        par[r + 32:r + 40, PARAMS['fox_b']] = heads
        par[r:r + 32, PARAMS['fox_l']] = np.array([0, 1], np.float32)
        par[r + 32:r + 40, PARAMS['fox_l']] = np.array([8, 0], np.float32)
    s5_bc = np.stack([lanes(a['l0_s5_b_re']), lanes(a['l0_s5_b_im']), lanes(a['l0_s5_c_re'].swapaxes(1, 2)),
                      lanes(a['l0_s5_c_im'].swapaxes(1, 2))], 1)
    w_in = a['l0_w_in']
    blocks = by_k(w_in[:, :2048]).reshape(16, P, D)
    w_f = np.zeros((KD, P, F_ROWS), np.float32)
    for r in (0, 32, 64, 96):
        w_f[:, :, r:r + 8] = w_in[:, 2048:].reshape(KD, P, 8)
    f_unit = np.zeros((1, P, D), np.float32)
    f_unit[0, :, :KD * F_ROWS] = w_f.transpose(1, 0, 2).reshape(P, KD * F_ROWS)
    units = np.zeros((N_UNITS, P, D), np.float32)
    w_v = w_in[:, 1536:2048].reshape(4, 2, P, 512).transpose(0, 2, 1, 3).reshape(4, P, D)
    w_out = a['l0_w_out'].reshape(8, P, D)
    glu = by_k(a['l0_s5_w_glu']).reshape(2, 2, P, 4 * P).transpose(0, 2, 1, 3).reshape(2, P, D)
    for mixer, by_kind in (('mix0', {'u': blocks[:4], 'f': f_unit, 'q': blocks[4:8], 'k': blocks[8:12], 'v': w_v, 'glu': glu,
                                     'out': np.concatenate([w_out[4:], w_out[:4]])}), ('mix1', odd_unit_arrays(a, by_k))):
        for what, part in by_kind.items():
            for i, unit in enumerate(part.reshape(-1, P, D)):
                units[UNIT[mixer, what, i]] = unit
    put('q_norm', a['l1_mla_q_norm'].reshape(QB, P).T)
    put('kv_norm', a['l1_mla_kv_norm'].reshape(KVB, P).T)
    par[:, PARAMS['b_gate']] = a['l1_nsa_b_gate'][None, :]
    put('pe', np.concatenate([a['l1_nsa_cmp_pe_' + c].reshape(CMP_PAIRS, P).T for c in 'kv'], 1))
    put('w2', np.concatenate([a['l1_nsa_cmp_k_w2'], a['l1_nsa_cmp_v_w2']], 1))
    put('rel', a['rel_bias'])
    par[BUCKETS, PARAMS['rel']] = MASKED / 8
    rows, cols = np.arange(P)[:, None], np.arange(P)[None, :]
    tri = np.where(cols <= rows, 0, MASKED).astype(np.float32)
    oc, onehot = odd_constants()
    arrays = {
        'x_t': a['x'][0].T.reshape(KD, P, SEQ).transpose(1, 0, 2),
        'w_gate_up': w_gu.reshape(-1, P, 2 * KD * P),
        'w_down': w_d,
        'params': par,
        's5_bc': s5_bc.reshape(P, -1),
        'mix_units': units,
        'ident_in': np.eye(P, dtype=np.float32),
        'odd_consts': oc,
        'onehot': onehot,
        'causal_in': np.concatenate([tri, np.zeros_like(tri), tri], 1).astype(ml_dtypes.bfloat16),
    }
    order = ['x_t', 'w_gate_up', 'w_down', 'params', 's5_bc', 'mix_units', 'ident_in', 'causal_in', 'odd_consts', 'onehot']
    arrays = {k: np.ascontiguousarray(arrays[k]) for k in order}
    args = [nc.dram_tensor(k, v.shape, mybir.dt.from_np(v.dtype), kind="ExternalInput").ap() for k, v in arrays.items()]
    out = nc.dram_tensor('out', (SEQ, D), F32, kind="ExternalOutput").ap()
    t5_rows = nc.dram_tensor('t5_rows', (HEADS, P, 512), F32, kind="Internal").ap()
    trunk(nc, *args, t5_rows, out)
    r = run(nc, [arrays], core_ids=[0])
    return r.results[0]['out'].reshape(1, SEQ, D)
```
